# Optimizing a Trainium2 kernel written in Bass

```python
import math
import jax, jax.numpy as jnp
from jax import lax
import numpy as np

D_MODEL = 1024
BATCH = 1
SEQ = 512
DEPTH = 2
DEC_BATCH = 8
DEC_SEQ = 4
PAST_LEN = 256
PAGE_SIZE = 128

N_A_LAYERS = DEPTH // 2
N_B_LAYERS = DEPTH - N_A_LAYERS
CHUNK = 128
A_INNER = D_MODEL
A_GROUPS = 8
A_GROUP_DIM = A_INNER // A_GROUPS
N_HEADS = 8
HEAD_DIM = D_MODEL // (2 * N_HEADS)
QK_DIM = 2 * HEAD_DIM
V_DIM = 2 * HEAD_DIM
Q_BLOCK = 128
N_EXPERTS = 16
N_EXPERT_GROUPS = 4
EXPERTS_PER_GROUP = N_EXPERTS // N_EXPERT_GROUPS
TOP_K = 2
D_EXPERT = D_MODEL // 2
ALPHA = (2.0 * DEPTH) ** 0.25
BETA = (8.0 * DEPTH) ** -0.25
LN_EPS = 1e-5
NEG = -1e30

kernel_name = "yoco_gmlp_diffattn_grouped_moe_step"

def layer_norm(x, g, b):
    xf = x.astype(jnp.float32)
    mu = jnp.mean(xf, -1, keepdims=True)
    var = jnp.mean(jnp.square(xf - mu), -1, keepdims=True)
    y = (xf - mu) * lax.rsqrt(var + LN_EPS) * g.astype(jnp.float32) + b.astype(jnp.float32)
    return y.astype(x.dtype)

def chunk_gmlp(x, w_in, b_in, lnv_g, lnv_b, w_s, b_s, w_out):
    n, length, _ = x.shape
    z = jax.nn.gelu(x @ w_in + b_in)
    u, v = jnp.split(z, 2, axis=-1)
    v = layer_norm(v, lnv_g, lnv_b)
    c = min(CHUNK, length)
    n_chunks = -(-length // c)
    pad = n_chunks * c - length
    vc = jnp.pad(v, ((0, 0), (0, pad), (0, 0))).reshape(n, n_chunks, c, A_GROUPS, A_GROUP_DIM)
    causal = jnp.tril(jnp.ones((c, c), dtype=bool))
    w_mix = jnp.where(causal, w_s[:, :c, :c], jnp.zeros((), w_s.dtype))
    s = jnp.einsum('gts,ncsgd->nctgd', w_mix, vc) + b_s[:, :c].T[None, None, :, :, None]
    s = s.reshape(n, n_chunks * c, A_INNER)[:, :length]
    return (u * s) @ w_out, v

def grouped_moe(x, router_w, router_bias, w_up, w_down):
    probs = jax.nn.softmax((x @ router_w).astype(jnp.float32), axis=-1)
    sel = probs + router_bias.astype(jnp.float32)
    sel_g = sel.reshape(*sel.shape[:-1], N_EXPERT_GROUPS, EXPERTS_PER_GROUP)
    group_score = jnp.sum(lax.top_k(sel_g, TOP_K)[0], axis=-1)
    g_best = jnp.argmax(group_score, axis=-1)
    in_group = (jnp.arange(N_EXPERTS) // EXPERTS_PER_GROUP) == g_best[..., None]
    _, expert_idx = lax.top_k(jnp.where(in_group, sel, NEG), TOP_K)
    gate = jnp.take_along_axis(probs, expert_idx, axis=-1)
    gate = gate / jnp.sum(gate, axis=-1, keepdims=True)
    combine = jnp.sum(jax.nn.one_hot(expert_idx, N_EXPERTS, dtype=jnp.float32) * gate[..., None], axis=-2)
    combine = combine.astype(x.dtype)
    out = jnp.zeros_like(x)
    for e in range(N_EXPERTS):
        h_gate, h_up = jnp.split(x @ w_up[e], 2, axis=-1)
        out = out + combine[..., e:e + 1] * ((jax.nn.silu(h_gate) * h_up) @ w_down[e])
    return out

def proj_heads(x, w):
    return (x @ w).reshape(x.shape[0], x.shape[1], N_HEADS, -1)

def diff_lambda(lq1, lk1, lq2, lk2, lam_init):
    f = jnp.float32
    return (jnp.exp(jnp.sum(lq1.astype(f) * lk1.astype(f)))
            - jnp.exp(jnp.sum(lq2.astype(f) * lk2.astype(f))) + lam_init)

def masked_softmax(scores, mask):
    return jax.nn.softmax(jnp.where(mask, scores, NEG), axis=-1)

def diff_attn_prompt(q, k, v, lam):
    n, s = q.shape[:2]
    nb = s // Q_BLOCK
    scale = HEAD_DIM ** -0.5
    k1, k2 = jnp.split(k, 2, axis=-1)
    key_pos = jnp.arange(s)
    qb = q.reshape(n, nb, Q_BLOCK, N_HEADS, QK_DIM).transpose(1, 0, 2, 3, 4)

    def block(args):
        q_blk, start = args
        q1, q2 = jnp.split(q_blk, 2, axis=-1)
        mask = (start + jnp.arange(Q_BLOCK))[:, None] >= key_pos[None, :]
        p1 = masked_softmax(jnp.einsum('bqhd,bkhd->bhqk', q1, k1).astype(jnp.float32) * scale, mask)
        p2 = masked_softmax(jnp.einsum('bqhd,bkhd->bhqk', q2, k2).astype(jnp.float32) * scale, mask)
        p = (p1 - lam * p2).astype(v.dtype)
        return jnp.einsum('bhqk,bkhe->bqhe', p, v)

    o = lax.map(block, (qb, jnp.arange(nb, dtype=jnp.int32) * Q_BLOCK))
    return o.transpose(1, 0, 2, 3, 4).reshape(n, s, N_HEADS, V_DIM)

def diff_attn_sample(q, k_past, v_past, k_new, v_new, lam):
    t = q.shape[1]
    p_len = k_past.shape[1]
    scale = HEAD_DIM ** -0.5
    causal = jnp.tril(jnp.ones((t, t), dtype=bool))
    q1, q2 = jnp.split(q, 2, axis=-1)
    kp1, kp2 = jnp.split(k_past, 2, axis=-1)
    kn1, kn2 = jnp.split(k_new, 2, axis=-1)

    def probs(qi, kpi, kni):
        s_past = jnp.einsum('bqhd,bkhd->bhqk', qi, kpi).astype(jnp.float32) * scale
        s_new = jnp.where(causal, jnp.einsum('bqhd,bkhd->bhqk', qi, kni).astype(jnp.float32) * scale, NEG)
        return jax.nn.softmax(jnp.concatenate([s_past, s_new], axis=-1), axis=-1)

    p = (probs(q1, kp1, kn1) - lam * probs(q2, kp2, kn2)).astype(v_new.dtype)
    return (jnp.einsum('bhqk,bkhe->bqhe', p[..., :p_len], v_past)
            + jnp.einsum('bhqk,bkhe->bqhe', p[..., p_len:], v_new))

def diff_head_merge(o, subln_g, lam_init, w_o):
    of = o.astype(jnp.float32)
    of = of * lax.rsqrt(jnp.mean(of * of, -1, keepdims=True) + LN_EPS) * subln_g.astype(jnp.float32) * (1.0 - lam_init)
    n, length = o.shape[:2]
    return of.astype(o.dtype).reshape(n, length, N_HEADS * V_DIM) @ w_o

def setup_inputs(seed: int = 0) -> dict:
    key = jax.random.key(seed)
    ks = jax.random.split(key, 32)
    f32 = jnp.float32
    n_pages = PAST_LEN // PAGE_SIZE
    n_used = DEC_BATCH * n_pages
    n_phys = n_used + max(1, n_used // 4)

    def nrm(k, shape, scale):
        return jax.random.normal(k, shape, f32) * scale

    page_table = jax.random.permutation(ks[0], n_phys)[:n_used].reshape(DEC_BATCH, n_pages).astype(jnp.int32)
    return {
        "x_prompt": nrm(ks[1], (BATCH, SEQ, D_MODEL), 1.0),
        "x_sample": nrm(ks[2], (DEC_BATCH, DEC_SEQ, D_MODEL), 1.0),
        "cache_k": nrm(ks[3], (n_phys, PAGE_SIZE, N_HEADS, QK_DIM), 1.0),
        "cache_v": nrm(ks[4], (n_phys, PAGE_SIZE, N_HEADS, V_DIM), BETA),
        "page_table": page_table,
        "ln1_g": 1.0 + nrm(ks[5], (DEPTH, D_MODEL), 0.05),
        "ln1_b": nrm(ks[6], (DEPTH, D_MODEL), 0.02),
        "ln2_g": 1.0 + nrm(ks[7], (DEPTH, D_MODEL), 0.05),
        "ln2_b": nrm(ks[8], (DEPTH, D_MODEL), 0.02),
        "a_w_in": nrm(ks[9], (N_A_LAYERS, D_MODEL, 2 * A_INNER), D_MODEL ** -0.5),
        "a_b_in": nrm(ks[10], (N_A_LAYERS, 2 * A_INNER), 0.02),
        "a_lnv_g": 1.0 + nrm(ks[11], (N_A_LAYERS, A_INNER), 0.05),
        "a_lnv_b": nrm(ks[12], (N_A_LAYERS, A_INNER), 0.02),
        "a_w_s": nrm(ks[13], (N_A_LAYERS, A_GROUPS, CHUNK, CHUNK), CHUNK ** -0.5),
        "a_b_s": 1.0 + nrm(ks[14], (N_A_LAYERS, A_GROUPS, CHUNK), 0.1),
        "a_w_out": nrm(ks[15], (N_A_LAYERS, A_INNER, D_MODEL), BETA * A_INNER ** -0.5),
        "w_k": nrm(ks[16], (D_MODEL, N_HEADS * QK_DIM), D_MODEL ** -0.5),
        "w_v": nrm(ks[17], (D_MODEL, N_HEADS * V_DIM), BETA * D_MODEL ** -0.5),
        "b_w_q": nrm(ks[18], (N_B_LAYERS, D_MODEL, N_HEADS * QK_DIM), D_MODEL ** -0.5),
        "b_lam_q1": nrm(ks[19], (N_B_LAYERS, HEAD_DIM), 0.1),
        "b_lam_k1": nrm(ks[20], (N_B_LAYERS, HEAD_DIM), 0.1),
        "b_lam_q2": nrm(ks[21], (N_B_LAYERS, HEAD_DIM), 0.1),
        "b_lam_k2": nrm(ks[22], (N_B_LAYERS, HEAD_DIM), 0.1),
        "b_subln_g": 1.0 + nrm(ks[23], (N_B_LAYERS, V_DIM), 0.05),
        "b_w_o": nrm(ks[24], (N_B_LAYERS, N_HEADS * V_DIM, D_MODEL), BETA * (N_HEADS * V_DIM) ** -0.5),
        "router_w": nrm(ks[25], (D_MODEL, N_EXPERTS), D_MODEL ** -0.5),
        "router_bias": nrm(ks[26], (N_EXPERTS,), 0.01),
        "moe_w_up": nrm(ks[27], (DEPTH, N_EXPERTS, D_MODEL, 2 * D_EXPERT), D_MODEL ** -0.5),
        "moe_w_down": nrm(ks[28], (DEPTH, N_EXPERTS, D_EXPERT, D_MODEL), BETA * D_EXPERT ** -0.5),
    }

def reference(x_prompt, x_sample, cache_k, cache_v, page_table, ln1_g, ln1_b, ln2_g, ln2_b,
              a_w_in, a_b_in, a_lnv_g, a_lnv_b, a_w_s, a_b_s, a_w_out, w_k, w_v,
              b_w_q, b_lam_q1, b_lam_k1, b_lam_q2, b_lam_k2, b_subln_g, b_w_o,
              router_w, router_bias, moe_w_up, moe_w_down):
    xp, xs = x_prompt, x_sample
    chunk_v_rows = []
    for l in range(DEPTH):
        if l < N_A_LAYERS:
            a_args = (a_w_in[l], a_b_in[l], a_lnv_g[l], a_lnv_b[l], a_w_s[l], a_b_s[l], a_w_out[l])
            mp, _ = chunk_gmlp(xp, *a_args)
            ms, vs = chunk_gmlp(xs, *a_args)
            chunk_v_rows.append(vs)
        else:
            j = l - N_A_LAYERS
            if j == 0:
                k_prompt = proj_heads(xp, w_k)
                v_prompt = proj_heads(xp, w_v)
                k_sample = proj_heads(xs, w_k)
                v_sample = proj_heads(xs, w_v)
                n_seq, n_pg = page_table.shape
                k_past = cache_k[page_table].reshape(n_seq, n_pg * PAGE_SIZE, N_HEADS, QK_DIM)
                v_past = cache_v[page_table].reshape(n_seq, n_pg * PAGE_SIZE, N_HEADS, V_DIM)
            lam_init = 0.8 - 0.6 * math.exp(-0.3 * l)
            lam = diff_lambda(b_lam_q1[j], b_lam_k1[j], b_lam_q2[j], b_lam_k2[j], lam_init)
            qp = proj_heads(xp, b_w_q[j])
            qs = proj_heads(xs, b_w_q[j])
            mp = diff_head_merge(diff_attn_prompt(qp, k_prompt, v_prompt, lam), b_subln_g[j], lam_init, b_w_o[j])
            ms = diff_head_merge(diff_attn_sample(qs, k_past, v_past, k_sample, v_sample, lam),
                                 b_subln_g[j], lam_init, b_w_o[j])
        xp = layer_norm(ALPHA * xp + mp, ln1_g[l], ln1_b[l])
        xs = layer_norm(ALPHA * xs + ms, ln1_g[l], ln1_b[l])
        xp = layer_norm(ALPHA * xp + grouped_moe(xp, router_w, router_bias, moe_w_up[l], moe_w_down[l]),
                        ln2_g[l], ln2_b[l])
        xs = layer_norm(ALPHA * xs + grouped_moe(xs, router_w, router_bias, moe_w_up[l], moe_w_down[l]),
                        ln2_g[l], ln2_b[l])
    state_chunk_v_sample = jnp.stack(chunk_v_rows)
    return (xp, xs, k_prompt, v_prompt, k_sample, v_sample, state_chunk_v_sample)


_drawn_inputs = setup_inputs


def setup_inputs(seed=0):
    import zlib

    import numpy as np

    out = dict(_drawn_inputs(seed))
    spreads = {}
    factors = {'a_lnv_b': 2.856, 'b_lam_q1': 3.89, 'b_lam_k1': 5.008, 'b_lam_k2': 4.953}
    for name, (base, spread) in spreads.items():
        noise = np.random.default_rng([zlib.crc32(name.encode()), seed]).standard_normal(out[name].shape)
        drawn = base * np.exp(spread * noise) if base else spread * noise
        out[name] = __import__('jax').numpy.asarray(drawn.astype(out[name].dtype))
    for name, factor in factors.items():
        out[name] = (out[name] * factor).astype(out[name].dtype)
    return out
```

```python
import math
from contextlib import ExitStack

import numpy as np

import concourse.bass as bass
from concourse import mybir

F32 = mybir.dt.float32
F32R = mybir.dt.float32r
F16 = mybir.dt.float16
I32 = mybir.dt.int32
ALU = mybir.AluOpType
ACT = mybir.ActivationFunctionType
AX = mybir.AxisListType.X

P = 128
D = 1024
KT_D = D // P
SEQ = 512
DEC_B, DEC_T = 8, 4
NSAMP = DEC_B * DEC_T
NTOK = SEQ + NSAMP
TILES = 5
ROWS = [P, P, P, P, NSAMP]
LAYERS = 2
ALPHA = (2.0 * LAYERS) ** 0.25
EPS = 1e-5
NEG = -1e30
HEADS = 8
HEAD_DIM = 64
SCALE = HEAD_DIM ** -0.5
LAM_INIT = 0.8 - 0.6 * math.exp(-0.3 * 1)
EXPERTS, GROUPS, PER_GROUP = 16, 4, 4
MAX_BLOCKS = EXPERTS + (2 * NTOK) // P
LIST_COLS = MAX_BLOCKS + 1
RAW_SLOTS = 6
SPLIT_SLOTS = 3
HALF = 512
PROJ_BANKS = 6
NO_ROW = 8192.0

A_WS, A_WOUT, A_CHUNKS, A_SPLITS = 8, 9, 13, 12
B_CACHE, B_WO, B_CHUNKS, B_SPLITS = 12, 28, 32, 16

M_WIN, M_MIX, M_WOUT, M_ROUTE_A, M_QKV, M_WO, M_ROUTE_B, M_END = 0, 20, 30, 40, 43, 73, 83, 86
T_US, T_LN1A, T_LN2A, T_O, T_LN1B = 0, 10, 20, 30, 40

C_IDENT, C_CAUSAL, C_IOTA, C_SMASK, C_RK4, C_RK16, C_IOTA16, C_IOTA8, C_THR, C_ID1, C_VALID, C_COEF, C_END = (
    0, 128, 256, 384, 512, 516, 532, 548, 556, 560, 570, 575, 577)


def constants():
    c = np.zeros((P, C_END), np.float32)
    i = np.arange(P)
    c[:, C_IDENT:C_IDENT + P] = np.eye(P)
    c[:, C_CAUSAL:C_CAUSAL + P] = np.where(i[None, :] <= i[:, None], 0.0, NEG)
    c[:, C_IOTA:C_IOTA + P] = i[None, :]
    row_b, row_q = i // 64, i % 4
    for g in range(4):
        j = np.arange(NSAMP)
        ok = (j[None, :] // DEC_T == 2 * g + row_b[:, None]) & (j[None, :] % DEC_T <= row_q[:, None])
        c[:, C_SMASK + 32 * g:C_SMASK + 32 * g + 32] = np.where(ok, 0.0, NEG)
    c[:, C_RK4:C_RK4 + 4] = 4 - np.arange(4)
    c[:, C_RK16:C_RK16 + 16] = 16 - np.arange(16)
    c[:, C_IOTA16:C_IOTA16 + 16] = np.arange(16)
    c[:, C_IOTA8:C_IOTA8 + 8] = np.arange(8)
    c[:, C_THR:C_THR + 4] = 128.0 * (1 + np.arange(4))
    for k in range(2):
        for t in range(TILES):
            c[:ROWS[t], C_ID1 + k * TILES + t] = k * NTOK + t * P + i[:ROWS[t]] + 1
    c[:, C_VALID:C_VALID + TILES] = 1.0
    c[NSAMP:, C_VALID + TILES - 1] = 0.0
    part = (i // 4) % 2
    c[:, C_COEF] = part == 0
    c[:, C_COEF + 1] = part == 1
    c16 = np.zeros((P, 2 * P), np.float16)
    c16[:, 0:P] = i[:, None] < i[None, :]
    c16[:, P:2 * P] = 1.0
    s = np.arange(NSAMP)
    cmix = np.zeros((P, P + NSAMP), np.float32)
    cmix[:, 0:P] = i[:, None] <= i[None, :]
    cmix[:NSAMP, P:] = (s[:, None] // DEC_T == s[None, :] // DEC_T) & (s[:, None] <= s[None, :])
    return c, c16, cmix


def last_before(slot, slots, count):
    return max(i for i in range(count) if i % slots == slot)


def trunk(nc, a, outs):
    y_prompt, y_sample, k_prompt, v_prompt, k_sample, v_sample, state_v = outs
    with ExitStack() as ctx:
        def sem(name):
            return ctx.enter_context(nc.semaphore(name))

        top = [(nc.sbuf_base + 63) // 64 * 64]

        def place(name, shape, dt, at=None):
            size = int(np.prod(shape[1:])) * (2 if dt == F16 else 4)
            off = top[0] if at is None else at
            t = nc.alloc_sbuf_tensor_at(name, shape, dt, offset=off)
            if at is None:
                top[0] += (size + 31) // 32 * 32
                assert top[0] <= nc.sbuf_usable_end
            assert off + size <= nc.sbuf_usable_end
            return t, off + (size + 31) // 32 * 32

        raw = place("raw", [P, RAW_SLOTS, 4, HALF], F32)[0]
        x = place("x", [P, TILES, D], F32)[0]
        xTh = place("xTh", [P, KT_D, NTOK], F32R)[0]
        xTl = place("xTl", [P, KT_D, NTOK], F32R)[0]
        split_at = top[0]
        wh = place("wh", [P, SPLIT_SLOTS, 4, HALF], F32R)[0]
        wl = place("wl", [P, SPLIT_SLOTS, 4, HALF], F32R)[0]
        gb = place("gb", [P, 2 * D], F32)[0]
        con = place("con", [P, C_END], F32)[0]
        con16 = place("con16", [P, 2 * P], F16)[0]
        rwh = place("rwh", [P, KT_D, EXPERTS], F32R)[0]
        rwl = place("rwl", [P, KT_D, EXPERTS], F32R)[0]
        rbias = place("rbias", [P, EXPERTS], F32)[0]
        stats = place("stats", [P, TILES, 2, 6], F32)[0]
        mv = place("mv", [P, TILES, 2], F32)[0]
        lns = place("lns", [P, 4, TILES], F32)[0]
        gates = place("gates", [P, 2, TILES], F32)[0]
        gidx = place("gidx", [P, LIST_COLS], I32)[0]
        sidx = place("sidx", [P, LIST_COLS], I32)[0]
        gcur = place("gcur", [P, 1], I32)[0]
        scur = place("scur", [P, 1], I32)[0]
        table = place("table", [P, LIST_COLS], I32)[0]
        pages = place("pages", [P, 16], I32)[0]
        lamc = place("lamc", [P, 12], F32)[0]
        arena = top[0]
        u, n = place("u", [P, TILES, D], F32, arena)
        v, n = place("v", [P, TILES, D], F32, n)
        cmix, n = place("cmix", [P, P + NSAMP], F32, n)
        wsm, n = place("wsm", [NSAMP, HEADS, NSAMP], F32, n)
        bsp, n = place("bsp", [P, 8], F32, n)
        bss, n = place("bss", [NSAMP, 8], F32, n)
        xT0 = place("xT0", [P, KT_D, NTOK], F32, arena)[0]
        rw_raw = place("rw_raw", [P, KT_D, EXPERTS], F32, arena + 20480)[0]
        QT, n = place("QT", [P, HEADS, NTOK], F32, arena)
        KT, n = place("KT", [P, HEADS, NTOK], F32, n)
        stg, _ = place("stg", [P, TILES, HALF], F32, n)
        qpad, _ = place("qpad", [P, 2176], F32, n)
        o, n = place("o", [P, TILES, D], F32, split_at)
        kts, n = place("kts", [P, HEADS, 256], F32, n)
        lamp, n = place("lamp", [P, 2, HEAD_DIM], F32, n)
        oss, n = place("oss", [P, 3, TILES, HEADS], F32, n)
        mxs, n = place("mxs", [P, 4, 2, 2], F32, n)
        smx, n = place("smx", [P, 6], F32, n)
        attn_work = n
        E, n = place("E", [P, 2, 2, HALF], F32, attn_work)
        Pm, n = place("Pm", [P, 2, HALF], F32, n)
        PTs, n = place("PTs", [P, 2, HALF], F32, n)
        assert n <= split_at + 2 * SPLIT_SLOTS * 4 * HALF * 4
        Es, n = place("Es", [P, 288], F32, attn_work)
        Ps, n = place("Ps", [P, 288], F32, n)
        ptz, n = place("ptz", [P, 2, 2, HEADS, NSAMP], F32, n)
        ptn, n = place("ptn", [NSAMP, HEADS, NSAMP], F32, n)
        osq, n = place("osq", [P, D], F32, n)
        subg = gb[:, 4 * HEAD_DIM:4 * HEAD_DIM + P]
        xg, n = place("xg", [P, D], F32, arena)
        xgTh, n = place("xgTh", [P, KT_D, P], F32R, n)
        xgTl, n = place("xgTl", [P, KT_D, P], F32R, n)
        sg, n = place("sg", [P, HALF], F32, n)
        hb, n = place("hb", [P, HALF], F32, n)
        hTh, n = place("hTh", [P, 4, P], F32R, n)
        hTl, n = place("hTl", [P, 4, P], F32R, n)
        yb, n = place("yb", [P, D], F32, n)
        yl, _ = place("yl", [P, 2, 2, D], F32, n)
        lg, n = place("lg", [P, TILES, EXPERTS], F32, n)
        prob, n = place("prob", [P, TILES, EXPERTS], F32, n)
        sel, n = place("sel", [P, TILES, EXPERTS], F32, n)
        tmp, n = place("tmp", [P, 2, TILES, EXPERTS], F32, n)
        oh, n = place("oh", [P, 2, TILES, EXPERTS], F32, n)
        hilo, n = place("hilo", [P, 2, TILES * GROUPS, 2], F32, n)
        gsc, n = place("gsc", [P, 4, TILES, GROUPS], F32, n)
        col, n = place("col", [P, 12, 2, TILES], F32, n)
        cnt, n = place("cnt", [P, 6, EXPERTS], F32, n)
        thr, n = place("thr", [P, 16, 16], F32, n)
        tblf, n = place("tblf", [P, LIST_COLS], F32, n)
        lst, n = place("lst", [P, 4, LIST_COLS], F32, n)
        m16, n = place("m16", [P, TILES, EXPERTS], F16, n)
        lo16, n = place("lo16", [P, 2 * TILES, P], F16, n)
        hi16, n = place("hi16", [P, 2 * TILES, LIST_COLS + 1], F16, n)
        ps = nc.alloc_psum_tensor("ps", [P, 8, HALF], F32)

        x_rows = [nc.dram_tensor(f"x_rows{l}", (NTOK, D), F32).ap() for l in range(LAYERS)]
        y_rows = [nc.dram_tensor(f"y_rows{l}", (2 * NTOK, D), F32).ap() for l in range(LAYERS)]
        x_parked = nc.dram_tensor("x_parked", (NTOK, D), F32).ap()

        con_in = sem("con_in"); rb_in = sem("rb_in"); xT0_in = sem("xT0_in"); rw_in = sem("rw_in"); x_in = sem("x_in")
        mixc_in = sem("mixc_in"); wsm_in = sem("wsm_in"); gb_in = sem("gb_in"); lam_in = sem("lam_in")
        pages_in = sem("pages_in")
        zeroed = sem("zeroed"); x0_high = sem("x0_high"); x0_low = sem("x0_low")
        rw_high = sem("rw_high"); rw_low = sem("rw_low")
        wsm_zeroed = sem("wsm_zeroed"); ws_masked = sem("ws_masked")
        raw_a = [sem(f"raw_a{i}") for i in range(RAW_SLOTS)]
        raw_b = [sem(f"raw_b{i}") for i in range(RAW_SLOTS)]
        raw_m = [[sem(f"raw_m{l}_{i}") for i in range(RAW_SLOTS)] for l in range(LAYERS)]
        high = {k: sem(f"high_{k}") for k in ("a", "b", "m0", "m1")}
        low = {k: sem(f"low_{k}") for k in ("a", "b", "m0", "m1")}
        used = {k: sem(f"used_{k}") for k in ("a", "b", "m0", "m1")}
        mix_done = sem("mix_done")
        proj_done = sem("proj_done"); proj_free = sem("proj_free")
        gelu_done = sem("gelu_done")
        tr_done = sem("tr_done"); tr_high = sem("tr_high"); tr_low = sem("tr_low")
        ln_var = sem("ln_var"); ln_std = sem("ln_std"); ln_rs = sem("ln_rs"); ln_norm = sem("ln_norm")
        ln_gain = sem("ln_gain"); ln_out = sem("ln_out")
        dve_step = sem("dve_step")
        stg_out = [sem(f"stg_out{t}") for t in range(TILES)]
        vs_out = sem("vs_out"); x_out = sem("x_out"); park_out = sem("park_out"); park_in = sem("park_in")
        kv_out = sem("kv_out"); y_out = sem("y_out")
        kq_tr = sem("kq_tr"); kq_copied = sem("kq_copied")
        exp_r = sem("exp_r"); lam_exp = sem("lam_exp"); lam_sum = sem("lam_sum")
        at_s = sem("at_s"); at_max = sem("at_max"); at_exp = sem("at_exp"); at_p = sem("at_p")
        at_pt = sem("at_pt"); at_ptc = sem("at_ptc"); at_pv = sem("at_pv"); at_o = sem("at_o")
        sm_kt = sem("sm_kt"); sm_ktc = sem("sm_ktc"); sm_s = sem("sm_s"); sm_q = sem("sm_q")
        sm_max = sem("sm_max"); sm_exp = sem("sm_exp"); sm_p = sem("sm_p"); sm_pt = sem("sm_pt")
        sm_zero = sem("sm_zero"); sm_ptz = sem("sm_ptz"); sm_pv = sem("sm_pv"); sm_o = sem("sm_o")
        cache_used = sem("cache_used")
        om_var = sem("om_var"); om_std = sem("om_std"); om_r = sem("om_r"); om_g = sem("om_g")
        logit_max = sem("logit_max"); plan = sem("plan"); onehots = sem("onehots"); masks = sem("masks")
        moe = [{k: sem(f"{k}{l}") for k in (
            "gcopy", "gathered", "xg_tr", "xg_high", "xg_low", "silu", "h_ready", "h_tr", "h_high", "h_low",
            "y_ready", "scopy", "scattered", "y_in0", "y_in1", "y_used")} for l in range(LAYERS)]

        ident = con[:, C_IDENT:C_IDENT + P]

        def after(eng, s, count):
            if not isinstance(count, int) or count > 0:
                eng.wait_ge(s, count)

        def dram_tile(t, ap):
            return ap[t * P:t * P + ROWS[t], :]

        def chunk(w, kh, cb):
            return w[kh * HALF:(kh + 1) * HALF, cb * HALF:(cb + 1) * HALF].rearrange("(k p) n -> p k n", p=P)

        def down_chunk(w, cb):
            return w[:, cb * HALF:(cb + 1) * HALF].rearrange("(k p) n -> p k n", p=P)

        w_in, w_out = a["a_w_in"][0], a["a_w_out"][0]
        WIN_COLS = [2, 3, 0, 1]
        block = ctx.enter_context(nc.Block())
        low_a = {c: c + 1 - (c > A_WS) for c in range(A_CHUNKS) if c != A_WS}
        low_b = {c: c + 1 - (B_WO - B_CACHE) * (c >= B_WO) for c in range(B_CHUNKS) if not B_CACHE <= c < B_WO}
        landed_b = {c: sum(32 if B_CACHE <= d < B_WO else 16 for d in range(c % RAW_SLOTS, c + 1, RAW_SLOTS))
                    for c in range(B_CHUNKS)}

        def landed_a(c):
            return 16 * (c // RAW_SLOTS + 1)

        @block.sync
        def _(sp):
            def up(l, e, i, slot_free):
                for q in range(4):
                    slot_free(q)
                    sp.dma_start(raw[:, q], chunk(a["moe_w_up"][l, e], q % 2, q // 2)).then_inc(raw_m[l][q], 16)

            def down(l, e, i, slot_free):
                for r in range(2):
                    slot_free(4 + r)
                    sp.dma_start(raw[:, 4 + r], down_chunk(a["moe_w_down"][l, e], r)).then_inc(raw_m[l][4 + r], 16)

            def moe_stream(l, first_free):
                low_m = low[f"m{l}"]

                def previous(i):
                    def free(slot):
                        if slot < 4:
                            sp.wait_ge(low_m, (slot if isinstance(i, int) and i == 1 else 6 * (i - 1) - 2 + slot) + 1)
                        else:
                            sp.wait_ge(low_m, 6 * (i - 1) + 8 + (slot - 4) + 1)
                    return free
                up(l, 0, 0, first_free)
                down(l, 0, 0, first_free)
                up(l, 1, 1, previous(1))
                with sp.Fori(2, EXPERTS - 1) as i:
                    up(l, i, i, previous(i))
                    down(l, i - 1, i - 1, previous(i - 1))
                sp.wait_ge(plan, l + 1)
                blocks = sp.value_load(table[0:1, LIST_COLS - 1:LIST_COLS], min_val=0, max_val=MAX_BLOCKS - EXPERTS) + EXPERTS
                with sp.Fori(EXPERTS - 1, blocks) as i:
                    e = sp.value_load(table[0:1, bass.ds(i, 1)], min_val=0, max_val=EXPERTS - 1)
                    up(l, e, i, previous(i))
                    before = sp.value_load(table[0:1, bass.ds(i - 1, 1)], min_val=0, max_val=EXPERTS - 1)
                    down(l, before, i - 1, previous(i - 1))
                e = sp.value_load(table[0:1, bass.ds(blocks - 1, 1)], min_val=0, max_val=EXPERTS - 1)
                down(l, e, blocks - 1, previous(blocks - 1))
                return blocks

            sp.dma_start(xT0[:, :, 0:SEQ], a["x_prompt_T"].rearrange("(k p) n -> p k n", p=P)).then_inc(xT0_in, 16)
            sp.dma_start(xT0[:, :, SEQ:NTOK], a["x_sample_T"].rearrange("(k p) n -> p k n", p=P)).then_inc(xT0_in, 16)
            for c in range(A_CHUNKS):
                s = c % RAW_SLOTS
                if c >= RAW_SLOTS:
                    sp.wait_ge(low["a"], low_a[c - RAW_SLOTS])
                if c < A_WS:
                    src = chunk(w_in, c % 2, WIN_COLS[c // 2])
                elif c == A_WS:
                    src = a["w_s_T"].rearrange("s (a g) t -> s a (g t)", a=2)
                else:
                    src = chunk(w_out, (c - A_WOUT) % 2, (c - A_WOUT) // 2)
                sp.dma_start(raw[:, s, 0:src.shape[1]], src).then_inc(raw_a[s], 16)

            def after_a(slot):
                c = last_before(slot, RAW_SLOTS, A_CHUNKS)
                if c == A_WS:
                    sp.wait_ge(mix_done, 1)
                else:
                    sp.wait_ge(low["a"], low_a[c])
            blocks = moe_stream(0, after_a)

            sp.wait_ge(pages_in, 16)
            for c in range(B_CHUNKS):
                s = c % RAW_SLOTS
                if c < RAW_SLOTS:
                    sp.wait_ge(low["m0"], 6 * blocks - 7 + s if s < 4 else 6 * blocks - 1 + (s - 4))
                elif B_CACHE <= c - RAW_SLOTS < B_WO:
                    sp.wait_ge(cache_used, c - RAW_SLOTS - B_CACHE + 1)
                else:
                    sp.wait_ge(low["b"], low_b[c - RAW_SLOTS])
                if B_CACHE <= c < B_WO:
                    pair, which, b2 = (c - B_CACHE) // 4, (c - B_CACHE) // 2 % 2, (c - B_CACHE) % 2
                    cache = a["cache_v"] if which else a["cache_k"]
                    for page in range(2):
                        j = (2 * pair + b2) * 2 + page
                        phys = sp.value_load(pages[0:1, j:j + 1], min_val=0, max_val=cache.shape[0] - 1)
                        sp.dma_start(raw[:, s, 2 * page:2 * page + 2, :].rearrange("p k n -> p (k n)"),
                                     cache[phys].rearrange("r h d -> r (h d)")).then_inc(raw_b[s], 16)
                else:
                    w = [a["w_k"], a["w_v"], a["b_w_q"][0]][c // 4] if c < B_CACHE else a["b_w_o"][0]
                    sp.dma_start(raw[:, s], chunk(w, c % 2, c // 2 % 2)).then_inc(raw_b[s], 16)

            def after_b(slot):
                c = last_before(slot, RAW_SLOTS, B_CHUNKS)
                if B_CACHE <= c < B_WO:
                    sp.wait_ge(cache_used, c - B_CACHE + 1)
                else:
                    sp.wait_ge(low["b"], low_b[c])
            moe_stream(1, after_b)

        @block.gpsimd
        def _(pool):
            def row(ap):
                return ap.unsqueeze(0).broadcast_to([P, ap.shape[0]])

            def load_gb(g, b):
                pool.dma_start(gb[:, 0:D], row(g)).then_inc(gb_in, 16)
                pool.dma_start(gb[:, D:2 * D], row(b)).then_inc(gb_in, 16)

            def gain(call, src):
                pool.wait_ge(gb_in, 16 + 32 * (call + 1))
                for t in range(TILES):
                    m = ROWS[t]
                    pool.wait_ge(ln_norm, TILES * call + t + 1)
                    pool.tensor_tensor(src[0:m, t], src[0:m, t], gb[0:m, 0:D], ALU.mult).then_inc(ln_gain, 1)

            pool.dma_start(rw_raw[:], a["router_w"].rearrange("(k p) e -> p k e", p=P)).then_inc(rw_in, 16)
            pool.dma_start(gb[:], row(a["a_b_in"][0])).then_inc(gb_in, 16)
            pool.dma_start(rbias[:], row(a["router_bias"])).then_inc(rb_in, 16)
            for t in range(TILES):
                src = dram_tile(t, a["x_prompt"][0]) if t < 4 else a["x_sample"].rearrange("b t d -> (b t) d")
                pool.dma_start(x[0:ROWS[t], t], src).then_inc(x_in, 16)
            pool.dma_start(pages[0:1, :], a["page_table"].rearrange("b n -> (b n)").unsqueeze(0)).then_inc(pages_in, 16)
            pool.dma_start(cmix[:], a["cmix"]).then_inc(mixc_in, 16)
            pool.dma_start(bsp[:], a["b_s_T"]).then_inc(mixc_in, 16)
            pool.dma_start(bss[:], a["b_s_rep"]).then_inc(mixc_in, 16)
            pool.wait_ge(wsm_zeroed, 1)
            with nc.allow_non_contiguous_dma("4-row blocks of the spatial weights"):
                for b in range(DEC_B):
                    pool.dma_start(wsm[b * DEC_T:(b + 1) * DEC_T, :, b * DEC_T:(b + 1) * DEC_T],
                                   a["w_s_T"][0:DEC_T, :, 0:DEC_T]).then_inc(wsm_in, 16)

            pool.wait_ge(proj_free, M_WIN + 20)
            load_gb(a["a_lnv_g"][0], a["a_lnv_b"][0])
            gain(0, v)
            pool.wait_ge(ln_out, TILES)
            pool.dma_start(state_v.rearrange("l b t d -> (l b t) d"), v[0:NSAMP, 4]).then_inc(vs_out, 16)

            def moe_pool(l):
                s = moe[l]
                load_gb(a["ln1_g"][l], a["ln1_b"][l])
                gain(1 + 2 * l, x)
                for t in range(TILES):
                    pool.wait_ge(ln_out, TILES * (1 + 2 * l) + t + 1)
                    pool.dma_start(dram_tile(t, x_rows[l]), x[0:ROWS[t], t]).then_inc(x_out, 16)
                load_gb(a["ln2_g"][l], a["ln2_b"][l])
                pool.wait_ge(x_out, 16 * TILES * (l + 1))
                pool.wait_ge(plan, l + 1)
                blocks = pool.value_load(table[0:1, LIST_COLS - 1:LIST_COLS], min_val=0, max_val=MAX_BLOCKS - EXPERTS) + EXPERTS

                def wait_apart(n, *sems):
                    if isinstance(n, int):
                        count = n
                    else:
                        count = pool.to_reg(n)
                    pool.wait_ge(plan, l + 1)
                    for sm in sems:
                        pool.wait_ge(sm, count)

                def gather(i):
                    after(pool, s["xg_tr"], i)
                    after(pool, s["gathered"], 16 * i)
                    pool.tensor_copy(gcur[:], gidx[:, bass.ds(i, 1)]).then_inc(s["gcopy"], 1)
                    wait_apart(i + 1, s["gcopy"])
                    pool.indirect_dma_start(xg[:], None, x_rows[l], bass.IndirectOffsetOnAxis(ap=gcur[:, 0:1], axis=0)
                                            ).then_inc(s["gathered"], 16)

                def scatter(i):
                    after(pool, s["scattered"], 16 * i)
                    pool.tensor_copy(scur[:], sidx[:, bass.ds(i, 1)]).then_inc(s["scopy"], 1)
                    wait_apart(i + 1, s["scopy"], s["y_ready"])
                    pool.indirect_dma_start(y_rows[l], bass.IndirectOffsetOnAxis(ap=scur[:, 0:1], axis=0), yb[:], None,
                                            bounds_check=2 * NTOK - 1, oob_is_err=False).then_inc(s["scattered"], 16)
                gather(0)
                gather(1)
                gather(2)
                gather(3)
                scatter(0)
                with pool.Fori(3, blocks) as i:
                    gather(i + 1)
                    scatter(i - 2)
                scatter(blocks - 2)
                scatter(blocks - 1)
                wait_apart(16 * blocks, s["scattered"])
                for t in range(TILES):
                    if t >= 2:
                        pool.wait_ge(s["y_used"], t - 1)
                    for k in range(2):
                        pool.dma_start(yl[0:ROWS[t], t % 2, k], y_rows[l][k * NTOK + t * P:k * NTOK + t * P + ROWS[t], :]
                                       ).then_inc(s[f"y_in{t % 2}"], 16)
                gain(2 + 2 * l, x)

            moe_pool(0)
            for t in range(TILES):
                pool.wait_ge(ln_out, 2 * TILES + t + 1)
                pool.dma_start(dram_tile(t, x_parked), x[0:ROWS[t], t]).then_inc(park_out, 16)
            for j, name in enumerate(("b_lam_q1", "b_lam_k1", "b_lam_q2", "b_lam_k2")):
                pool.dma_start(gb[:, j * HEAD_DIM:(j + 1) * HEAD_DIM], row(a[name][0])).then_inc(lam_in, 16)
            pool.dma_start(subg, row(a["b_subln_g"][0])).then_inc(lam_in, 16)
            k_rows = [k_prompt[0].rearrange("s h d -> s (h d)"), k_sample.rearrange("b t h d -> (b t) (h d)")]
            v_rows = [v_prompt[0].rearrange("s h d -> s (h d)"), v_sample.rearrange("b t h d -> (b t) (h d)")]

            def out_tile(rows, t):
                return dram_tile(t, rows[0]) if t < 4 else rows[1]
            for cb in range(2):
                for t in range(TILES):
                    pool.wait_ge(proj_free, M_QKV + cb * TILES + t + 1)
                    pool.dma_start(out_tile(k_rows, t)[:, cb * HALF:(cb + 1) * HALF], stg[0:ROWS[t], t]
                                   ).then_inc(stg_out[t], 16)
            for t in range(TILES):
                pool.wait_ge(proj_free, M_QKV + 3 * TILES + t + 1)
                pool.dma_start(out_tile(v_rows, t), x[0:ROWS[t], t]).then_inc(kv_out, 16)
            for t in range(TILES):
                m = ROWS[t]
                pool.wait_ge(om_r, t + 1)
                ot = o[0:m, t].rearrange("p (h e) -> p h e", e=P)
                pool.tensor_tensor(ot, ot, subg[0:m].unsqueeze(1).broadcast_to([m, HEADS, P]), ALU.mult).then_inc(om_g, 1)
            pool.wait_ge(kv_out, 16 * TILES)
            pool.wait_ge(park_out, 16 * TILES)
            pool.wait_ge(sm_o, 1)
            pool.wait_ge(at_o, 4 * HEADS)
            for t in range(TILES):
                pool.dma_start(x[0:ROWS[t], t], dram_tile(t, x_parked)).then_inc(park_in, 16)
            pool.wait_ge(om_g, TILES)
            moe_pool(1)
            y_tiles = [y_prompt[0], y_sample.rearrange("b t d -> (b t) d")]
            for t in range(TILES):
                pool.wait_ge(ln_out, 4 * TILES + t + 1)
                pool.dma_start(out_tile(y_tiles, t), x[0:ROWS[t], t]).then_inc(y_out, 16)
            pool.wait_ge(y_out, 16 * TILES)
            pool.wait_ge(vs_out, 16)
            for t in range(TILES):
                pool.wait_ge(stg_out[t], 32)

        @block.scalar
        def _(act):
            act.dma_start(con[:], a["con"]).then_inc(con_in, 16)
            act.dma_start(con16[:], a["con16"]).then_inc(con_in, 16)

            def split_high(key, n, slot, src, landed, count):
                act.wait_ge(landed, count)
                if not (isinstance(n, int) and n < SPLIT_SLOTS):
                    act.wait_ge(used[key], n - SPLIT_SLOTS + 1)
                act.activation(wh[:, slot], src, ACT.Copy).then_inc(high[key], 1)

            def split_a(s):
                c = s + (s >= A_WS)
                split_high("a", s, s % SPLIT_SLOTS, raw[:, c % RAW_SLOTS], raw_a[c % RAW_SLOTS], landed_a(c))

            def split_b(s):
                c = s if s < B_CACHE else s - B_CACHE + B_WO
                split_high("b", s, s % SPLIT_SLOTS, raw[:, c % RAW_SLOTS], raw_b[c % RAW_SLOTS], landed_b[c])

            def turn_high(n0):
                for n in (n0, n0 + 1):
                    t, half = n % 10 // 2, n % 2
                    act.wait_ge(tr_done, n + 1)
                    act.activation(xTh[:, 4 * half:4 * half + 4, t * P:t * P + ROWS[t]],
                                   ps[:, 6 + n % 2].rearrange("p (k m) -> p k m", k=4)[:, :, 0:ROWS[t]],
                                   ACT.Copy).then_inc(tr_high, 1)

            def gelu(dst, m0, cols):
                for t in range(TILES):
                    act.wait_ge(proj_free, m0 + t + 1)
                    w = dst[0:ROWS[t], t, cols:cols + HALF]
                    act.activation(w, w, ACT.Gelu_apprx_tanh).then_inc(gelu_done, 1)

            def normalise(call, src):
                act.wait_ge(ln_var, call + 1)
                act.activation(lns[:, 1], lns[:, 0], ACT.Sqrt).then_inc(ln_std, 1)
                act.wait_ge(ln_rs, call + 1)
                for t in range(TILES):
                    m = ROWS[t]
                    act.activation(src[0:m, t], src[0:m, t], ACT.Identity, bias=lns[0:m, 3, t:t + 1],
                                   scale=lns[0:m, 2, t:t + 1]).then_inc(ln_norm, 1)

            act.wait_ge(xT0_in, 32)
            for half in range(2):
                act.activation(xTh[:, 4 * half:4 * half + 4], xT0[:, 4 * half:4 * half + 4], ACT.Copy).then_inc(x0_high, 1)
            split_a(0)
            split_a(1)
            act.wait_ge(rw_in, 16)
            act.activation(rwh[:], rw_raw[:], ACT.Copy).then_inc(rw_high, 1)
            for j in range(4):
                split_a(2 * j + 2)
                split_a(2 * j + 3)
                if j == 2:
                    normalise(0, v)
                gelu(v if j < 2 else u, M_WIN + 5 * j, j % 2 * HALF)
            for t in range(TILES):
                turn_high(T_US + 2 * t)
            split_a(10)
            split_a(11)

            def moe_act(l, first_used, base_key):
                s, key = moe[l], f"m{l}"

                def split(n, slot, q, i):
                    split_high(key, n, slot, raw[:, q], raw_m[l][q], 16 * (i + 1))

                for n in range(3):
                    act.wait_ge(used[base_key], first_used[n])
                    split(n, n, n, 0)
                act.wait_ge(logit_max, l + 1)
                act.activation(prob[:], lg[:], ACT.Exp).then_inc(exp_r, 1)

                def xg_high(i):
                    act.wait_ge(s["xg_tr"], i + 1)
                    act.activation(xgTh[:], ps[:, 2:4].rearrange("p a (k m) -> p (a k) m", m=P), ACT.Copy
                                   ).then_inc(s["xg_high"], 1)

                def silu(i):
                    act.wait_ge(used[key], 6 * i + 2 if not (isinstance(i, int) and i == 0) else 4)
                    after(act, s["h_ready"], i)
                    act.activation(sg[:], ps[:, 0], ACT.Silu).then_inc(s["silu"], 1)

                def h_high(i):
                    act.wait_ge(s["h_tr"], i + 1)
                    act.activation(hTh[:], ps[:, 6].rearrange("p (k m) -> p k m", k=4), ACT.Copy
                                   ).then_inc(s["h_high"], 1)

                def y_out_(i, n_last):
                    act.wait_ge(used[key], n_last)
                    after(act, s["scattered"], 16 * i)
                    act.activation(yb[:], ps[:, 4:6].rearrange("p a n -> p (a n)"), ACT.Copy).then_inc(s["y_ready"], 1)

                def body(i, first=False):
                    split(6 * i - 2, 1, 0, i)
                    split(6 * i - 1, 2, 1, i)
                    if not first:
                        y_out_(i - 2, 6 * i - 2)
                    h_high(i - 1)
                    for q in range(2, 4):
                        split(6 * i - 2 + q, (q + 1) % 3, q, i)
                    for r in range(2):
                        split(6 * i + 2 + r, (r + 5) % 3, 4 + r, i - 1)
                    silu(i)
                    xg_high(i + 1)

                xg_high(0)
                split(3, 0, 3, 0)
                silu(0)
                xg_high(1)
                body(1, True)
                body(2)
                act.wait_ge(plan, l + 1)
                blocks = act.value_load(table[0:1, LIST_COLS - 1:LIST_COLS], min_val=0, max_val=MAX_BLOCKS - EXPERTS) + EXPERTS
                with act.Fori(3, blocks) as i:
                    body(i)
                for r in range(2):
                    split(6 * blocks - 2 + r, r + 1, 4 + r, blocks - 1)
                y_out_(blocks - 2, 6 * blocks - 2)
                h_high(blocks - 1)
                y_out_(blocks - 1, 6 * blocks)
                return blocks

            normalise(1, x)
            for t in range(TILES):
                turn_high(T_LN1A + 2 * t)
            blocks = moe_act(0, [10, 11, 12], "a")
            act.wait_ge(used["m0"], 6 * blocks)
            split_b(0)
            split_b(1)
            normalise(2, x)
            for t in range(TILES):
                turn_high(T_LN2A + 2 * t)

            def kq_copy(kk):
                dst, cb, t = (KT if kk < 10 else QT), kk % 10 // 5, kk % 5
                act.wait_ge(kq_tr, kk + 1)
                act.activation(dst[:, 4 * cb:4 * cb + 4, t * P:t * P + ROWS[t]],
                               ps[:, 6 + kk % 2].rearrange("p (k m) -> p k m", k=4)[:, :, 0:ROWS[t]],
                               ACT.Copy).then_inc(kq_copied, 1)
            for j in range(6):
                if j < 5:
                    split_b(2 * j + 2)
                if j in (1, 2, 5):
                    for t in range(TILES):
                        kq_copy((0 if j < 5 else 10) + (j - 1) % 4 * 5 + t)
                if j < 5:
                    split_b(2 * j + 3)
            for t in range(TILES):
                kq_copy(15 + t)
            act.wait_ge(lam_sum, 1)
            act.activation(lamc[:, 2:4], lamc[:, 0:2], ACT.Exp).then_inc(lam_exp, 1)

            act.wait_ge(used["b"], B_CACHE)

            def att_exp(n):
                w = (n // HEADS + 1) * P
                act.wait_ge(at_max, n + 1)
                after(act, at_p, n - 1)
                for j in range(2):
                    e = act.activation(E[:, n % 2, j, 0:w], ps[:, 2 * (n % 2) + j, 0:w], ACT.Exp,
                                       bias=mxs[:, 1, n % 2, j:j + 1], scale=SCALE,
                                       accum_out=mxs[:, 2, n % 2, j:j + 1])
                e.then_inc(at_exp, 1)

            def att_pt(n):
                w = (n // HEADS + 1) * P
                act.wait_ge(at_pt, n + 1)
                after(act, at_pv, n - 1)
                act.activation(PTs[:, n % 2, 0:w], ps[:, 4 + n % 2, 0:w], ACT.Copy).then_inc(at_ptc, 1)

            def att_o(n):
                act.wait_ge(at_pv, n + 1)
                act.activation(o[:, n // HEADS, n % HEADS * P:(n % HEADS + 1) * P], ps[:, 6 + n % 2, 0:P],
                               ACT.Copy).then_inc(at_o, 1)
            steps = 4 * HEADS
            att_exp(0)
            for n in range(steps):
                if n + 1 < steps:
                    att_exp(n + 1)
                att_pt(n)
                if n >= 1:
                    att_o(n - 1)
            att_o(steps - 1)

            for g in range(4):
                for j in range(4):
                    n = 4 * g + j
                    act.wait_ge(sm_kt, n + 1)
                    if j in (0, 2):
                        after(act, sm_s, 2 * g + j // 2)
                    act.activation(kts[:, :, j % 2 * P:(j % 2 + 1) * P],
                                   ps[:, 2 * (n % 2):2 * (n % 2) + 2].rearrange("p a (h m) -> p (a h) m", m=P),
                                   ACT.Copy).then_inc(sm_ktc, 1)
                act.wait_ge(sm_max, g + 1)
                act.activation(Es[:], ps[:, 4, 0:288], ACT.Exp, bias=smx[:, 1:2], scale=SCALE,
                               accum_out=smx[:, 2:3]).then_inc(sm_exp, 1)
            act.wait_ge(sm_pv, 5)
            act.activation(o[0:NSAMP, 4], ps[0:NSAMP, 6:8].rearrange("p a n -> p (a n)"), ACT.Copy).then_inc(sm_o, 1)
            act.wait_ge(om_var, 1)
            act.activation(oss[:, 1], oss[:, 0], ACT.Sqrt).then_inc(om_std, 1)
            for t in range(TILES):
                turn_high(T_O + 2 * t)
            act.wait_ge(tr_low, T_O + 10)
            for s in range(12, 16):
                split_b(s)
            normalise(3, x)
            for t in range(TILES):
                turn_high(T_LN1B + 2 * t)
            moe_act(1, [16, 14, 15], "b")
            normalise(4, x)

        @block.vector
        def _(dve):
            chain = [0]

            def link(ins):
                chain[0] += 1
                ins.then_inc(dve_step, 1)
                dve.wait_ge(dve_step, chain[0])

            def split_low(key, n, slot, src):
                dve.wait_ge(high[key], n + 1)
                dve.tensor_tensor(wl[:, slot], src, wh[:, slot].bitcast(F32), ALU.subtract).then_inc(low[key], 1)

            def split_a(s):
                split_low("a", s, s % SPLIT_SLOTS, raw[:, (s + (s >= A_WS)) % RAW_SLOTS])

            def split_b(s):
                c = s if s < B_CACHE else s - B_CACHE + B_WO
                split_low("b", s, s % SPLIT_SLOTS, raw[:, c % RAW_SLOTS])

            def turn_low(n0):
                for n in (n0, n0 + 1):
                    t, half = n % 10 // 2, n % 2
                    dve.wait_ge(tr_high, n + 1)
                    w = (slice(None), slice(4 * half, 4 * half + 4), slice(t * P, t * P + ROWS[t]))
                    dve.tensor_tensor(xTl[w], ps[:, 6 + n % 2].rearrange("p (k m) -> p k m", k=4)[:, :, 0:ROWS[t]],
                                      xTh[w].bitcast(F32), ALU.subtract).then_inc(tr_low, 1)

            def ln_stats(t, src):
                m = ROWS[t]
                dve.bn_stats(stats[0:m, t, 0], src[0:m, t, 0:HALF])
                link(dve.bn_stats(stats[0:m, t, 1], src[0:m, t, HALF:D]))
                link(dve.bn_aggr(mv[0:m, t], stats[0:m, t].rearrange("p a b -> p (a b)")))

            def ln_scale(call):
                dve.tensor_scalar(lns[:, 0], mv[:, :, 1], EPS, None, ALU.add).then_inc(ln_var, 1)
                dve.wait_ge(ln_std, call + 1)
                link(dve.reciprocal(lns[:, 2], lns[:, 1]))
                dve.scalar_tensor_tensor(out=lns[:, 3], in0=mv[:, :, 0], scalar=-1.0, in1=lns[:, 2],
                                         op0=ALU.mult, op1=ALU.mult).then_inc(ln_rs, 1)

            def ln_shift(call, t, src):
                m = ROWS[t]
                dve.wait_ge(ln_gain, TILES * call + t + 1)
                dve.tensor_tensor(src[0:m, t], src[0:m, t], gb[0:m, D:2 * D], ALU.add).then_inc(ln_out, 1)

            def residual(m_step, t, cb):
                m = ROWS[t]
                dve.wait_ge(proj_done, m_step + 1)
                w = x[0:m, t, cb * HALF:(cb + 1) * HALF]
                dve.scalar_tensor_tensor(out=w, in0=w, scalar=ALPHA, in1=ps[0:m, m_step % PROJ_BANKS],
                                         op0=ALU.mult, op1=ALU.add).then_inc(proj_free, 1)

            def ln_turned(call, t0, src):
                for t in range(TILES):
                    ln_shift(call, t, src)
                    if t:
                        turn_low(t0 + 2 * t - 2)
                turn_low(t0 + 2 * TILES - 2)

            link(dve.memset(mv[:], 1.0))
            dve.memset(wsm[:], 0.0).then_inc(wsm_zeroed, 1)
            for half in range(2):
                dve.wait_ge(x0_high, half + 1)
                w = (slice(None), slice(4 * half, 4 * half + 4))
                dve.tensor_tensor(xTl[w], xT0[w], xTh[w].bitcast(F32), ALU.subtract).then_inc(x0_low, 1)
            split_a(0)
            split_a(1)
            dve.wait_ge(rw_high, 1)
            dve.tensor_tensor(rwl[:], rw_raw[:], rwh[:].bitcast(F32), ALU.subtract).then_inc(rw_low, 1)
            dve.wait_ge(rw_low, 1)
            dve.wait_ge(gb_in, 16)
            for j in range(4):
                split_a(2 * j + 2)
                split_a(2 * j + 3)
                if j == 2:
                    for t in range(TILES):
                        dve.wait_ge(gelu_done, TILES + t + 1)
                        ln_stats(t, v)
                    ln_scale(0)
                if j == 3:
                    dve.wait_ge(mixc_in, 48)
                    dve.wait_ge(raw_a[A_WS % RAW_SLOTS], landed_a(A_WS))
                    w = raw[:, A_WS % RAW_SLOTS, 0:2].rearrange("p a (g t) -> p (a g) t", t=P)
                    dve.tensor_tensor(w, w, cmix[:, 0:P].unsqueeze(1).broadcast_to([P, HEADS, P]), ALU.mult
                                      ).then_inc(ws_masked, 1)
                    dve.wait_ge(wsm_in, 16 * DEC_B)
                    dve.tensor_tensor(wsm[:], wsm[:],
                                      cmix[0:NSAMP, P:P + NSAMP].unsqueeze(1).broadcast_to([NSAMP, HEADS, NSAMP]),
                                      ALU.mult).then_inc(ws_masked, 1)
                dst, cols = (v if j < 2 else u), j % 2 * HALF
                for t in range(TILES):
                    m, step = ROWS[t], M_WIN + 5 * j + t
                    dve.wait_ge(proj_done, step + 1)
                    bias = gb[0:m, WIN_COLS[j] * HALF:(WIN_COLS[j] + 1) * HALF]
                    dve.tensor_tensor(dst[0:m, t, cols:cols + HALF], ps[0:m, step % PROJ_BANKS], bias, ALU.add
                                      ).then_inc(proj_free, 1)
            for t in range(TILES):
                ln_shift(0, t, v)
            dve.wait_ge(gelu_done, 4 * TILES)
            for g in range(HEADS):
                step = M_MIX + g
                w = u[:, 0:4, g * P:(g + 1) * P]
                dve.wait_ge(proj_done, step + 1)
                dve.scalar_tensor_tensor(out=w, in0=ps[:, step % PROJ_BANKS].rearrange("p (c n) -> p c n", c=4),
                                         scalar=bsp[:, g:g + 1], in1=w, op0=ALU.add, op1=ALU.mult
                                         ).then_inc(proj_free, 1)
            for half in range(2):
                step = M_MIX + 8 + half
                dve.wait_ge(proj_done, step + 1)
                for j in range(4):
                    g = 4 * half + j
                    w = u[0:NSAMP, 4, g * P:(g + 1) * P]
                    ins = dve.scalar_tensor_tensor(out=w, in0=ps[0:NSAMP, step % PROJ_BANKS, j * P:(j + 1) * P],
                                                   scalar=bss[:, g:g + 1], in1=w, op0=ALU.add, op1=ALU.mult)
                ins.then_inc(proj_free, 1)
            for t in range(TILES):
                turn_low(T_US + 2 * t)
            split_a(10)
            split_a(11)
            dve.wait_ge(x_in, 16 * TILES)
            for cb in range(2):
                for t in range(TILES):
                    residual(M_WOUT + 5 * cb + t, t, cb)
                    if cb:
                        dve.wait_ge(proj_free, M_WOUT + 5 * cb + t + 1)
                        ln_stats(t, x)
            ln_scale(1)

            def route(l, m0):
                def first_max(out, val, mx, rank, n, work):
                    shape = [P, TILES, n]
                    link(dve.tensor_tensor(work, val, mx.unsqueeze(2).broadcast_to(shape), ALU.is_equal))
                    link(dve.tensor_tensor(work, work, rank.unsqueeze(1).broadcast_to(shape), ALU.mult))
                    link(dve.tensor_reduce(col[:, 11, 0], work, AX, ALU.max))
                    link(dve.tensor_tensor(out, work, col[:, 11, 0].unsqueeze(2).broadcast_to(shape), ALU.is_equal))

                full = [P, TILES, EXPERTS]
                bank = m0 % PROJ_BANKS
                link(dve.memset(lg[:], 0.0))
                dve.wait_ge(proj_done, m0 + 1)
                dve.wait_ge(rb_in, 16)
                dve.tensor_copy(lg[:, 0:4], ps[:, bank, 0:4 * EXPERTS].rearrange("p (t e) -> p t e", e=EXPERTS))
                link(dve.tensor_copy(lg[0:NSAMP, 4], ps[0:NSAMP, bank, 4 * EXPERTS:5 * EXPERTS]))
                dve.sem_inc(proj_free, 1)
                link(dve.tensor_reduce(col[:, 0, 0], lg[:], AX, ALU.max))
                dve.tensor_tensor(lg[:], lg[:], col[:, 0, 0].unsqueeze(2).broadcast_to(full), ALU.subtract
                                  ).then_inc(logit_max, 1)
                dve.wait_ge(exp_r, l + 1)
                link(dve.tensor_reduce(col[:, 1, 0], prob[:], AX, ALU.add))
                link(dve.reciprocal(col[:, 2, 0], col[:, 1, 0]))
                link(dve.tensor_tensor(prob[:], prob[:], col[:, 2, 0].unsqueeze(2).broadcast_to(full), ALU.mult))
                link(dve.tensor_tensor(sel[:], prob[:], rbias[:].unsqueeze(1).broadcast_to(full), ALU.add))
                s4 = sel[:].rearrange("p t (g e) -> p (t g) e", e=PER_GROUP)
                dve.tensor_tensor(hilo[:, 0], s4[:, :, 0::2], s4[:, :, 1::2], ALU.max)
                link(dve.tensor_tensor(hilo[:, 1], s4[:, :, 0::2], s4[:, :, 1::2], ALU.min))
                gv = [gsc[:, j].rearrange("p t g -> p (t g)") for j in range(4)]
                dve.tensor_tensor(gv[0], hilo[:, 0, :, 0], hilo[:, 0, :, 1], ALU.max)
                dve.tensor_tensor(gv[1], hilo[:, 0, :, 0], hilo[:, 0, :, 1], ALU.min)
                link(dve.tensor_tensor(gv[2], hilo[:, 1, :, 0], hilo[:, 1, :, 1], ALU.max))
                link(dve.tensor_tensor(gv[1], gv[1], gv[2], ALU.max))
                link(dve.tensor_tensor(gv[0], gv[0], gv[1], ALU.add))
                link(dve.tensor_reduce(col[:, 3, 0], gsc[:, 0], AX, ALU.max))
                first_max(gsc[:, 3], gsc[:, 0], col[:, 3, 0], con[:, C_RK4:C_RK4 + 4], GROUPS, gsc[:, 2])
                link(dve.tensor_scalar(gsc[:, 1], gsc[:, 3], 1.0, -NEG, ALU.subtract, ALU.mult))
                four = [P, TILES * GROUPS, PER_GROUP]
                g3 = gsc[:, 3].rearrange("p t g -> p (t g)").unsqueeze(2).broadcast_to(four)
                g1 = gsc[:, 1].rearrange("p t g -> p (t g)").unsqueeze(2).broadcast_to(four)
                link(dve.tensor_tensor(s4, s4, g3, ALU.mult))
                link(dve.tensor_tensor(s4, s4, g1, ALU.add))
                link(dve.tensor_reduce(col[:, 4, 0], sel[:], AX, ALU.max))
                rk16 = con[:, C_RK16:C_RK16 + 16]
                first_max(oh[:, 0], sel[:], col[:, 4, 0], rk16, EXPERTS, tmp[:, 0])
                link(dve.scalar_tensor_tensor(out=sel[:], in0=oh[:, 0], scalar=3 * NEG, in1=sel[:],
                                              op0=ALU.mult, op1=ALU.add))
                link(dve.tensor_reduce(col[:, 5, 0], sel[:], AX, ALU.max))
                first_max(oh[:, 1], sel[:], col[:, 5, 0], rk16, EXPERTS, tmp[:, 0])
                both = [P, 2, TILES, EXPERTS]
                link(dve.tensor_tensor(tmp[:], oh[:], prob[:].unsqueeze(1).broadcast_to(both), ALU.mult))
                link(dve.tensor_reduce(gates[:], tmp[:], AX, ALU.add))
                link(dve.tensor_tensor(col[:, 6, 0], gates[:, 0], gates[:, 1], ALU.add))
                link(dve.reciprocal(col[:, 6, 1], col[:, 6, 0]))
                link(dve.tensor_tensor(gates[:], gates[:], col[:, 6, 1].unsqueeze(1).broadcast_to([P, 2, TILES]),
                                       ALU.mult))
                link(dve.tensor_tensor(oh[:], oh[:], con[:, C_VALID:C_VALID + TILES].unsqueeze(1).unsqueeze(3)
                                       .broadcast_to(both), ALU.mult))
                dve.tensor_tensor(m16[:], oh[:, 0], oh[:, 1], ALU.add).then_inc(masks, 1)
                dve.wait_ge(proj_done, m0 + 2)
                bank = (m0 + 1) % PROJ_BANKS
                rank = ps[:, bank, 0:TILES * EXPERTS].rearrange("p (t e) -> p t e", e=EXPERTS)
                link(dve.tensor_copy(cnt[:, 0], ps[:, bank, TILES * EXPERTS:(TILES + 1) * EXPERTS]))
                link(dve.tensor_tensor(tmp[:], oh[:], rank.unsqueeze(1).broadcast_to(both), ALU.mult))
                dve.sem_inc(proj_free, 1)
                link(dve.tensor_reduce(col[:, 0], tmp[:], AX, ALU.add))
                c_thr = con[:, C_THR:C_THR + 4]
                link(dve.tensor_tensor(thr[:, :, 0:4], cnt[:, 0].unsqueeze(2).broadcast_to([P, EXPERTS, 4]),
                                       c_thr.unsqueeze(1).broadcast_to([P, EXPERTS, 4]), ALU.is_gt))
                link(dve.tensor_reduce(cnt[:, 1], thr[:, :, 0:4], AX, ALU.add))
                link(dve.tensor_copy(cnt[:, 2], cnt[:, 1]))
                a_, b_ = 2, 3
                for sh in (1, 2, 4, 8):
                    dve.tensor_copy(cnt[:, b_, 0:sh], cnt[:, a_, 0:sh])
                    link(dve.tensor_tensor(cnt[:, b_, sh:16], cnt[:, a_, sh:16], cnt[:, a_, 0:16 - sh], ALU.add))
                    a_, b_ = b_, a_
                incl = cnt[:, a_]
                link(dve.tensor_tensor(cnt[:, 4], incl, cnt[:, 1], ALU.subtract))
                link(dve.tensor_tensor(tmp[:], oh[:], cnt[:, 4].unsqueeze(1).unsqueeze(1).broadcast_to(both), ALU.mult))
                link(dve.tensor_reduce(col[:, 1], tmp[:], AX, ALU.add))
                link(dve.tensor_tensor(tmp[:], oh[:], con[:, C_IOTA16:C_IOTA16 + 16].unsqueeze(1).unsqueeze(1)
                                       .broadcast_to(both), ALU.mult))
                link(dve.tensor_reduce(col[:, 2], tmp[:], AX, ALU.add))
                link(dve.tensor_scalar(col[:, 3], col[:, 0], 1.0 * P, None, ALU.is_ge))
                for j in range(2, 5):
                    link(dve.scalar_tensor_tensor(out=col[:, 3], in0=col[:, 0], scalar=1.0 * P * j, in1=col[:, 3],
                                                  op0=ALU.is_ge, op1=ALU.add))
                link(dve.scalar_tensor_tensor(out=col[:, 4], in0=col[:, 3], scalar=-1.0 * P, in1=col[:, 0],
                                              op0=ALU.mult, op1=ALU.add))
                link(dve.tensor_tensor(col[:, 5], col[:, 1], col[:, 3], ALU.add))
                link(dve.scalar_tensor_tensor(out=col[:, 5], in0=col[:, 5], scalar=EXPERTS - 1.0, in1=col[:, 2],
                                              op0=ALU.add, op1=ALU.subtract))
                link(dve.scalar_tensor_tensor(out=col[:, 5], in0=col[:, 3], scalar=0.0, in1=col[:, 5],
                                              op0=ALU.is_gt, op1=ALU.mult))
                link(dve.tensor_tensor(col[:, 5], col[:, 5], col[:, 2], ALU.add))
                iota = con[:, C_IOTA:C_IOTA + P]
                for k in range(2):
                    for t in range(TILES):
                        n = k * TILES + t
                        dve.tensor_scalar(lo16[:, n], iota, col[:, 4, k, t:t + 1], None, ALU.is_equal)
                        ins = dve.tensor_scalar(hi16[:, n, 0:LIST_COLS], iota[:, 0:LIST_COLS], col[:, 5, k, t:t + 1],
                                                con[:, C_ID1 + n:C_ID1 + n + 1], ALU.is_equal, ALU.mult)
                ins.then_inc(onehots, 1)
                link(dve.tensor_tensor(thr[:, 0:8], incl.unsqueeze(1).broadcast_to([P, 8, EXPERTS]),
                                       con[:, C_IOTA8:C_IOTA8 + 8].unsqueeze(2).broadcast_to([P, 8, EXPERTS]),
                                       ALU.is_le))
                link(dve.tensor_copy(tblf[:, 0:EXPERTS], con[:, C_IOTA16:C_IOTA16 + 16]))
                link(dve.tensor_reduce(tblf[:, EXPERTS:MAX_BLOCKS], thr[:, 0:8], AX, ALU.add))
                link(dve.tensor_scalar(tblf[:, 0:MAX_BLOCKS], tblf[:, 0:MAX_BLOCKS], EXPERTS - 1.0, None, ALU.min))
                link(dve.tensor_copy(tblf[:, MAX_BLOCKS:LIST_COLS], incl[:, 15:16]))
                dve.tensor_copy(table[:], tblf[:])
                dve.wait_ge(proj_done, m0 + 3)
                val = ps[:, (m0 + 2) % PROJ_BANKS, 0:LIST_COLS]
                link(dve.tensor_scalar(lst[:, 0], val, 0.0, NO_ROW, ALU.is_equal, ALU.mult))
                link(dve.tensor_scalar(lst[:, 1], val, 1.0, None, ALU.subtract))
                dve.sem_inc(proj_free, 1)
                link(dve.tensor_tensor(lst[:, 0], lst[:, 0], lst[:, 1], ALU.add))
                link(dve.tensor_copy(sidx[:], lst[:, 0]))
                link(dve.tensor_scalar(lst[:, 1], lst[:, 1], 0.0, None, ALU.max))
                link(dve.tensor_scalar(lst[:, 2], lst[:, 1], 1.0 * NTOK, -1.0 * NTOK, ALU.is_ge, ALU.mult))
                link(dve.tensor_tensor(lst[:, 1], lst[:, 1], lst[:, 2], ALU.add))
                link(dve.tensor_copy(gidx[:], lst[:, 1]))
                dve.sem_inc(plan, 1)

            def moe_dve(l, m0):
                s, key = moe[l], f"m{l}"

                def split(n, slot, q):
                    split_low(key, n, slot, raw[:, q])

                for n in range(3):
                    split(n, n, n)
                route(l, m0)

                def xg_low(i):
                    dve.wait_ge(s["xg_high"], i + 1)
                    dve.tensor_tensor(xgTl[:], ps[:, 2:4].rearrange("p a (k m) -> p (a k) m", m=P),
                                      xgTh[:].bitcast(F32), ALU.subtract).then_inc(s["xg_low"], 1)

                def gate_up(i):
                    dve.wait_ge(s["silu"], i + 1)
                    after(dve, s["h_tr"], i)
                    dve.tensor_tensor(hb[:], sg[:], ps[:, 1], ALU.mult).then_inc(s["h_ready"], 1)

                def h_low(i):
                    dve.wait_ge(s["h_high"], i + 1)
                    dve.tensor_tensor(hTl[:], ps[:, 6].rearrange("p (k m) -> p k m", k=4), hTh[:].bitcast(F32),
                                      ALU.subtract).then_inc(s["h_low"], 1)

                def body(i):
                    split(6 * i - 2, 1, 0)
                    split(6 * i - 1, 2, 1)
                    h_low(i - 1)
                    for q in range(2, 4):
                        split(6 * i - 2 + q, (q + 1) % 3, q)
                    for r in range(2):
                        split(6 * i + 2 + r, (r + 5) % 3, 4 + r)
                    gate_up(i)
                    xg_low(i + 1)

                xg_low(0)
                split(3, 0, 3)
                gate_up(0)
                xg_low(1)
                blocks = dve.value_load(table[0:1, LIST_COLS - 1:LIST_COLS], min_val=0, max_val=MAX_BLOCKS - EXPERTS) + EXPERTS
                with dve.Fori(1, blocks) as i:
                    body(i)
                for r in range(2):
                    split(6 * blocks - 2 + r, r + 1, 4 + r)
                h_low(blocks - 1)

            def combine(l):
                s = moe[l]
                for t in range(TILES):
                    m = ROWS[t]
                    y1, y2 = yl[0:m, t % 2, 0], yl[0:m, t % 2, 1]
                    dve.wait_ge(s[f"y_in{t % 2}"], 32 * (t // 2 + 1))
                    link(dve.tensor_scalar(y1, y1, gates[0:m, 0, t:t + 1], None, ALU.mult))
                    link(dve.scalar_tensor_tensor(out=y1, in0=y2, scalar=gates[0:m, 1, t:t + 1], in1=y1,
                                                  op0=ALU.mult, op1=ALU.add))
                    dve.scalar_tensor_tensor(out=x[0:m, t], in0=x[0:m, t], scalar=ALPHA, in1=y1,
                                             op0=ALU.mult, op1=ALU.add).then_inc(s["y_used"], 1)
                    dve.wait_ge(s["y_used"], t + 1)
                    ln_stats(t, x)

            ln_turned(1, T_LN1A, x)
            moe_dve(0, M_ROUTE_A)
            split_b(0)
            split_b(1)
            combine(0)
            ln_scale(2)
            ln_turned(2, T_LN2A, x)

            for j in range(6):
                if j < 5:
                    split_b(2 * j + 2)
                    split_b(2 * j + 3)
                for t in range(TILES):
                    m, step = ROWS[t], M_QKV + 5 * j + t
                    if j in (2, 3):
                        dve.wait_ge(park_out, 16 * TILES)
                        dst = x[0:m, t, (j - 2) * HALF:(j - 1) * HALF]
                    else:
                        kk = (5 * j if j < 2 else 10 + 5 * (j - 4)) + t
                        after(dve, kq_tr, kk - 4)
                        if 5 <= kk < 15:
                            dve.wait_ge(stg_out[t], 16 * (kk // 5))
                        dst = stg[0:m, t]
                    dve.wait_ge(proj_done, step + 1)
                    dve.tensor_copy(dst, ps[0:m, step % PROJ_BANKS]).then_inc(proj_free, 1)

            dve.wait_ge(lam_in, 16 * 5)
            dve.wait_ge(used["b"], B_CACHE)
            lq = gb[:, 0:4 * HEAD_DIM].rearrange("p (a b d) -> p a b d", a=2, b=2)
            link(dve.tensor_tensor(lamp[:], lq[:, :, 0], lq[:, :, 1], ALU.mult))
            dve.tensor_reduce(lamc[:, 0:2], lamp[:], AX, ALU.add).then_inc(lam_sum, 1)
            dve.wait_ge(lam_exp, 1)
            link(dve.tensor_tensor(lamc[:, 4:5], lamc[:, 3:4], lamc[:, 2:3], ALU.subtract))
            link(dve.tensor_scalar(lamc[:, 5:6], lamc[:, 4:5], LAM_INIT, None, ALU.subtract))
            link(dve.tensor_tensor(lamc[:, 6:7], con[:, C_COEF + 1:C_COEF + 2], lamc[:, 5:6], ALU.mult))
            link(dve.tensor_tensor(lamc[:, 7:8], lamc[:, 6:7], con[:, C_COEF:C_COEF + 1], ALU.add))
            link(dve.memset(oss[:], 1.0))
            neg_lam, coef = lamc[:, 5:6], lamc[:, 7:8]

            def att_max(n):
                w = (n // HEADS + 1) * P
                pair = ps[:, 2 * (n % 2):2 * (n % 2) + 2]
                dve.wait_ge(at_s, n + 1)
                diag = pair[:, :, w - P:w]
                link(dve.tensor_tensor(diag, diag, con[:, C_CAUSAL:C_CAUSAL + P].unsqueeze(1)
                                       .broadcast_to([P, 2, P]), ALU.add))
                link(dve.tensor_reduce(mxs[:, 0, n % 2], pair[:, :, 0:w], AX, ALU.max))
                dve.tensor_scalar(mxs[:, 1, n % 2], mxs[:, 0, n % 2], -SCALE, None, ALU.mult).then_inc(at_max, 1)

            def att_p(n):
                w = (n // HEADS + 1) * P
                dve.wait_ge(at_exp, n + 1)
                link(dve.reciprocal(mxs[:, 3, n % 2], mxs[:, 2, n % 2]))
                e1, e2 = E[:, n % 2, 0, 0:w], E[:, n % 2, 1, 0:w]
                link(dve.tensor_scalar(e2, e2, mxs[:, 3, n % 2, 1:2], neg_lam, ALU.mult, ALU.mult))
                after(dve, at_pt, n - 1)
                dve.scalar_tensor_tensor(out=Pm[:, n % 2, 0:w], in0=e1, scalar=mxs[:, 3, n % 2, 0:1], in1=e2,
                                         op0=ALU.mult, op1=ALU.add).then_inc(at_p, 1)
            steps = 4 * HEADS
            att_max(0)
            for n in range(steps):
                if n + 1 < steps:
                    att_max(n + 1)
                att_p(n)

            dve.wait_ge(at_pv, steps)
            dve.wait_ge(kq_tr, 20)
            link(dve.memset(qpad[:], 0.0))
            for g in range(4):
                after(dve, sm_s, 2 * g)
                for b2 in range(2):
                    b = 2 * g + b2
                    for part in range(2):
                        r = slice(64 * part, 64 * part + 64)
                        wide = qpad[r, b2 * 1088:(b2 + 1) * 1088].rearrange("p (h c) -> p h c", c=136)
                        ins = dve.tensor_copy(wide[:, :, 4 * part:4 * part + 4],
                                              QT[r, :, SEQ + b * DEC_T:SEQ + (b + 1) * DEC_T])
                ins.then_inc(sm_q, 1)
                dve.wait_ge(sm_s, 2 * g + 2)
                new = ps[:, 4, 256:288]
                link(dve.tensor_tensor(new, new, con[:, C_SMASK + 32 * g:C_SMASK + 32 * g + 32], ALU.add))
                link(dve.tensor_reduce(smx[:, 0:1], ps[:, 4, 0:288], AX, ALU.max))
                dve.tensor_scalar(smx[:, 1:2], smx[:, 0:1], -SCALE, None, ALU.mult).then_inc(sm_max, 1)
                dve.wait_ge(sm_exp, g + 1)
                link(dve.reciprocal(smx[:, 3:4], smx[:, 2:3]))
                dve.tensor_scalar(Ps[:], Es[:], smx[:, 3:4], coef, ALU.mult, ALU.mult).then_inc(sm_p, 1)
                after(dve, sm_pv, g)
                link(dve.memset(ptz[:], 0.0))
                dve.wait_ge(sm_pt, g + 1)
                for b2 in range(2):
                    c0 = (2 * g + b2) * DEC_T
                    for page in range(3):
                        m, dst = (P, ptz[:, page, b2]) if page < 2 else (NSAMP, ptn[:])
                        rows = ps[0:m, 5, page * P + b2 * 64:page * P + b2 * 64 + 64].rearrange(
                            "p (h a q) -> p h a q", a=2, q=DEC_T)
                        dve.tensor_copy(dst[:, :, c0:c0 + DEC_T], rows[:, :, 0])
                link(dve.memset(smx[:, 4:5], 0.0))
                for b2 in range(2):
                    c0 = (2 * g + b2) * DEC_T
                    for page in range(3):
                        m, dst = (P, ptz[:, page, b2]) if page < 2 else (NSAMP, ptn[:])
                        rows = ps[0:m, 5, page * P + b2 * 64:page * P + b2 * 64 + 64].rearrange(
                            "p (h a q) -> p h a q", a=2, q=DEC_T)
                        w = dst[:, :, c0:c0 + DEC_T]
                        ins = dve.tensor_tensor(w, w, rows[:, :, 1], ALU.add)
                ins.then_inc(sm_ptz, 1)

            dve.wait_ge(at_o, steps)
            dve.wait_ge(sm_o, 1)
            for t in range(TILES):
                m = ROWS[t]
                link(dve.tensor_tensor(osq[0:m], o[0:m, t], o[0:m, t], ALU.mult))
                link(dve.tensor_reduce(oss[0:m, 2, t], osq[0:m].rearrange("p (h e) -> p h e", e=P), AX, ALU.add))
            dve.tensor_scalar(oss[:, 0], oss[:, 2], 1.0 / P, EPS, ALU.mult, ALU.add).then_inc(om_var, 1)
            dve.wait_ge(om_std, 1)
            link(dve.reciprocal(oss[:, 2], oss[:, 1]))
            link(dve.tensor_scalar(oss[:, 2], oss[:, 2], 1.0 - LAM_INIT, None, ALU.mult))
            for t in range(TILES):
                m = ROWS[t]
                ot = o[0:m, t].rearrange("p (h e) -> p h e", e=P)
                dve.tensor_tensor(ot, ot, oss[0:m, 2, t].unsqueeze(2).broadcast_to([m, HEADS, P]), ALU.mult
                                  ).then_inc(om_r, 1)
            for t in range(TILES):
                turn_low(T_O + 2 * t)
            split_b(12)
            split_b(13)
            dve.wait_ge(park_in, 16 * TILES)
            for cb in range(2):
                for t in range(TILES):
                    residual(M_WO + 5 * cb + t, t, cb)
                    if cb:
                        dve.wait_ge(proj_free, M_WO + 5 * cb + t + 1)
                        ln_stats(t, x)
                if cb == 0:
                    split_b(14)
                    split_b(15)
            ln_scale(3)
            ln_turned(3, T_LN1B, x)
            moe_dve(1, M_ROUTE_B)
            combine(1)
            ln_scale(4)
            for t in range(TILES):
                ln_shift(4, t, x)

        @block.tensor
        def _(pe):
            def three(out, high_, low_, w_high, w_low, start, stop):
                pe.matmul(out, high_, w_high, start=start, stop=False)
                pe.matmul(out, high_, w_low, start=False, stop=False)
                return pe.matmul(out, low_, w_high, start=False, stop=stop)

            def bank_for(step):
                after(pe, proj_free, step - PROJ_BANKS + 1)
                return step % PROJ_BANKS

            def project(key, s0, m0, between=None):
                for kh in range(2):
                    s = s0 + kh
                    pe.wait_ge(low[key], s + 1)
                    for t in range(TILES):
                        bank = (m0 + t) % PROJ_BANKS
                        if kh == 0:
                            bank_for(m0 + t)
                        tok = slice(t * P, t * P + ROWS[t])
                        for j in range(4):
                            k = 4 * kh + j
                            mm = three(ps[0:ROWS[t], bank], xTh[:, k, tok], xTl[:, k, tok],
                                       wh[:, s % SPLIT_SLOTS, j], wl[:, s % SPLIT_SLOTS, j],
                                       start=(k == 0), stop=(k == KT_D - 1))
                            if k == KT_D - 1 and t < TILES - 1:
                                mm.then_inc(proj_done, 1)
                        if kh == 0 and between:
                            between(t)
                    if kh == 0:
                        mm.then_inc(used[key], 1)
                    else:
                        mm.then_inc(proj_done, 1)
                        pe.wait_ge(proj_done, m0 + TILES)
                        pe.sem_inc(used[key], 1)

            def turn(t, n0, src):
                m = ROWS[t]
                for half in range(2):
                    n = n0 + 2 * t + half
                    after(pe, tr_low, n - 1)
                    for j in range(4):
                        k = 4 * half + j
                        mm = pe.transpose(ps[:, 6 + n % 2, j * P:j * P + m], src[0:m, t, k * P:(k + 1) * P],
                                          ident[0:m, 0:m])
                    mm.then_inc(tr_done, 1)

            pe.wait_ge(con_in, 32)
            pe.wait_ge(x0_low, 2)
            for j in range(4):
                project("a", 2 * j, M_WIN + 5 * j)
            pe.wait_ge(ln_out, TILES)
            pe.wait_ge(ws_masked, 2)
            ws = raw[:, A_WS % RAW_SLOTS, 0:2].rearrange("p a (g t) -> p (a g) t", t=P)
            for g in range(HEADS):
                bank = bank_for(M_MIX + g)
                mm = pe.matmul(ps[:, bank].rearrange("p (c n) -> p c n", c=4), ws[:, g], v[:, 0:4, g * P:(g + 1) * P],
                               start=True, stop=True)
                mm.then_inc(proj_done, 1)
            for half in range(2):
                bank = bank_for(M_MIX + 8 + half)
                for j in range(4):
                    g = 4 * half + j
                    mm = pe.matmul(ps[0:NSAMP, bank, j * P:(j + 1) * P], wsm[:, g], v[0:NSAMP, 4, g * P:(g + 1) * P],
                                   start=True, stop=True)
                mm.then_inc(proj_done, 1)
            pe.wait_ge(proj_done, M_MIX + 8)
            pe.sem_inc(mix_done, 1)
            pe.wait_ge(proj_free, M_MIX + 10)
            for t in range(TILES):
                turn(t, T_US, u)
            pe.wait_ge(tr_low, T_US + 10)
            for cb in range(2):
                project("a", 8 + 2 * cb, M_WOUT + 5 * cb)

            def route(l, m0, t0):
                pe.wait_ge(tr_low, t0 + 10)
                pe.wait_ge(rw_low, 1)
                bank = bank_for(m0)
                for t in range(TILES):
                    tok = slice(t * P, t * P + ROWS[t])
                    for k in range(KT_D):
                        mm = three(ps[0:ROWS[t], bank, t * EXPERTS:(t + 1) * EXPERTS], xTh[:, k, tok], xTl[:, k, tok],
                                   rwh[:, k], rwl[:, k], start=(k == 0), stop=(k == KT_D - 1))
                mm.then_inc(proj_done, 1)
                before, ones = con16[:, 0:P], con16[:, P:2 * P]
                bank = bank_for(m0 + 1)
                pe.wait_ge(masks, l + 1)
                for t in range(TILES + 1):
                    for b in range(min(t + 1, TILES)):
                        mm = pe.matmul(ps[:, bank, t * EXPERTS:(t + 1) * EXPERTS], before if b == t else ones, m16[:, b],
                                       start=(b == 0), stop=(b == min(t, TILES - 1)))
                mm.then_inc(proj_done, 1)
                bank = bank_for(m0 + 2)
                pe.wait_ge(onehots, l + 1)
                for n in range(2 * TILES):
                    mm = pe.matmul(ps[:, bank, 0:LIST_COLS], lo16[:, n], hi16[:, n, 0:LIST_COLS],
                                   start=(n == 0), stop=(n == 2 * TILES - 1))
                mm.then_inc(proj_done, 1)

            def moe_pe(l, m_end):
                s, key = moe[l], f"m{l}"
                pe.wait_ge(proj_free, m_end)

                def up(i, n0):
                    pe.wait_ge(s["xg_low"], i + 1)
                    after(pe, s["h_ready"], i)
                    for q in range(4):
                        slot = (q + 1) % 3 if n0 else q % 3
                        pe.wait_ge(low[key], (6 * i - 2 + q if n0 else q) + 1)
                        for j in range(4):
                            k = 4 * (q % 2) + j
                            mm = three(ps[:, q // 2], xgTh[:, k], xgTl[:, k], wh[:, slot, j], wl[:, slot, j],
                                       start=(k == 0), stop=(k == KT_D - 1))
                        mm.then_inc(used[key], 1)

                def turn_x(i):
                    pe.wait_ge(s["gathered"], 16 * (i + 1))
                    after(pe, s["xg_low"], i)
                    for k in range(KT_D):
                        mm = pe.transpose(ps[:, 2 + k // 4, k % 4 * P:(k % 4 + 1) * P], xg[:, k * P:(k + 1) * P], ident)
                    mm.then_inc(s["xg_tr"], 1)

                def turn_h(i):
                    pe.wait_ge(s["h_ready"], i + 1)
                    after(pe, s["h_low"], i)
                    for k in range(4):
                        mm = pe.transpose(ps[:, 6, k * P:(k + 1) * P], hb[:, k * P:(k + 1) * P], ident)
                    mm.then_inc(s["h_tr"], 1)

                def down(i, n, slots):
                    pe.wait_ge(s["h_low"], i + 1)
                    after(pe, s["y_ready"], i)
                    for r in range(2):
                        pe.wait_ge(low[key], n + r + 1)
                        for j in range(4):
                            mm = three(ps[:, 4 + r], hTh[:, j], hTl[:, j], wh[:, slots[r], j], wl[:, slots[r], j],
                                       start=(j == 0), stop=(j == 3))
                        mm.then_inc(used[key], 1)

                turn_x(0)
                up(0, 0)
                turn_x(1)
                turn_h(0)
                pe.wait_ge(plan, l + 1)
                blocks = pe.value_load(table[0:1, LIST_COLS - 1:LIST_COLS], min_val=0, max_val=MAX_BLOCKS - EXPERTS) + EXPERTS

                def body(i):
                    up(i, 1)
                    turn_x(i + 1)
                    down(i - 1, 6 * i + 2, (2, 0))
                    turn_h(i)
                body(1)
                with pe.Fori(2, blocks) as i:
                    body(i)
                down(blocks - 1, 6 * blocks - 2, (1, 2))
                return blocks

            for t in range(TILES):
                pe.wait_ge(ln_out, TILES + t + 1)
                turn(t, T_LN1A, x)
            route(0, M_ROUTE_A, T_LN1A)
            blocks = moe_pe(0, M_QKV)
            for t in range(TILES):
                pe.wait_ge(ln_out, 2 * TILES + t + 1)
                turn(t, T_LN2A, x)
            pe.wait_ge(tr_low, T_LN2A + 10)
            pe.wait_ge(moe[0]["y_ready"], blocks)

            def turn_kq(kk, step):
                m = ROWS[kk % 5]
                pe.wait_ge(proj_free, step + 1)
                after(pe, kq_copied, kk - 1)
                for j in range(4):
                    mm = pe.transpose(ps[:, 6 + kk % 2, j * P:j * P + m], stg[0:m, kk % 5, j * P:(j + 1) * P],
                                      ident[0:m, 0:m])
                mm.then_inc(kq_tr, 1)
            for j in range(6):
                between = None
                if j in (1, 2, 5):
                    kk0 = 5 * (j - 1) if j < 5 else 10
                    def between(t, kk0=kk0, j=j):
                        turn_kq(kk0 + t, M_QKV + 5 * (j - 1) + t)
                project("b", 2 * j, M_QKV + 5 * j, between)
            for t in range(TILES):
                turn_kq(15 + t, M_QKV + 25 + t)

            def scores(n):
                qt, h = n // HEADS, n % HEADS
                w = (qt + 1) * P
                after(pe, at_exp, n - 1)
                for part in range(2):
                    r = slice(64 * part, 64 * part + 64)
                    mm = pe.matmul(ps[:, 2 * (n % 2) + part, 0:w], QT[r, h, qt * P:(qt + 1) * P], KT[r, h, 0:w],
                                   start=True, stop=True)
                mm.then_inc(at_s, 1)

            def turn_p(n):
                pe.wait_ge(at_p, n + 1)
                after(pe, at_ptc, n - 1)
                for b in range(n // HEADS + 1):
                    mm = pe.transpose(ps[:, 4 + n % 2, b * P:(b + 1) * P], Pm[:, n % 2, b * P:(b + 1) * P], ident)
                mm.then_inc(at_pt, 1)

            def values(n):
                qt, h = n // HEADS, n % HEADS
                pe.wait_ge(at_ptc, n + 1)
                after(pe, at_o, n - 1)
                for b in range(qt + 1):
                    mm = pe.matmul(ps[:, 6 + n % 2, 0:P], PTs[:, n % 2, b * P:(b + 1) * P], x[:, b, h * P:(h + 1) * P],
                                   start=(b == 0), stop=(b == qt))
                mm.then_inc(at_pv, 1)
            pe.wait_ge(kq_copied, 20)
            pe.wait_ge(proj_free, M_WO)
            steps = 4 * HEADS
            scores(0)
            for n in range(steps):
                if n + 1 < steps:
                    scores(n + 1)
                turn_p(n)
                if n >= 1:
                    values(n - 1)
            values(steps - 1)

            pe.wait_ge(at_o, steps)
            for g in range(4):
                def cache_chunk(j):
                    c = B_CACHE + 4 * g + j
                    return raw[:, c % RAW_SLOTS].rearrange("p (a k) n -> p a (k n)", a=2), c
                for b2 in range(2):
                    keys, c = cache_chunk(b2)
                    pe.wait_ge(raw_b[c % RAW_SLOTS], landed_b[c])
                    for page in range(2):
                        n = 4 * g + 2 * b2 + page
                        after(pe, sm_ktc, n - 1)
                        for h in range(HEADS):
                            mm = pe.transpose(ps[:, 2 * (n % 2) + h // 4, h % 4 * P:(h % 4 + 1) * P],
                                              keys[:, page, h * P:(h + 1) * P], ident)
                        mm.then_inc(sm_kt, 1)
                    pe.wait_ge(sm_ktc, 4 * g + 2 * b2 + 2)
                    pe.sem_inc(cache_used, 1)
                    if b2 == 0:
                        pe.wait_ge(sm_q, g + 1)
                        after(pe, sm_exp, g)
                    for h in range(HEADS):
                        lhs = qpad[:, (b2 * 8 + h) * P:(b2 * 8 + h + 1) * P]
                        edge = (b2 == 0 and h == 0, b2 == 1 and h == HEADS - 1)
                        pe.matmul(ps[:, 4, 0:256], lhs, kts[:, h], start=edge[0], stop=False, skip_group_check=True)
                        mm = pe.matmul(ps[:, 4, 256:288], lhs, KT[:, h, SEQ:NTOK], start=False, stop=edge[1],
                                       skip_group_check=True)
                    mm.then_inc(sm_s, 1)
                pe.wait_ge(sm_p, g + 1)
                after(pe, sm_ptz, g)
                pe.transpose(ps[:, 5, 0:P], Ps[:, 0:P], ident)
                pe.transpose(ps[:, 5, P:2 * P], Ps[:, P:2 * P], ident)
                pe.transpose(ps[0:NSAMP, 5, 2 * P:3 * P], Ps[:, 256:288], ident).then_inc(sm_pt, 1)
                pe.wait_ge(sm_ptz, g + 1)
                for b2 in range(2):
                    vals, c = cache_chunk(2 + b2)
                    pe.wait_ge(raw_b[c % RAW_SLOTS], landed_b[c])
                    for page in range(2):
                        for h in range(HEADS):
                            mm = pe.matmul(ps[0:NSAMP, 6 + h // 4, h % 4 * P:(h % 4 + 1) * P], ptz[:, page, b2, h],
                                           vals[:, page, h * P:(h + 1) * P],
                                           start=(g == 0 and b2 == 0 and page == 0 and h % 4 == 0), stop=False,
                                           skip_group_check=True)
                    mm.then_inc(cache_used, 1) if b2 == 0 else mm.then_inc(sm_pv, 1)
                pe.wait_ge(sm_pv, g + 1)
                pe.sem_inc(cache_used, 1)
            for h in range(HEADS):
                mm = pe.matmul(ps[0:NSAMP, 6 + h // 4, h % 4 * P:(h % 4 + 1) * P], ptn[:, h],
                               x[0:NSAMP, 4, h * P:(h + 1) * P], start=False, stop=(h % 4 == 3), skip_group_check=True)
            mm.then_inc(sm_pv, 1)

            pe.wait_ge(sm_o, 1)
            for t in range(TILES):
                pe.wait_ge(om_g, t + 1)
                turn(t, T_O, o)
            pe.wait_ge(tr_low, T_O + 10)
            for cb in range(2):
                project("b", B_CACHE + 2 * cb, M_WO + 5 * cb)
            for t in range(TILES):
                pe.wait_ge(ln_out, 3 * TILES + t + 1)
                turn(t, T_LN1B, x)
            route(1, M_ROUTE_B, T_LN1B)
            moe_pe(1, M_END)


IN_NAMES = ["con", "con16", "cmix", "x_prompt", "x_sample", "x_prompt_T", "x_sample_T", "w_s_T", "b_s_T", "b_s_rep",
            "cache_k", "cache_v", "page_table", "ln1_g", "ln1_b", "ln2_g", "ln2_b", "a_w_in", "a_b_in", "a_lnv_g",
            "a_lnv_b", "a_w_out", "w_k", "w_v", "b_w_q", "b_lam_q1", "b_lam_k1", "b_lam_q2", "b_lam_k2", "b_subln_g",
            "b_w_o", "router_w", "router_bias", "moe_w_up", "moe_w_down"]
OUT_SHAPES = [(1, SEQ, D), (DEC_B, DEC_T, D), (1, SEQ, HEADS, P), (1, SEQ, HEADS, P), (DEC_B, DEC_T, HEADS, P),
              (DEC_B, DEC_T, HEADS, P), (1, DEC_B, DEC_T, D)]


def kernel(**inputs):
    import concourse.bacc as bacc
    from concourse.bass_utils import run_bass_kernel_spmd

    arrays = {k: np.asarray(x) for k, x in inputs.items()}
    arrays["x_prompt_T"] = arrays["x_prompt"][0].T
    arrays["x_sample_T"] = arrays["x_sample"].reshape(NSAMP, D).T
    arrays["w_s_T"] = arrays["a_w_s"][0].transpose(2, 0, 1)
    arrays["b_s_T"] = arrays["a_b_s"][0].T
    arrays["b_s_rep"] = np.tile(arrays["a_b_s"][0, :, 0:DEC_T].T, (DEC_B, 1))
    arrays["con"], arrays["con16"], arrays["cmix"] = constants()

    nc = bacc.Bacc("TRN2", target_bir_lowering=False, num_devices=1)
    given, aps = {}, {}
    for name in IN_NAMES:
        arr = np.ascontiguousarray(arrays[name])
        given[f"in_{name}"] = arr
        aps[name] = nc.dram_tensor(f"in_{name}", arr.shape, mybir.dt.from_np(arr.dtype), kind="ExternalInput").ap()
    outs = [nc.dram_tensor(f"out_{i}", s, F32, kind="ExternalOutput").ap() for i, s in enumerate(OUT_SHAPES)]
    trunk(nc, aps, outs)
    r = run_bass_kernel_spmd(nc, [given], core_ids=[0])
    return tuple(r.results[0][f"out_{i}"] for i in range(len(OUT_SHAPES)))
```

```python
import math
from contextlib import ExitStack

import numpy as np

import concourse.bass as bass
from concourse import mybir

F32 = mybir.dt.float32
F32R = mybir.dt.float32r
F16 = mybir.dt.float16
I32 = mybir.dt.int32
ALU = mybir.AluOpType
ACT = mybir.ActivationFunctionType
AX = mybir.AxisListType.X

P = 128
D = 1024
KT_D = D // P
SEQ = 512
DEC_B, DEC_T = 8, 4
NSAMP = DEC_B * DEC_T
NTOK = SEQ + NSAMP
TILES = 5
ROWS = [P, P, P, P, NSAMP]
LAYERS = 2
ALPHA = (2.0 * LAYERS) ** 0.25
EPS = 1e-5
NEG = -1e30
HEADS = 8
HEAD_DIM = 64
SCALE = HEAD_DIM ** -0.5
LAM_INIT = 0.8 - 0.6 * math.exp(-0.3 * 1)
EXPERTS, GROUPS, PER_GROUP = 16, 4, 4
MAX_BLOCKS = EXPERTS + (2 * NTOK) // P
LIST_COLS = MAX_BLOCKS + 1
RAW_SLOTS = 6
SPLIT_SLOTS = 3
HALF = 512
PROJ_BANKS = 6
NO_ROW = 8192.0

A_WS, A_WOUT, A_CHUNKS, A_SPLITS = 8, 9, 13, 12
B_CACHE, B_WO, B_CHUNKS, B_SPLITS = 12, 28, 32, 16

M_WIN, M_MIX, M_WOUT, M_ROUTE_A, M_QKV, M_WO, M_ROUTE_B, M_END = 0, 20, 30, 40, 43, 73, 83, 86
T_US, T_LN1A, T_LN2A, T_O, T_LN1B = 0, 10, 20, 30, 40

C_IDENT, C_CAUSAL, C_IOTA, C_SMASK, C_RK4, C_RK16, C_IOTA16, C_IOTA8, C_THR, C_ID1, C_VALID, C_COEF, C_END = (
    0, 128, 256, 384, 512, 516, 532, 548, 556, 560, 570, 575, 577)


def constants():
    c = np.zeros((P, C_END), np.float32)
    i = np.arange(P)
    c[:, C_IDENT:C_IDENT + P] = np.eye(P)
    c[:, C_CAUSAL:C_CAUSAL + P] = np.where(i[None, :] <= i[:, None], 0.0, NEG)
    c[:, C_IOTA:C_IOTA + P] = i[None, :]
    row_b, row_q = i // 64, i % 4
    for g in range(4):
        j = np.arange(NSAMP)
        ok = (j[None, :] // DEC_T == 2 * g + row_b[:, None]) & (j[None, :] % DEC_T <= row_q[:, None])
        c[:, C_SMASK + 32 * g:C_SMASK + 32 * g + 32] = np.where(ok, 0.0, NEG)
    c[:, C_RK4:C_RK4 + 4] = 4 - np.arange(4)
    c[:, C_RK16:C_RK16 + 16] = 16 - np.arange(16)
    c[:, C_IOTA16:C_IOTA16 + 16] = np.arange(16)
    c[:, C_IOTA8:C_IOTA8 + 8] = np.arange(8)
    c[:, C_THR:C_THR + 4] = 128.0 * (1 + np.arange(4))
    for k in range(2):
        for t in range(TILES):
            c[:ROWS[t], C_ID1 + k * TILES + t] = k * NTOK + t * P + i[:ROWS[t]] + 1
    c[:, C_VALID:C_VALID + TILES] = 1.0
    c[NSAMP:, C_VALID + TILES - 1] = 0.0
    part = (i // 4) % 2
    c[:, C_COEF] = part == 0
    c[:, C_COEF + 1] = part == 1
    c16 = np.zeros((P, 2 * P), np.float16)
    c16[:, 0:P] = i[:, None] < i[None, :]
    c16[:, P:2 * P] = 1.0
    s = np.arange(NSAMP)
    cmix = np.zeros((P, P + NSAMP), np.float32)
    cmix[:, 0:P] = i[:, None] <= i[None, :]
    cmix[:NSAMP, P:] = (s[:, None] // DEC_T == s[None, :] // DEC_T) & (s[:, None] <= s[None, :])
    return c, c16, cmix


def last_before(slot, slots, count):
    return max(i for i in range(count) if i % slots == slot)


def trunk(nc, a, outs):
    y_prompt, y_sample, k_prompt, v_prompt, k_sample, v_sample, state_v = outs
    with ExitStack() as ctx:
        def sem(name):
            return ctx.enter_context(nc.semaphore(name))

        top = [(nc.sbuf_base + 63) // 64 * 64]

        def place(name, shape, dt, at=None):
            size = int(np.prod(shape[1:])) * (2 if dt == F16 else 4)
            off = top[0] if at is None else at
            t = nc.alloc_sbuf_tensor_at(name, shape, dt, offset=off)
            if at is None:
                top[0] += (size + 31) // 32 * 32
                assert top[0] <= nc.sbuf_usable_end
            assert off + size <= nc.sbuf_usable_end
            return t, off + (size + 31) // 32 * 32

        raw = place("raw", [P, RAW_SLOTS, 4, HALF], F32)[0]
        x = place("x", [P, TILES, D], F32)[0]
        xT_at = top[0]
        xTh = place("xTh", [P, KT_D, NTOK], F32R)[0]
        xTl = place("xTl", [P, KT_D, NTOK], F32R)[0]
        split_at = top[0]
        wh = place("wh", [P, SPLIT_SLOTS, 4, HALF], F32R)[0]
        wl = place("wl", [P, SPLIT_SLOTS, 4, HALF], F32R)[0]
        gb = place("gb", [P, 2 * D], F32)[0]
        con = place("con", [P, C_END], F32)[0]
        con16 = place("con16", [P, 2 * P], F16)[0]
        rwh = place("rwh", [P, KT_D, EXPERTS], F32R)[0]
        rwl = place("rwl", [P, KT_D, EXPERTS], F32R)[0]
        rbias = place("rbias", [P, EXPERTS], F32)[0]
        stats = place("stats", [P, TILES, 2, 6], F32)[0]
        mv = place("mv", [P, TILES, 2], F32)[0]
        lns = place("lns", [P, 4, TILES], F32)[0]
        gates = place("gates", [P, 2, TILES], F32)[0]
        gidx = place("gidx", [P, LIST_COLS], I32)[0]
        sidx = place("sidx", [P, LIST_COLS], I32)[0]
        gcur = place("gcur", [P, 1], I32)[0]
        scur = place("scur", [P, 1], I32)[0]
        table = place("table", [P, LIST_COLS], I32)[0]
        pages = place("pages", [P, 16], I32)[0]
        lamc = place("lamc", [P, 12], F32)[0]
        arena = top[0]
        u, n = place("u", [P, TILES, D], F32, arena)
        v, n = place("v", [P, TILES, D], F32, n)
        cmix, n = place("cmix", [P, P + NSAMP], F32, n)
        wsm, n = place("wsm", [NSAMP, HEADS, NSAMP], F32, n)
        bsp, n = place("bsp", [P, 8], F32, n)
        bss, n = place("bss", [NSAMP, 8], F32, n)
        xT0 = place("xT0", [P, KT_D, NTOK], F32, arena)[0]
        rw_raw = place("rw_raw", [P, KT_D, EXPERTS], F32, arena + 20480)[0]
        QT, n = place("QT", [P, HEADS, NTOK], F32, arena)
        KT, n = place("KT", [P, HEADS, NTOK], F32, n)
        stg, _ = place("stg", [P, TILES, HALF], F32, n)
        o, n = place("o", [P, TILES, D], F32, split_at)
        lamp, n = place("lamp", [P, 2, HEAD_DIM], F32, n)
        oss, n = place("oss", [P, 3, TILES, HEADS], F32, n)
        mxs, n = place("mxs", [P, 4, 2, 2], F32, n)
        osq, n = place("osq", [P, D], F32, n)
        E, n = place("E", [P, 2, 2, HALF], F32, n)
        Pm, n = place("Pm", [P, 2, HALF], F32, n)
        PTs, n = place("PTs", [P, 2, HALF], F32, n)
        assert n <= split_at + 2 * SPLIT_SLOTS * 4 * HALF * 4
        kts, n = place("kts", [P, 2, HEADS, 256], F32, xT_at)
        qpad, n = place("qpad", [P, 2176], F32, n)
        Es, n = place("Es", [P, 288], F32, n)
        Ps, n = place("Ps", [P, 288], F32, n)
        ptz, n = place("ptz", [P, 2, 2, HEADS, NSAMP], F32, n)
        ptn, n = place("ptn", [NSAMP, HEADS, NSAMP], F32, n)
        smx, n = place("smx", [P, 6], F32, n)
        assert n <= split_at
        subg = lamc[:, 8:9]
        xg, n = place("xg", [P, D], F32, arena)
        xgTh, n = place("xgTh", [P, KT_D, P], F32R, n)
        xgTl, n = place("xgTl", [P, KT_D, P], F32R, n)
        sg, n = place("sg", [P, HALF], F32, n)
        hb, n = place("hb", [P, HALF], F32, n)
        hTh, n = place("hTh", [P, 4, P], F32R, n)
        hTl, n = place("hTl", [P, 4, P], F32R, n)
        yb, n = place("yb", [P, D], F32, n)
        yl, _ = place("yl", [P, TILES, 2, D], F32, arena)
        lg, n = place("lg", [P, TILES, EXPERTS], F32, n)
        prob, n = place("prob", [P, TILES, EXPERTS], F32, n)
        sel, n = place("sel", [P, TILES, EXPERTS], F32, n)
        tmp, n = place("tmp", [P, 2, TILES, EXPERTS], F32, n)
        oh, n = place("oh", [P, 2, TILES, EXPERTS], F32, n)
        hilo, n = place("hilo", [P, 2, TILES * GROUPS, 2], F32, n)
        gsc, n = place("gsc", [P, 4, TILES, GROUPS], F32, n)
        col, n = place("col", [P, 12, 2, TILES], F32, n)
        cnt, n = place("cnt", [P, 6, EXPERTS], F32, n)
        thr, n = place("thr", [P, 16, 16], F32, n)
        tblf, n = place("tblf", [P, LIST_COLS], F32, n)
        lst, n = place("lst", [P, 4, LIST_COLS], F32, n)
        m16, n = place("m16", [P, TILES, EXPERTS], F16, n)
        lo16, n = place("lo16", [P, 2 * TILES, P], F16, n)
        hi16, n = place("hi16", [P, 2 * TILES, LIST_COLS + 1], F16, n)
        ps = nc.alloc_psum_tensor("ps", [P, 8, HALF], F32)

        x_rows = [nc.dram_tensor(f"x_rows{l}", (NTOK, D), F32).ap() for l in range(LAYERS)]
        y_rows = [nc.dram_tensor(f"y_rows{l}", (2 * NTOK, D), F32).ap() for l in range(LAYERS)]
        x_parked = nc.dram_tensor("x_parked", (NTOK, D), F32).ap()

        con_in = sem("con_in"); rb_in = sem("rb_in"); xT0_in = sem("xT0_in"); rw_in = sem("rw_in"); x_in = sem("x_in")
        mixc_in = sem("mixc_in"); wsm_in = sem("wsm_in"); gb_in = sem("gb_in"); lam_in = sem("lam_in")
        pages_in = sem("pages_in")
        zeroed = sem("zeroed"); x0_high = sem("x0_high"); x0_low = sem("x0_low")
        rw_high = sem("rw_high"); rw_low = sem("rw_low")
        wsm_zeroed = sem("wsm_zeroed"); ws_masked = sem("ws_masked")
        raw_a = [sem(f"raw_a{i}") for i in range(RAW_SLOTS)]
        raw_b = [sem(f"raw_b{i}") for i in range(RAW_SLOTS)]
        raw_m = [[sem(f"raw_m{l}_{i}") for i in range(RAW_SLOTS)] for l in range(LAYERS)]
        high = {k: sem(f"high_{k}") for k in ("a", "b", "m0", "m1")}
        low = {k: sem(f"low_{k}") for k in ("a", "b", "m0", "m1")}
        used = {k: sem(f"used_{k}") for k in ("a", "b", "m0", "m1")}
        mix_done = sem("mix_done")
        proj_done = sem("proj_done"); proj_free = sem("proj_free")
        gelu_done = sem("gelu_done")
        tr_done = sem("tr_done"); tr_high = sem("tr_high"); tr_low = sem("tr_low")
        ln_var = sem("ln_var"); ln_std = sem("ln_std"); ln_rs = sem("ln_rs"); ln_norm = sem("ln_norm")
        ln_gain = sem("ln_gain"); ln_out = sem("ln_out")
        dve_step = sem("dve_step")
        stg_out = [sem(f"stg_out{t}") for t in range(TILES)]
        vs_out = sem("vs_out"); x_out = sem("x_out"); park_out = sem("park_out"); park_in = sem("park_in")
        kv_out = sem("kv_out"); y_out = sem("y_out")
        kq_tr = sem("kq_tr"); kq_copied = sem("kq_copied")
        exp_r = sem("exp_r"); lam_exp = sem("lam_exp"); lam_sum = sem("lam_sum")
        at_s = sem("at_s"); at_max = sem("at_max"); at_exp = sem("at_exp"); at_p = sem("at_p")
        at_pt = sem("at_pt"); at_ptc = sem("at_ptc"); at_pv = sem("at_pv"); at_o = sem("at_o")
        sm_kt = sem("sm_kt"); sm_ktc = sem("sm_ktc"); sm_s = sem("sm_s"); sm_q = sem("sm_q")
        sm_max = sem("sm_max"); sm_exp = sem("sm_exp"); sm_p = sem("sm_p"); sm_pt = sem("sm_pt")
        sm_zero = sem("sm_zero"); sm_ptz = sem("sm_ptz"); sm_pv = sem("sm_pv"); sm_o = sem("sm_o")
        keys_used = sem("keys_used"); vals_used = sem("vals_used"); lnv_in = sem("lnv_in")
        om_var = sem("om_var"); om_std = sem("om_std"); om_r = sem("om_r"); om_g = sem("om_g")
        logit_max = sem("logit_max"); plan = sem("plan"); onehots = sem("onehots"); masks = sem("masks")
        moe = [{k: sem(f"{k}{l}") for k in (
            "gcopy", "gathered", "xg_tr", "xg_high", "xg_low", "silu", "h_ready", "h_tr", "h_high", "h_low",
            "y_ready", "scopy", "scattered", "y_in0", "y_in1", "y_in2", "y_in3", "y_in4", "xg_zero", "scaled")} for l in range(LAYERS)]

        ident = con[:, C_IDENT:C_IDENT + P]

        def after(eng, s, count):
            if not isinstance(count, int) or count > 0:
                eng.wait_ge(s, count)

        def dram_tile(t, ap):
            return ap[t * P:t * P + ROWS[t]]

        def chunk(w, kh, cb):
            return w[kh * HALF:(kh + 1) * HALF, cb * HALF:(cb + 1) * HALF].rearrange("(k p) n -> p k n", p=P)

        def down_chunk(w, cb):
            return w[:, cb * HALF:(cb + 1) * HALF].rearrange("(k p) n -> p k n", p=P)

        w_in, w_out = a["a_w_in"][0], a["a_w_out"][0]
        WIN_COLS = [2, 3, 0, 1]
        block = ctx.enter_context(nc.Block())
        low_a = {c: c + 1 - (c > A_WS) for c in range(A_CHUNKS) if c != A_WS}
        low_b = {c: c + 1 - (B_WO - B_CACHE) * (c >= B_WO) for c in range(B_CHUNKS) if not B_CACHE <= c < B_WO}
        landed_b = {c: sum(32 if B_CACHE <= d < B_WO else 16 for d in range(c % RAW_SLOTS, c + 1, RAW_SLOTS))
                    for c in range(B_CHUNKS)}

        def landed_a(c):
            return 16 * (c // RAW_SLOTS + 1)

        @block.sync
        def _(sp):
            def up(l, e, i, slot_free):
                for q in range(4):
                    slot_free(q)
                    sp.dma_start(raw[:, q], chunk(a["moe_w_up"][l, e], q % 2, q // 2)).then_inc(raw_m[l][q], 16)

            def down(l, e, i, slot_free):
                for r in range(2):
                    slot_free(4 + r)
                    sp.dma_start(raw[:, 4 + r], down_chunk(a["moe_w_down"][l, e], r)).then_inc(raw_m[l][4 + r], 16)

            def moe_stream(l, first_free):
                low_m = low[f"m{l}"]

                def previous(i):
                    def free(slot):
                        if slot < 4:
                            sp.wait_ge(low_m, (slot if isinstance(i, int) and i == 1 else 6 * (i - 1) - 2 + slot) + 1)
                        else:
                            sp.wait_ge(low_m, 6 * (i - 1) + 8 + (slot - 4) + 1)
                    return free
                up(l, 0, 0, first_free)
                down(l, 0, 0, first_free)
                up(l, 1, 1, previous(1))
                with sp.Fori(2, EXPERTS - 1) as i:
                    up(l, i, i, previous(i))
                    down(l, i - 1, i - 1, previous(i - 1))
                sp.wait_ge(plan, l + 1)
                blocks = sp.value_load(table[0:1, LIST_COLS - 1:LIST_COLS], min_val=0, max_val=MAX_BLOCKS - EXPERTS) + EXPERTS
                with sp.Fori(EXPERTS - 1, blocks) as i:
                    e = sp.value_load(table[0:1, bass.ds(i, 1)], min_val=0, max_val=EXPERTS - 1)
                    up(l, e, i, previous(i))
                    before = sp.value_load(table[0:1, bass.ds(i - 1, 1)], min_val=0, max_val=EXPERTS - 1)
                    down(l, before, i - 1, previous(i - 1))
                e = sp.value_load(table[0:1, bass.ds(blocks - 1, 1)], min_val=0, max_val=EXPERTS - 1)
                down(l, e, blocks - 1, previous(blocks - 1))
                return blocks

            sp.dma_start(xT0[:, :, 0:SEQ], a["x_prompt_T"].rearrange("(k p) n -> p k n", p=P)).then_inc(xT0_in, 16)
            sp.dma_start(xT0[:, :, SEQ:NTOK], a["x_sample_T"].rearrange("(k p) n -> p k n", p=P)).then_inc(xT0_in, 16)
            for c in range(A_CHUNKS):
                s = c % RAW_SLOTS
                if c >= RAW_SLOTS:
                    sp.wait_ge(low["a"], low_a[c - RAW_SLOTS])
                if c < A_WS:
                    src = chunk(w_in, c % 2, WIN_COLS[c // 2])
                elif c == A_WS:
                    src = a["w_s_T"].rearrange("s (a g) t -> s a (g t)", a=2)
                else:
                    src = chunk(w_out, (c - A_WOUT) % 2, (c - A_WOUT) // 2)
                sp.dma_start(raw[:, s, 0:src.shape[1]], src).then_inc(raw_a[s], 16)

            def after_a(slot):
                c = last_before(slot, RAW_SLOTS, A_CHUNKS)
                if c == A_WS:
                    sp.wait_ge(mix_done, 1)
                else:
                    sp.wait_ge(low["a"], low_a[c])
            blocks = moe_stream(0, after_a)

            sp.wait_ge(pages_in, 16)

            def cache_freed(c):
                pair, which, b2 = (c - B_CACHE) // 4, (c - B_CACHE) // 2 % 2, (c - B_CACHE) % 2
                sp.wait_ge(vals_used if which else keys_used, 2 * pair + b2 + 1)
            for c in range(B_CHUNKS):
                s = c % RAW_SLOTS
                if c < RAW_SLOTS:
                    sp.wait_ge(low["m0"], 6 * blocks - 7 + s if s < 4 else 6 * blocks - 1 + (s - 4))
                elif B_CACHE <= c - RAW_SLOTS < B_WO:
                    cache_freed(c - RAW_SLOTS)
                else:
                    sp.wait_ge(low["b"], low_b[c - RAW_SLOTS])
                if B_CACHE <= c < B_WO:
                    pair, which, b2 = (c - B_CACHE) // 4, (c - B_CACHE) // 2 % 2, (c - B_CACHE) % 2
                    cache = a["cache_v"] if which else a["cache_k"]
                    for page in range(2):
                        j = (2 * pair + b2) * 2 + page
                        phys = sp.value_load(pages[0:1, j:j + 1], min_val=0, max_val=cache.shape[0] - 1)
                        sp.dma_start(raw[:, s, 2 * page:2 * page + 2, :].rearrange("p k n -> p (k n)"),
                                     cache[phys].rearrange("r h d -> r (h d)")).then_inc(raw_b[s], 16)
                else:
                    w = [a["w_k"], a["w_v"], a["b_w_q"][0]][c // 4] if c < B_CACHE else a["b_w_o"][0]
                    sp.dma_start(raw[:, s], chunk(w, c % 2, c // 2 % 2)).then_inc(raw_b[s], 16)

            def after_b(slot):
                c = last_before(slot, RAW_SLOTS, B_CHUNKS)
                if B_CACHE <= c < B_WO:
                    cache_freed(c)
                else:
                    sp.wait_ge(low["b"], low_b[c])
            moe_stream(1, after_b)

        @block.gpsimd
        def _(pool):
            def row(ap):
                return ap.unsqueeze(0).broadcast_to([P, ap.shape[0]])

            def load_gb(g, b):
                pool.dma_start(gb[:, 0:D], row(g)).then_inc(gb_in, 16)
                pool.dma_start(gb[:, D:2 * D], row(b)).then_inc(gb_in, 16)

            def gain(call, src):
                if call:
                    pool.wait_ge(gb_in, 16 + 32 * call)
                else:
                    pool.wait_ge(lnv_in, 32)
                for t in range(TILES):
                    m = ROWS[t]
                    pool.wait_ge(ln_norm, TILES * call + t + 1)
                    pool.tensor_tensor(src[0:m, t], src[0:m, t], gb[0:m, 0:D] if call else x[0:m, 0], ALU.mult).then_inc(ln_gain, 1)

            pool.dma_start(rw_raw[:], a["router_w"].rearrange("(k p) e -> p k e", p=P)).then_inc(rw_in, 16)
            pool.dma_start(gb[:], row(a["a_b_in"][0])).then_inc(gb_in, 16)
            pool.dma_start(rbias[:], row(a["router_bias"])).then_inc(rb_in, 16)
            pool.dma_start(x[:, 0], row(a["a_lnv_g"][0])).then_inc(lnv_in, 16)
            pool.dma_start(x[:, 1], row(a["a_lnv_b"][0])).then_inc(lnv_in, 16)
            pool.dma_start(pages[0:1, :], a["page_table"].rearrange("b n -> (b n)").unsqueeze(0)).then_inc(pages_in, 16)
            pool.dma_start(cmix[:], a["cmix"]).then_inc(mixc_in, 16)
            pool.dma_start(bsp[:], a["b_s_T"]).then_inc(mixc_in, 16)
            pool.dma_start(bss[:], a["b_s_rep"]).then_inc(mixc_in, 16)
            pool.wait_ge(wsm_zeroed, 1)
            with nc.allow_non_contiguous_dma("4-row blocks of the spatial weights"):
                for b in range(DEC_B):
                    pool.dma_start(wsm[b * DEC_T:(b + 1) * DEC_T, :, b * DEC_T:(b + 1) * DEC_T],
                                   a["w_s_T"][0:DEC_T, :, 0:DEC_T]).then_inc(wsm_in, 16)

            gain(0, v)
            pool.wait_ge(ln_out, TILES)
            pool.wait_ge(ln_gain, TILES)
            for t in range(TILES):
                src = dram_tile(t, a["x_prompt"][0]) if t < 4 else a["x_sample"].rearrange("b t d -> (b t) d")
                pool.dma_start(x[0:ROWS[t], t], src).then_inc(x_in, 16)
            pool.dma_start(state_v.rearrange("l b t d -> (l b t) d"), v[0:NSAMP, 4]).then_inc(vs_out, 16)

            def moe_pool(l):
                s = moe[l]
                if l == 0:
                    pool.wait_ge(proj_free, M_WIN + 20)
                load_gb(a["ln1_g"][l], a["ln1_b"][l])
                gain(1 + 2 * l, x)
                for t in range(TILES):
                    pool.wait_ge(ln_out, TILES * (1 + 2 * l) + t + 1)
                    pool.dma_start(dram_tile(t, x_rows[l]), x[0:ROWS[t], t]).then_inc(x_out, 16)
                load_gb(a["ln2_g"][l], a["ln2_b"][l])
                pool.wait_ge(plan, l + 1)
                pool.memset(xg[:], 0.0).then_inc(s["xg_zero"], 1)
                pool.wait_ge(s["xg_zero"], 1)
                pool.wait_ge(x_out, 16 * TILES * (l + 1))
                blocks = pool.value_load(table[0:1, LIST_COLS - 1:LIST_COLS], min_val=0, max_val=MAX_BLOCKS - EXPERTS) + EXPERTS

                def wait_apart(n, *sems):
                    if isinstance(n, int):
                        count = n
                    else:
                        count = pool.to_reg(n)
                    pool.wait_ge(plan, l + 1)
                    for sm in sems:
                        pool.wait_ge(sm, count)

                def gather(i):
                    after(pool, s["xg_tr"], i)
                    after(pool, s["gathered"], 16 * i)
                    pool.tensor_copy(gcur[:], gidx[:, bass.ds(i, 1)]).then_inc(s["gcopy"], 1)
                    wait_apart(i + 1, s["gcopy"])
                    pool.indirect_dma_start(xg[:], None, x_rows[l], bass.IndirectOffsetOnAxis(ap=gcur[:, 0:1], axis=0),
                                            bounds_check=NTOK - 1, oob_is_err=False).then_inc(s["gathered"], 16)

                def scatter(i):
                    after(pool, s["scattered"], 16 * i)
                    pool.tensor_copy(scur[:], sidx[:, bass.ds(i, 1)]).then_inc(s["scopy"], 1)
                    wait_apart(i + 1, s["scopy"], s["y_ready"])
                    pool.indirect_dma_start(y_rows[l], bass.IndirectOffsetOnAxis(ap=scur[:, 0:1], axis=0), yb[:], None,
                                            bounds_check=2 * NTOK - 1, oob_is_err=False).then_inc(s["scattered"], 16)
                gather(0)
                gather(1)
                gather(2)
                for t in range(TILES):
                    m = ROWS[t]
                    pool.tensor_scalar(x[0:m, t], x[0:m, t], ALPHA, None, ALU.mult).then_inc(s["scaled"], 1)
                gather(3)
                scatter(0)
                with pool.Fori(3, blocks) as i:
                    gather(i + 1)
                    scatter(i - 2)
                scatter(blocks - 2)
                scatter(blocks - 1)
                wait_apart(16 * blocks, s["scattered"])
                wait_apart(blocks + 1, s["xg_low"])
                pairs = y_rows[l].rearrange("(k n) d -> n k d", k=2)
                for t in range(TILES):
                    pool.dma_start(yl[0:ROWS[t], t], dram_tile(t, pairs)).then_inc(s[f"y_in{t}"], 16)
                gain(2 + 2 * l, x)

            moe_pool(0)
            for t in range(TILES):
                pool.wait_ge(ln_out, 2 * TILES + t + 1)
                pool.dma_start(dram_tile(t, x_parked), x[0:ROWS[t], t]).then_inc(park_out, 16)
            for j, name in enumerate(("b_lam_q1", "b_lam_k1", "b_lam_q2", "b_lam_k2")):
                pool.dma_start(gb[:, j * HEAD_DIM:(j + 1) * HEAD_DIM], row(a[name][0])).then_inc(lam_in, 16)
            pool.dma_start(subg, a["b_subln_g"][0].unsqueeze(1)).then_inc(lam_in, 16)
            k_rows = [k_prompt[0].rearrange("s h d -> s (h d)"), k_sample.rearrange("b t h d -> (b t) (h d)")]
            v_rows = [v_prompt[0].rearrange("s h d -> s (h d)"), v_sample.rearrange("b t h d -> (b t) (h d)")]

            def out_tile(rows, t):
                return dram_tile(t, rows[0]) if t < 4 else rows[1]
            for cb in range(2):
                for t in range(TILES):
                    pool.wait_ge(proj_free, M_QKV + cb * TILES + t + 1)
                    pool.dma_start(out_tile(k_rows, t)[:, cb * HALF:(cb + 1) * HALF], stg[0:ROWS[t], t]
                                   ).then_inc(stg_out[t], 16)
            for t in range(TILES):
                pool.wait_ge(proj_free, M_QKV + 3 * TILES + t + 1)
                pool.dma_start(out_tile(v_rows, t), x[0:ROWS[t], t]).then_inc(kv_out, 16)
            pool.wait_ge(used["b"], B_CACHE)
            for g in range(4):
                after(pool, sm_pv, g)
                pool.memset(ptz[:], 0.0).then_inc(sm_zero, 1)
            pool.wait_ge(kv_out, 16 * TILES)
            pool.wait_ge(park_out, 16 * TILES)
            pool.wait_ge(sm_o, 1)
            pool.wait_ge(at_o, 4 * HEADS)
            for t in range(TILES):
                pool.dma_start(x[0:ROWS[t], t], dram_tile(t, x_parked)).then_inc(park_in, 16)
            pool.wait_ge(lam_sum, 1)
            moe_pool(1)
            y_tiles = [y_prompt[0], y_sample.rearrange("b t d -> (b t) d")]
            for t in range(TILES):
                pool.wait_ge(ln_out, 4 * TILES + t + 1)
                pool.dma_start(out_tile(y_tiles, t), x[0:ROWS[t], t]).then_inc(y_out, 16)
            pool.wait_ge(y_out, 16 * TILES)
            pool.wait_ge(vs_out, 16)
            for t in range(TILES):
                pool.wait_ge(stg_out[t], 32)

        @block.scalar
        def _(act):
            act.dma_start(con[:], a["con"]).then_inc(con_in, 16)
            act.dma_start(con16[:], a["con16"]).then_inc(con_in, 16)

            def split_high(key, n, slot, src, landed, count):
                act.wait_ge(landed, count)
                if not (isinstance(n, int) and n < SPLIT_SLOTS):
                    act.wait_ge(used[key], n - SPLIT_SLOTS + 1)
                act.activation(wh[:, slot], src, ACT.Copy).then_inc(high[key], 1)

            def split_a(s):
                c = s + (s >= A_WS)
                split_high("a", s, s % SPLIT_SLOTS, raw[:, c % RAW_SLOTS], raw_a[c % RAW_SLOTS], landed_a(c))

            def split_b(s):
                c = s if s < B_CACHE else s - B_CACHE + B_WO
                split_high("b", s, s % SPLIT_SLOTS, raw[:, c % RAW_SLOTS], raw_b[c % RAW_SLOTS], landed_b[c])

            def turn_high(n0, gain=1.0):
                for n in (n0, n0 + 1):
                    t, half = n % 10 // 2, n % 2
                    act.wait_ge(tr_done, n + 1)
                    act.activation(xTh[:, 4 * half:4 * half + 4, t * P:t * P + ROWS[t]],
                                   ps[:, 6 + n % 2].rearrange("p (k m) -> p k m", k=4)[:, :, 0:ROWS[t]],
                                   ACT.Copy, scale=gain).then_inc(tr_high, 1)

            def gelu(dst, m0, cols):
                for t in range(TILES):
                    act.wait_ge(proj_free, m0 + t + 1)
                    w = dst[0:ROWS[t], t, cols:cols + HALF]
                    act.activation(w, w, ACT.Gelu_apprx_tanh).then_inc(gelu_done, 1)

            def normalise(call, t, src):
                m, n = ROWS[t], TILES * call + t + 1
                act.wait_ge(ln_var, n)
                act.activation(lns[0:m, 1, t:t + 1], lns[0:m, 0, t:t + 1], ACT.Sqrt).then_inc(ln_std, 1)
                act.wait_ge(ln_rs, n)
                act.activation(src[0:m, t], src[0:m, t], ACT.Identity, bias=lns[0:m, 3, t:t + 1],
                               scale=lns[0:m, 2, t:t + 1]).then_inc(ln_norm, 1)

            def ln_tiles(call, src, t0):
                for i in range(TILES + 3):
                    if i >= 3:
                        turn_high(t0 + 2 * (i - 3))
                    if i < TILES:
                        normalise(call, i, src)

            act.wait_ge(xT0_in, 32)
            for half in range(2):
                act.activation(xTh[:, 4 * half:4 * half + 4], xT0[:, 4 * half:4 * half + 4], ACT.Copy).then_inc(x0_high, 1)
            split_a(0)
            split_a(1)
            act.wait_ge(rw_in, 16)
            act.activation(rwh[:], rw_raw[:], ACT.Copy).then_inc(rw_high, 1)
            for j in range(4):
                split_a(2 * j + 2)
                split_a(2 * j + 3)
                if j == 2:
                    for t in range(TILES):
                        normalise(0, t, v)
                gelu(v if j < 2 else u, M_WIN + 5 * j, j % 2 * HALF)
            for t in range(TILES):
                turn_high(T_US + 2 * t)
            split_a(10)
            split_a(11)

            def moe_act(l, first_used, base_key):
                s, key = moe[l], f"m{l}"

                def split(n, slot, q, i):
                    split_high(key, n, slot, raw[:, q], raw_m[l][q], 16 * (i + 1))

                for n in range(3):
                    act.wait_ge(used[base_key], first_used[n])
                    split(n, n, n, 0)
                act.wait_ge(logit_max, l + 1)
                act.activation(prob[:], lg[:], ACT.Exp).then_inc(exp_r, 1)

                def xg_high(i):
                    act.wait_ge(s["xg_tr"], i + 1)
                    act.activation(xgTh[:], ps[:, 2:4].rearrange("p a (k m) -> p (a k) m", m=P), ACT.Copy
                                   ).then_inc(s["xg_high"], 1)

                def silu(i):
                    act.wait_ge(used[key], 6 * i + 2 if not (isinstance(i, int) and i == 0) else 4)
                    after(act, s["h_ready"], i)
                    act.activation(sg[:], ps[:, 0], ACT.Silu).then_inc(s["silu"], 1)

                def h_high(i):
                    act.wait_ge(s["h_tr"], i + 1)
                    act.activation(hTh[:], ps[:, 6].rearrange("p (k m) -> p k m", k=4), ACT.Copy
                                   ).then_inc(s["h_high"], 1)

                def y_out_(i, n_last):
                    act.wait_ge(used[key], n_last)
                    after(act, s["scattered"], 16 * i)
                    act.activation(yb[:], ps[:, 4:6].rearrange("p a n -> p (a n)"), ACT.Copy).then_inc(s["y_ready"], 1)

                def body(i, first=False):
                    split(6 * i - 2, 1, 0, i)
                    split(6 * i - 1, 2, 1, i)
                    if not first:
                        y_out_(i - 2, 6 * i - 2)
                    h_high(i - 1)
                    for q in range(2, 4):
                        split(6 * i - 2 + q, (q + 1) % 3, q, i)
                    for r in range(2):
                        split(6 * i + 2 + r, (r + 5) % 3, 4 + r, i - 1)
                    silu(i)
                    xg_high(i + 1)

                xg_high(0)
                split(3, 0, 3, 0)
                silu(0)
                xg_high(1)
                body(1, True)
                body(2)
                act.wait_ge(plan, l + 1)
                blocks = act.value_load(table[0:1, LIST_COLS - 1:LIST_COLS], min_val=0, max_val=MAX_BLOCKS - EXPERTS) + EXPERTS
                with act.Fori(3, blocks) as i:
                    body(i)
                for r in range(2):
                    split(6 * blocks - 2 + r, r + 1, 4 + r, blocks - 1)
                y_out_(blocks - 2, 6 * blocks - 2)
                h_high(blocks - 1)
                y_out_(blocks - 1, 6 * blocks)
                return blocks

            ln_tiles(1, x, T_LN1A)
            blocks = moe_act(0, [10, 11, 12], "a")
            act.wait_ge(used["m0"], 6 * blocks)
            split_b(0)
            split_b(1)
            ln_tiles(2, x, T_LN2A)

            def kq_copy(kk):
                dst, cb, t = (KT if kk < 10 else QT), kk % 10 // 5, kk % 5
                act.wait_ge(kq_tr, kk + 1)
                act.activation(dst[:, 4 * cb:4 * cb + 4, t * P:t * P + ROWS[t]],
                               ps[:, 6 + kk % 2].rearrange("p (k m) -> p k m", k=4)[:, :, 0:ROWS[t]],
                               ACT.Copy).then_inc(kq_copied, 1)
            for j in range(6):
                if j < 5:
                    split_b(2 * j + 2)
                if j in (1, 2, 5):
                    for t in range(TILES):
                        kq_copy((0 if j < 5 else 10) + (j - 1) % 4 * 5 + t)
                if j < 5:
                    split_b(2 * j + 3)
            for t in range(TILES):
                kq_copy(15 + t)
            act.wait_ge(lam_sum, 1)
            act.activation(lamc[:, 2:4], lamc[:, 0:2], ACT.Exp).then_inc(lam_exp, 1)

            act.wait_ge(used["b"], B_CACHE)

            def att_exp(n):
                w = (n // HEADS + 1) * P
                act.wait_ge(at_max, n + 1)
                after(act, at_p, n - 1)
                for j in range(2):
                    e = act.activation(E[:, n % 2, j, 0:w], ps[:, j, 0:w], ACT.Exp,
                                       bias=mxs[:, 1, n % 2, j:j + 1], scale=SCALE,
                                       accum_out=mxs[:, 2, n % 2, j:j + 1])
                e.then_inc(at_exp, 1)

            def att_pt(n):
                w = (n // HEADS + 1) * P
                act.wait_ge(at_pt, n + 1)
                after(act, at_pv, n - 1)
                act.activation(PTs[:, n % 2, 0:w], ps[:, 2, 0:w], ACT.Copy).then_inc(at_ptc, 1)

            def att_o(n):
                act.wait_ge(at_pv, n + 1)
                act.activation(o[:, n // HEADS, n % HEADS * P:(n % HEADS + 1) * P], ps[:, 3, 0:P],
                               ACT.Copy).then_inc(at_o, 1)

            def keys_copy(g, hk):
                b2, page, half = hk // 4, hk // 2 % 2, hk % 2
                act.wait_ge(sm_kt, 8 * g + hk + 1)
                after(act, sm_s, 2 * (g - 1) + b2 + 1)
                act.activation(kts[:, b2, 4 * half:4 * half + 4, page * P:(page + 1) * P],
                               ps[:, 4].rearrange("p (h m) -> p h m", m=P), ACT.Copy).then_inc(sm_ktc, 1)

            steps = 4 * HEADS
            att_exp(0)
            for n in range(steps):
                g, j = n // 8, n % 8
                if n + 1 < steps:
                    att_exp(n + 1)
                if j < 4:
                    keys_copy(g, 2 * j)
                att_pt(n)
                if n >= 1:
                    att_o(n - 1)
                if j < 4:
                    keys_copy(g, 2 * j + 1)
                if j == 7:
                    act.wait_ge(sm_max, g + 1)
                    act.activation(Es[:], ps[:, 5, 0:288], ACT.Exp, bias=smx[:, 1:2], scale=SCALE,
                                   accum_out=smx[:, 2:3]).then_inc(sm_exp, 1)
            att_o(steps - 1)
            act.wait_ge(sm_pv, 5)
            act.activation(o[0:NSAMP, 4], ps[0:NSAMP, 6:8].rearrange("p a n -> p (a n)"), ACT.Copy).then_inc(sm_o, 1)
            act.wait_ge(om_var, 1)
            act.activation(oss[:, 1], oss[:, 0], ACT.Sqrt).then_inc(om_std, 1)
            for t in range(TILES):
                turn_high(T_O + 2 * t, subg)
            act.wait_ge(tr_low, T_O + 10)
            for s in range(12, 16):
                split_b(s)
            ln_tiles(3, x, T_LN1B)
            moe_act(1, [16, 14, 15], "b")
            for t in range(TILES):
                normalise(4, t, x)

        @block.vector
        def _(dve):
            chain = [0]

            def link(ins):
                chain[0] += 1
                ins.then_inc(dve_step, 1)
                dve.wait_ge(dve_step, chain[0])

            def split_low(key, n, slot, src):
                dve.wait_ge(high[key], n + 1)
                dve.tensor_tensor(wl[:, slot], src, wh[:, slot].bitcast(F32), ALU.subtract).then_inc(low[key], 1)

            def split_a(s):
                split_low("a", s, s % SPLIT_SLOTS, raw[:, (s + (s >= A_WS)) % RAW_SLOTS])

            def split_b(s):
                c = s if s < B_CACHE else s - B_CACHE + B_WO
                split_low("b", s, s % SPLIT_SLOTS, raw[:, c % RAW_SLOTS])

            def turn_low(n0, gain=1.0):
                for n in (n0, n0 + 1):
                    t, half = n % 10 // 2, n % 2
                    dve.wait_ge(tr_high, n + 1)
                    w = (slice(None), slice(4 * half, 4 * half + 4), slice(t * P, t * P + ROWS[t]))
                    dve.scalar_tensor_tensor(
                        out=xTl[w], in0=ps[:, 6 + n % 2].rearrange("p (k m) -> p k m", k=4)[:, :, 0:ROWS[t]],
                        scalar=gain, in1=xTh[w].bitcast(F32), op0=ALU.mult, op1=ALU.subtract).then_inc(tr_low, 1)

            def ln_stats(call, t, src):
                m = ROWS[t]
                dve.bn_stats(stats[0:m, t, 0], src[0:m, t, 0:HALF])
                link(dve.bn_stats(stats[0:m, t, 1], src[0:m, t, HALF:D]))
                link(dve.bn_aggr(mv[0:m, t], stats[0:m, t].rearrange("p a b -> p (a b)")))
                dve.tensor_scalar(lns[0:m, 0, t:t + 1], mv[0:m, t, 1:2], EPS, None, ALU.add).then_inc(ln_var, 1)

            def ln_scale(call, t):
                m = ROWS[t]
                dve.wait_ge(ln_std, TILES * call + t + 1)
                link(dve.reciprocal(lns[0:m, 2, t:t + 1], lns[0:m, 1, t:t + 1]))
                dve.scalar_tensor_tensor(out=lns[0:m, 3, t:t + 1], in0=mv[0:m, t, 0:1], scalar=-1.0,
                                         in1=lns[0:m, 2, t:t + 1], op0=ALU.mult, op1=ALU.mult).then_inc(ln_rs, 1)

            def ln_shift(call, t, src):
                m = ROWS[t]
                dve.wait_ge(ln_gain, TILES * call + t + 1)
                shift = gb[0:m, D:2 * D] if call else x[0:m, 1]
                dve.tensor_tensor(src[0:m, t], src[0:m, t], shift, ALU.add).then_inc(ln_out, 1)

            def ln_tiles(call, produce, t0):
                for i in range(TILES + 3):
                    if i < TILES:
                        produce(i)
                        ln_stats(call, i, x)
                    if 0 <= i - 2 < TILES:
                        ln_shift(call, i - 2, x)
                    if i < TILES:
                        ln_scale(call, i)
                    if i >= 3 and t0 is not None:
                        turn_low(t0 + 2 * (i - 3))

            def residual(m_step, t, cb):
                m = ROWS[t]
                dve.wait_ge(proj_done, m_step + 1)
                w = x[0:m, t, cb * HALF:(cb + 1) * HALF]
                dve.scalar_tensor_tensor(out=w, in0=w, scalar=ALPHA, in1=ps[0:m, m_step % PROJ_BANKS],
                                         op0=ALU.mult, op1=ALU.add).then_inc(proj_free, 1)

            dve.memset(wsm[:], 0.0).then_inc(wsm_zeroed, 1)
            for half in range(2):
                dve.wait_ge(x0_high, half + 1)
                w = (slice(None), slice(4 * half, 4 * half + 4))
                dve.tensor_tensor(xTl[w], xT0[w], xTh[w].bitcast(F32), ALU.subtract).then_inc(x0_low, 1)
            split_a(0)
            split_a(1)
            dve.wait_ge(rw_high, 1)
            dve.tensor_tensor(rwl[:], rw_raw[:], rwh[:].bitcast(F32), ALU.subtract).then_inc(rw_low, 1)
            dve.wait_ge(rw_low, 1)
            dve.wait_ge(gb_in, 16)
            for j in range(4):
                split_a(2 * j + 2)
                split_a(2 * j + 3)
                if j == 2:
                    for t in range(TILES):
                        dve.wait_ge(gelu_done, TILES + t + 1)
                        ln_stats(0, t, v)
                        ln_scale(0, t)
                if j == 3:
                    for t in range(TILES):
                        ln_shift(0, t, v)
                    dve.wait_ge(mixc_in, 48)
                    dve.wait_ge(raw_a[A_WS % RAW_SLOTS], landed_a(A_WS))
                    w = raw[:, A_WS % RAW_SLOTS, 0:2].rearrange("p a (g t) -> p (a g) t", t=P)
                    dve.tensor_tensor(w, w, cmix[:, 0:P].unsqueeze(1).broadcast_to([P, HEADS, P]), ALU.mult
                                      ).then_inc(ws_masked, 1)
                    dve.wait_ge(wsm_in, 16 * DEC_B)
                    dve.tensor_tensor(wsm[:], wsm[:],
                                      cmix[0:NSAMP, P:P + NSAMP].unsqueeze(1).broadcast_to([NSAMP, HEADS, NSAMP]),
                                      ALU.mult).then_inc(ws_masked, 1)
                dst, cols = (v if j < 2 else u), j % 2 * HALF
                for t in range(TILES):
                    m, step = ROWS[t], M_WIN + 5 * j + t
                    dve.wait_ge(proj_done, step + 1)
                    bias = gb[0:m, WIN_COLS[j] * HALF:(WIN_COLS[j] + 1) * HALF]
                    dve.tensor_tensor(dst[0:m, t, cols:cols + HALF], ps[0:m, step % PROJ_BANKS], bias, ALU.add
                                      ).then_inc(proj_free, 1)
            dve.wait_ge(gelu_done, 4 * TILES)
            for g in range(HEADS):
                step = M_MIX + g
                w = u[:, 0:4, g * P:(g + 1) * P]
                dve.wait_ge(proj_done, step + 1)
                dve.scalar_tensor_tensor(out=w, in0=ps[:, step % PROJ_BANKS].rearrange("p (c n) -> p c n", c=4),
                                         scalar=bsp[:, g:g + 1], in1=w, op0=ALU.add, op1=ALU.mult
                                         ).then_inc(proj_free, 1)
            for half in range(2):
                step = M_MIX + 8 + half
                dve.wait_ge(proj_done, step + 1)
                for j in range(4):
                    g = 4 * half + j
                    w = u[0:NSAMP, 4, g * P:(g + 1) * P]
                    ins = dve.scalar_tensor_tensor(out=w, in0=ps[0:NSAMP, step % PROJ_BANKS, j * P:(j + 1) * P],
                                                   scalar=bss[:, g:g + 1], in1=w, op0=ALU.add, op1=ALU.mult)
                ins.then_inc(proj_free, 1)
            for t in range(TILES):
                turn_low(T_US + 2 * t)
            split_a(10)
            split_a(11)
            dve.wait_ge(x_in, 16 * TILES)
            for t in range(TILES):
                residual(M_WOUT + t, t, 0)

            def second_half(m0):
                def produce(t):
                    residual(m0 + t, t, 1)
                    dve.wait_ge(proj_free, m0 + t + 1)
                return produce
            ln_tiles(1, second_half(M_WOUT + 5), T_LN1A)

            def route(l, m0):
                def first_max(out, val, mx, rank, n, work):
                    shape = [P, TILES, n]
                    link(dve.tensor_tensor(work, val, mx.unsqueeze(2).broadcast_to(shape), ALU.is_equal))
                    link(dve.tensor_tensor(work, work, rank.unsqueeze(1).broadcast_to(shape), ALU.mult))
                    link(dve.tensor_reduce(col[:, 11, 0], work, AX, ALU.max))
                    link(dve.tensor_tensor(out, work, col[:, 11, 0].unsqueeze(2).broadcast_to(shape), ALU.is_equal))

                full = [P, TILES, EXPERTS]
                bank = m0 % PROJ_BANKS
                link(dve.memset(lg[:], 0.0))
                dve.wait_ge(proj_done, m0 + 1)
                dve.wait_ge(rb_in, 16)
                dve.tensor_copy(lg[:, 0:4], ps[:, bank, 0:4 * EXPERTS].rearrange("p (t e) -> p t e", e=EXPERTS))
                link(dve.tensor_copy(lg[0:NSAMP, 4], ps[0:NSAMP, bank, 4 * EXPERTS:5 * EXPERTS]))
                dve.sem_inc(proj_free, 1)
                link(dve.tensor_reduce(col[:, 0, 0], lg[:], AX, ALU.max))
                dve.tensor_tensor(lg[:], lg[:], col[:, 0, 0].unsqueeze(2).broadcast_to(full), ALU.subtract
                                  ).then_inc(logit_max, 1)
                dve.wait_ge(exp_r, l + 1)
                link(dve.tensor_reduce(col[:, 1, 0], prob[:], AX, ALU.add))
                link(dve.reciprocal(col[:, 2, 0], col[:, 1, 0]))
                link(dve.tensor_tensor(prob[:], prob[:], col[:, 2, 0].unsqueeze(2).broadcast_to(full), ALU.mult))
                link(dve.tensor_tensor(sel[:], prob[:], rbias[:].unsqueeze(1).broadcast_to(full), ALU.add))
                s4 = sel[:].rearrange("p t (g e) -> p (t g) e", e=PER_GROUP)
                dve.tensor_tensor(hilo[:, 0], s4[:, :, 0::2], s4[:, :, 1::2], ALU.max)
                link(dve.tensor_tensor(hilo[:, 1], s4[:, :, 0::2], s4[:, :, 1::2], ALU.min))
                gv = [gsc[:, j].rearrange("p t g -> p (t g)") for j in range(4)]
                dve.tensor_tensor(gv[0], hilo[:, 0, :, 0], hilo[:, 0, :, 1], ALU.max)
                dve.tensor_tensor(gv[1], hilo[:, 0, :, 0], hilo[:, 0, :, 1], ALU.min)
                link(dve.tensor_tensor(gv[2], hilo[:, 1, :, 0], hilo[:, 1, :, 1], ALU.max))
                link(dve.tensor_tensor(gv[1], gv[1], gv[2], ALU.max))
                link(dve.tensor_tensor(gv[0], gv[0], gv[1], ALU.add))
                link(dve.tensor_reduce(col[:, 3, 0], gsc[:, 0], AX, ALU.max))
                first_max(gsc[:, 3], gsc[:, 0], col[:, 3, 0], con[:, C_RK4:C_RK4 + 4], GROUPS, gsc[:, 2])
                link(dve.tensor_scalar(gsc[:, 1], gsc[:, 3], 1.0, -NEG, ALU.subtract, ALU.mult))
                four = [P, TILES * GROUPS, PER_GROUP]
                g3 = gsc[:, 3].rearrange("p t g -> p (t g)").unsqueeze(2).broadcast_to(four)
                g1 = gsc[:, 1].rearrange("p t g -> p (t g)").unsqueeze(2).broadcast_to(four)
                link(dve.tensor_tensor(s4, s4, g3, ALU.mult))
                link(dve.tensor_tensor(s4, s4, g1, ALU.add))
                link(dve.tensor_reduce(col[:, 4, 0], sel[:], AX, ALU.max))
                rk16 = con[:, C_RK16:C_RK16 + 16]
                first_max(oh[:, 0], sel[:], col[:, 4, 0], rk16, EXPERTS, tmp[:, 0])
                link(dve.scalar_tensor_tensor(out=sel[:], in0=oh[:, 0], scalar=3 * NEG, in1=sel[:],
                                              op0=ALU.mult, op1=ALU.add))
                link(dve.tensor_reduce(col[:, 5, 0], sel[:], AX, ALU.max))
                first_max(oh[:, 1], sel[:], col[:, 5, 0], rk16, EXPERTS, tmp[:, 0])
                both = [P, 2, TILES, EXPERTS]
                link(dve.tensor_tensor(tmp[:], oh[:], prob[:].unsqueeze(1).broadcast_to(both), ALU.mult))
                link(dve.tensor_reduce(gates[:], tmp[:], AX, ALU.add))
                link(dve.tensor_tensor(col[:, 6, 0], gates[:, 0], gates[:, 1], ALU.add))
                link(dve.reciprocal(col[:, 6, 1], col[:, 6, 0]))
                link(dve.tensor_tensor(gates[:], gates[:], col[:, 6, 1].unsqueeze(1).broadcast_to([P, 2, TILES]),
                                       ALU.mult))
                link(dve.tensor_tensor(oh[:], oh[:], con[:, C_VALID:C_VALID + TILES].unsqueeze(1).unsqueeze(3)
                                       .broadcast_to(both), ALU.mult))
                dve.tensor_tensor(m16[:], oh[:, 0], oh[:, 1], ALU.add).then_inc(masks, 1)
                dve.wait_ge(proj_done, m0 + 2)
                bank = (m0 + 1) % PROJ_BANKS
                rank = ps[:, bank, 0:TILES * EXPERTS].rearrange("p (t e) -> p t e", e=EXPERTS)
                link(dve.tensor_copy(cnt[:, 0], ps[:, bank, TILES * EXPERTS:(TILES + 1) * EXPERTS]))
                link(dve.tensor_tensor(tmp[:], oh[:], rank.unsqueeze(1).broadcast_to(both), ALU.mult))
                dve.sem_inc(proj_free, 1)
                link(dve.tensor_reduce(col[:, 0], tmp[:], AX, ALU.add))
                c_thr = con[:, C_THR:C_THR + 4]
                link(dve.tensor_tensor(thr[:, :, 0:4], cnt[:, 0].unsqueeze(2).broadcast_to([P, EXPERTS, 4]),
                                       c_thr.unsqueeze(1).broadcast_to([P, EXPERTS, 4]), ALU.is_gt))
                link(dve.tensor_reduce(cnt[:, 1], thr[:, :, 0:4], AX, ALU.add))
                link(dve.tensor_copy(cnt[:, 2], cnt[:, 1]))
                a_, b_ = 2, 3
                for sh in (1, 2, 4, 8):
                    dve.tensor_copy(cnt[:, b_, 0:sh], cnt[:, a_, 0:sh])
                    link(dve.tensor_tensor(cnt[:, b_, sh:16], cnt[:, a_, sh:16], cnt[:, a_, 0:16 - sh], ALU.add))
                    a_, b_ = b_, a_
                incl = cnt[:, a_]
                link(dve.tensor_tensor(cnt[:, 4], incl, cnt[:, 1], ALU.subtract))
                link(dve.tensor_tensor(tmp[:], oh[:], cnt[:, 4].unsqueeze(1).unsqueeze(1).broadcast_to(both), ALU.mult))
                link(dve.tensor_reduce(col[:, 1], tmp[:], AX, ALU.add))
                link(dve.tensor_tensor(tmp[:], oh[:], con[:, C_IOTA16:C_IOTA16 + 16].unsqueeze(1).unsqueeze(1)
                                       .broadcast_to(both), ALU.mult))
                link(dve.tensor_reduce(col[:, 2], tmp[:], AX, ALU.add))
                link(dve.tensor_scalar(col[:, 3], col[:, 0], 1.0 * P, None, ALU.is_ge))
                for j in range(2, 5):
                    link(dve.scalar_tensor_tensor(out=col[:, 3], in0=col[:, 0], scalar=1.0 * P * j, in1=col[:, 3],
                                                  op0=ALU.is_ge, op1=ALU.add))
                link(dve.scalar_tensor_tensor(out=col[:, 4], in0=col[:, 3], scalar=-1.0 * P, in1=col[:, 0],
                                              op0=ALU.mult, op1=ALU.add))
                link(dve.tensor_tensor(col[:, 5], col[:, 1], col[:, 3], ALU.add))
                link(dve.scalar_tensor_tensor(out=col[:, 5], in0=col[:, 5], scalar=EXPERTS - 1.0, in1=col[:, 2],
                                              op0=ALU.add, op1=ALU.subtract))
                link(dve.scalar_tensor_tensor(out=col[:, 5], in0=col[:, 3], scalar=0.0, in1=col[:, 5],
                                              op0=ALU.is_gt, op1=ALU.mult))
                link(dve.tensor_tensor(col[:, 5], col[:, 5], col[:, 2], ALU.add))
                iota = con[:, C_IOTA:C_IOTA + P]
                for k in range(2):
                    for t in range(TILES):
                        n = k * TILES + t
                        dve.tensor_scalar(lo16[:, n], iota, col[:, 4, k, t:t + 1], None, ALU.is_equal)
                        ins = dve.tensor_scalar(hi16[:, n, 0:LIST_COLS], iota[:, 0:LIST_COLS], col[:, 5, k, t:t + 1],
                                                con[:, C_ID1 + n:C_ID1 + n + 1], ALU.is_equal, ALU.mult)
                ins.then_inc(onehots, 1)
                link(dve.tensor_tensor(thr[:, 0:8], incl.unsqueeze(1).broadcast_to([P, 8, EXPERTS]),
                                       con[:, C_IOTA8:C_IOTA8 + 8].unsqueeze(2).broadcast_to([P, 8, EXPERTS]),
                                       ALU.is_le))
                link(dve.tensor_copy(tblf[:, 0:EXPERTS], con[:, C_IOTA16:C_IOTA16 + 16]))
                link(dve.tensor_reduce(tblf[:, EXPERTS:MAX_BLOCKS], thr[:, 0:8], AX, ALU.add))
                link(dve.tensor_scalar(tblf[:, 0:MAX_BLOCKS], tblf[:, 0:MAX_BLOCKS], EXPERTS - 1.0, None, ALU.min))
                link(dve.tensor_copy(tblf[:, MAX_BLOCKS:LIST_COLS], incl[:, 15:16]))
                dve.tensor_copy(table[:], tblf[:])
                dve.wait_ge(proj_done, m0 + 3)
                val = ps[:, (m0 + 2) % PROJ_BANKS, 0:LIST_COLS]
                link(dve.tensor_scalar(lst[:, 0], val, 0.0, NO_ROW, ALU.is_equal, ALU.mult))
                link(dve.tensor_scalar(lst[:, 1], val, 1.0, None, ALU.subtract))
                dve.sem_inc(proj_free, 1)
                link(dve.tensor_tensor(lst[:, 0], lst[:, 0], lst[:, 1], ALU.add))
                dve.tensor_copy(sidx[:], lst[:, 0])
                link(dve.tensor_scalar(lst[:, 2], lst[:, 0], 1.0 * NTOK, -1.0 * NTOK, ALU.is_ge, ALU.mult))
                link(dve.tensor_tensor(lst[:, 1], lst[:, 0], lst[:, 2], ALU.add))
                link(dve.tensor_copy(gidx[:], lst[:, 1]))
                dve.sem_inc(plan, 1)

            def moe_dve(l, m0):
                s, key = moe[l], f"m{l}"

                def split(n, slot, q):
                    split_low(key, n, slot, raw[:, q])

                for n in range(3):
                    split(n, n, n)
                route(l, m0)

                def xg_low(i):
                    dve.wait_ge(s["xg_high"], i + 1)
                    dve.tensor_tensor(xgTl[:], ps[:, 2:4].rearrange("p a (k m) -> p (a k) m", m=P),
                                      xgTh[:].bitcast(F32), ALU.subtract).then_inc(s["xg_low"], 1)

                def gate_up(i):
                    dve.wait_ge(s["silu"], i + 1)
                    after(dve, s["h_tr"], i)
                    dve.tensor_tensor(hb[:], sg[:], ps[:, 1], ALU.mult).then_inc(s["h_ready"], 1)

                def h_low(i):
                    dve.wait_ge(s["h_high"], i + 1)
                    dve.tensor_tensor(hTl[:], ps[:, 6].rearrange("p (k m) -> p k m", k=4), hTh[:].bitcast(F32),
                                      ALU.subtract).then_inc(s["h_low"], 1)

                def body(i):
                    split(6 * i - 2, 1, 0)
                    split(6 * i - 1, 2, 1)
                    h_low(i - 1)
                    for q in range(2, 4):
                        split(6 * i - 2 + q, (q + 1) % 3, q)
                    for r in range(2):
                        split(6 * i + 2 + r, (r + 5) % 3, 4 + r)
                    gate_up(i)
                    xg_low(i + 1)

                xg_low(0)
                split(3, 0, 3)
                gate_up(0)
                xg_low(1)
                blocks = dve.value_load(table[0:1, LIST_COLS - 1:LIST_COLS], min_val=0, max_val=MAX_BLOCKS - EXPERTS) + EXPERTS
                with dve.Fori(1, blocks) as i:
                    body(i)
                for r in range(2):
                    split(6 * blocks - 2 + r, r + 1, 4 + r)
                h_low(blocks - 1)

            def add_experts(l):
                s = moe[l]

                def produce(t):
                    m = ROWS[t]
                    dve.wait_ge(s["scaled"], t + 1)
                    dve.wait_ge(s[f"y_in{t}"], 16)
                    for k in range(2):
                        link(dve.scalar_tensor_tensor(out=x[0:m, t], in0=yl[0:m, t, k], scalar=gates[0:m, k, t:t + 1],
                                                      in1=x[0:m, t], op0=ALU.mult, op1=ALU.add))
                return produce

            moe_dve(0, M_ROUTE_A)
            split_b(0)
            split_b(1)
            ln_tiles(2, add_experts(0), T_LN2A)

            for j in range(6):
                if j < 5:
                    split_b(2 * j + 2)
                    split_b(2 * j + 3)
                for t in range(TILES):
                    m, step = ROWS[t], M_QKV + 5 * j + t
                    if j in (2, 3):
                        dve.wait_ge(park_out, 16 * TILES)
                        dst = x[0:m, t, (j - 2) * HALF:(j - 1) * HALF]
                    else:
                        kk = (5 * j if j < 2 else 10 + 5 * (j - 4)) + t
                        after(dve, kq_tr, kk - 4)
                        if 5 <= kk < 15:
                            dve.wait_ge(stg_out[t], 16 * (kk // 5))
                        dst = stg[0:m, t]
                    dve.wait_ge(proj_done, step + 1)
                    dve.tensor_copy(dst, ps[0:m, step % PROJ_BANKS]).then_inc(proj_free, 1)

            dve.wait_ge(lam_in, 16 * 5)
            dve.wait_ge(used["b"], B_CACHE)
            lq = gb[:, 0:4 * HEAD_DIM].rearrange("p (a b d) -> p a b d", a=2, b=2)
            link(dve.tensor_tensor(lamp[:], lq[:, :, 0], lq[:, :, 1], ALU.mult))
            dve.tensor_reduce(lamc[:, 0:2], lamp[:], AX, ALU.add).then_inc(lam_sum, 1)
            dve.wait_ge(lam_exp, 1)
            link(dve.tensor_tensor(lamc[:, 4:5], lamc[:, 3:4], lamc[:, 2:3], ALU.subtract))
            link(dve.tensor_scalar(lamc[:, 5:6], lamc[:, 4:5], LAM_INIT, None, ALU.subtract))
            link(dve.tensor_tensor(lamc[:, 6:7], con[:, C_COEF + 1:C_COEF + 2], lamc[:, 5:6], ALU.mult))
            link(dve.tensor_tensor(lamc[:, 7:8], lamc[:, 6:7], con[:, C_COEF:C_COEF + 1], ALU.add))
            link(dve.memset(oss[:], 1.0))
            neg_lam, coef = lamc[:, 5:6], lamc[:, 7:8]

            def att_max(n):
                w = (n // HEADS + 1) * P
                pair = ps[:, 0:2]
                dve.wait_ge(at_s, n + 1)
                diag = pair[:, :, w - P:w]
                link(dve.tensor_tensor(diag, diag, con[:, C_CAUSAL:C_CAUSAL + P].unsqueeze(1)
                                       .broadcast_to([P, 2, P]), ALU.add))
                link(dve.tensor_reduce(mxs[:, 0, n % 2], pair[:, :, 0:w], AX, ALU.max))
                dve.tensor_scalar(mxs[:, 1, n % 2], mxs[:, 0, n % 2], -SCALE, None, ALU.mult).then_inc(at_max, 1)

            def att_p(n):
                w = (n // HEADS + 1) * P
                dve.wait_ge(at_exp, n + 1)
                link(dve.reciprocal(mxs[:, 3, n % 2], mxs[:, 2, n % 2]))
                e1, e2 = E[:, n % 2, 0, 0:w], E[:, n % 2, 1, 0:w]
                link(dve.tensor_scalar(e2, e2, mxs[:, 3, n % 2, 1:2], neg_lam, ALU.mult, ALU.mult))
                after(dve, at_pt, n - 1)
                dve.scalar_tensor_tensor(out=Pm[:, n % 2, 0:w], in0=e1, scalar=mxs[:, 3, n % 2, 0:1], in1=e2,
                                         op0=ALU.mult, op1=ALU.add).then_inc(at_p, 1)
            def queries(g):
                after(dve, sm_s, 2 * g)
                for b2 in range(2):
                    b = 2 * g + b2
                    for part in range(2):
                        r = slice(64 * part, 64 * part + 64)
                        wide = qpad[r, b2 * 1088:(b2 + 1) * 1088].rearrange("p (h c) -> p h c", c=136)
                        ins = dve.tensor_copy(wide[:, :, 4 * part:4 * part + 4],
                                              QT[r, :, SEQ + b * DEC_T:SEQ + (b + 1) * DEC_T])
                ins.then_inc(sm_q, 1)

            def sample_max(g):
                dve.wait_ge(sm_s, 2 * g + 2)
                new = ps[:, 5, 256:288]
                link(dve.tensor_tensor(new, new, con[:, C_SMASK + 32 * g:C_SMASK + 32 * g + 32], ALU.add))
                link(dve.tensor_reduce(smx[:, 0:1], ps[:, 5, 0:288], AX, ALU.max))
                dve.tensor_scalar(smx[:, 1:2], smx[:, 0:1], -SCALE, None, ALU.mult).then_inc(sm_max, 1)

            def sample_p(g):
                dve.wait_ge(sm_exp, g + 1)
                link(dve.reciprocal(smx[:, 3:4], smx[:, 2:3]))
                dve.tensor_scalar(Ps[:], Es[:], smx[:, 3:4], coef, ALU.mult, ALU.mult).then_inc(sm_p, 1)

            def sample_columns(g):
                dve.wait_ge(sm_zero, g + 1)
                dve.wait_ge(sm_pt, g + 1)
                for half in range(2):
                    for b2 in range(2):
                        c0 = (2 * g + b2) * DEC_T
                        for page in range(3):
                            m, dst = (P, ptz[:, page, b2]) if page < 2 else (NSAMP, ptn[:])
                            rows = ps[0:m, 5, page * P + b2 * 64:page * P + b2 * 64 + 64].rearrange(
                                "p (h a q) -> p h a q", a=2, q=DEC_T)
                            mine = dst[:, :, c0:c0 + DEC_T]
                            if half == 0:
                                ins = dve.tensor_copy(mine, rows[:, :, 0])
                            else:
                                ins = dve.tensor_tensor(mine, mine, rows[:, :, 1], ALU.add)
                    if half == 0:
                        link(ins)
                ins.then_inc(sm_ptz, 1)

            def squares(t):
                m = ROWS[t]
                link(dve.tensor_tensor(osq[0:m], o[0:m, t], o[0:m, t], ALU.mult))
                link(dve.tensor_reduce(oss[0:m, 2, t], osq[0:m].rearrange("p (h e) -> p h e", e=P), AX, ALU.add))

            link(dve.memset(qpad[:], 0.0))
            steps = 4 * HEADS
            att_max(0)
            for n in range(steps):
                g, j = n // 8, n % 8
                if n + 1 < steps:
                    att_max(n + 1)
                att_p(n)
                if j == 0:
                    queries(g)
                    if g:
                        sample_p(g - 1)
                if j == 1 and g:
                    sample_columns(g - 1)
                if j == 3 and g:
                    dve.wait_ge(at_o, 8 * g)
                    squares(g - 1)
                if j == 7:
                    sample_max(g)
            sample_p(3)
            sample_columns(3)

            dve.wait_ge(at_o, steps)
            dve.wait_ge(sm_o, 1)
            squares(3)
            squares(4)
            dve.tensor_scalar(oss[:, 0], oss[:, 2], 1.0 / P, EPS, ALU.mult, ALU.add).then_inc(om_var, 1)
            dve.wait_ge(om_std, 1)
            link(dve.reciprocal(oss[:, 2], oss[:, 1]))
            link(dve.tensor_scalar(oss[:, 2], oss[:, 2], 1.0 - LAM_INIT, None, ALU.mult))
            for t in range(TILES):
                m = ROWS[t]
                ot = o[0:m, t].rearrange("p (h e) -> p h e", e=P)
                dve.tensor_tensor(ot, ot, oss[0:m, 2, t].unsqueeze(2).broadcast_to([m, HEADS, P]), ALU.mult
                                  ).then_inc(om_r, 1)
            for t in range(TILES):
                turn_low(T_O + 2 * t, subg)
            split_b(12)
            split_b(13)
            dve.wait_ge(park_in, 16 * TILES)
            for t in range(TILES):
                residual(M_WO + t, t, 0)
            split_b(14)
            split_b(15)
            ln_tiles(3, second_half(M_WO + 5), T_LN1B)
            moe_dve(1, M_ROUTE_B)
            ln_tiles(4, add_experts(1), None)

        @block.tensor
        def _(pe):
            def three(out, high_, low_, w_high, w_low, start, stop):
                pe.matmul(out, high_, w_high, start=start, stop=False)
                pe.matmul(out, high_, w_low, start=False, stop=False)
                return pe.matmul(out, low_, w_high, start=False, stop=stop)

            def bank_for(step):
                after(pe, proj_free, step - PROJ_BANKS + 1)
                return step % PROJ_BANKS

            def project(key, s0, m0, between=None):
                for kh in range(2):
                    s = s0 + kh
                    pe.wait_ge(low[key], s + 1)
                    for t in range(TILES):
                        bank = (m0 + t) % PROJ_BANKS
                        if kh == 0:
                            bank_for(m0 + t)
                        tok = slice(t * P, t * P + ROWS[t])
                        for j in range(4):
                            k = 4 * kh + j
                            mm = three(ps[0:ROWS[t], bank], xTh[:, k, tok], xTl[:, k, tok],
                                       wh[:, s % SPLIT_SLOTS, j], wl[:, s % SPLIT_SLOTS, j],
                                       start=(k == 0), stop=(k == KT_D - 1))
                            if k == KT_D - 1 and t < TILES - 1:
                                mm.then_inc(proj_done, 1)
                        if kh == 0 and between:
                            between(t)
                    if kh == 0:
                        mm.then_inc(used[key], 1)
                    else:
                        mm.then_inc(proj_done, 1)
                        pe.wait_ge(proj_done, m0 + TILES)
                        pe.sem_inc(used[key], 1)

            def turn(t, n0, src):
                m = ROWS[t]
                for half in range(2):
                    n = n0 + 2 * t + half
                    after(pe, tr_low, n - 1)
                    for j in range(4):
                        k = 4 * half + j
                        mm = pe.transpose(ps[:, 6 + n % 2, j * P:j * P + m], src[0:m, t, k * P:(k + 1) * P],
                                          ident[0:m, 0:m])
                    mm.then_inc(tr_done, 1)

            pe.wait_ge(con_in, 32)
            pe.wait_ge(x0_low, 2)
            for j in range(4):
                project("a", 2 * j, M_WIN + 5 * j)
            pe.wait_ge(ln_out, TILES)
            pe.wait_ge(ws_masked, 2)
            ws = raw[:, A_WS % RAW_SLOTS, 0:2].rearrange("p a (g t) -> p (a g) t", t=P)
            for g in range(HEADS):
                bank = bank_for(M_MIX + g)
                mm = pe.matmul(ps[:, bank].rearrange("p (c n) -> p c n", c=4), ws[:, g], v[:, 0:4, g * P:(g + 1) * P],
                               start=True, stop=True)
                mm.then_inc(proj_done, 1)
            for half in range(2):
                bank = bank_for(M_MIX + 8 + half)
                for j in range(4):
                    g = 4 * half + j
                    mm = pe.matmul(ps[0:NSAMP, bank, j * P:(j + 1) * P], wsm[:, g], v[0:NSAMP, 4, g * P:(g + 1) * P],
                                   start=True, stop=True)
                mm.then_inc(proj_done, 1)
            pe.wait_ge(proj_done, M_MIX + 8)
            pe.sem_inc(mix_done, 1)
            pe.wait_ge(proj_free, M_MIX + 10)
            for t in range(TILES):
                turn(t, T_US, u)
            pe.wait_ge(tr_low, T_US + 10)
            for cb in range(2):
                project("a", 8 + 2 * cb, M_WOUT + 5 * cb)

            def route(l, m0, t0, call):
                pe.wait_ge(rw_low, 1)
                bank = bank_for(m0)
                for t in range(TILES + 1):
                    if t < TILES:
                        pe.wait_ge(ln_out, TILES * call + t + 1)
                        turn(t, t0, x)
                    if t:
                        b = t - 1
                        tok = slice(b * P, b * P + ROWS[b])
                        pe.wait_ge(tr_low, t0 + 2 * t)
                        for k in range(KT_D):
                            mm = three(ps[0:ROWS[b], bank, b * EXPERTS:(b + 1) * EXPERTS], xTh[:, k, tok],
                                       xTl[:, k, tok], rwh[:, k], rwl[:, k], start=(k == 0), stop=(k == KT_D - 1))
                mm.then_inc(proj_done, 1)
                before, ones = con16[:, 0:P], con16[:, P:2 * P]
                bank = bank_for(m0 + 1)
                pe.wait_ge(masks, l + 1)
                for t in range(TILES + 1):
                    for b in range(min(t + 1, TILES)):
                        mm = pe.matmul(ps[:, bank, t * EXPERTS:(t + 1) * EXPERTS], before if b == t else ones, m16[:, b],
                                       start=(b == 0), stop=(b == min(t, TILES - 1)))
                mm.then_inc(proj_done, 1)
                bank = bank_for(m0 + 2)
                pe.wait_ge(onehots, l + 1)
                for n in range(2 * TILES):
                    mm = pe.matmul(ps[:, bank, 0:LIST_COLS], lo16[:, n], hi16[:, n, 0:LIST_COLS],
                                   start=(n == 0), stop=(n == 2 * TILES - 1))
                mm.then_inc(proj_done, 1)

            def moe_pe(l, m_end):
                s, key = moe[l], f"m{l}"
                pe.wait_ge(proj_free, m_end)

                def up(i, n0):
                    pe.wait_ge(s["xg_low"], i + 1)
                    after(pe, s["h_ready"], i)
                    for q in range(4):
                        slot = (q + 1) % 3 if n0 else q % 3
                        pe.wait_ge(low[key], (6 * i - 2 + q if n0 else q) + 1)
                        for j in range(4):
                            k = 4 * (q % 2) + j
                            mm = three(ps[:, q // 2], xgTh[:, k], xgTl[:, k], wh[:, slot, j], wl[:, slot, j],
                                       start=(k == 0), stop=(k == KT_D - 1))
                        mm.then_inc(used[key], 1)

                def turn_x(i):
                    pe.wait_ge(s["gathered"], 16 * (i + 1))
                    after(pe, s["xg_low"], i)
                    for k in range(KT_D):
                        mm = pe.transpose(ps[:, 2 + k // 4, k % 4 * P:(k % 4 + 1) * P], xg[:, k * P:(k + 1) * P], ident)
                    mm.then_inc(s["xg_tr"], 1)

                def turn_h(i):
                    pe.wait_ge(s["h_ready"], i + 1)
                    after(pe, s["h_low"], i)
                    for k in range(4):
                        mm = pe.transpose(ps[:, 6, k * P:(k + 1) * P], hb[:, k * P:(k + 1) * P], ident)
                    mm.then_inc(s["h_tr"], 1)

                def down(i, n, slots):
                    pe.wait_ge(s["h_low"], i + 1)
                    after(pe, s["y_ready"], i)
                    for r in range(2):
                        pe.wait_ge(low[key], n + r + 1)
                        for j in range(4):
                            mm = three(ps[:, 4 + r], hTh[:, j], hTl[:, j], wh[:, slots[r], j], wl[:, slots[r], j],
                                       start=(j == 0), stop=(j == 3))
                        mm.then_inc(used[key], 1)

                turn_x(0)
                up(0, 0)
                turn_x(1)
                turn_h(0)
                pe.wait_ge(plan, l + 1)
                blocks = pe.value_load(table[0:1, LIST_COLS - 1:LIST_COLS], min_val=0, max_val=MAX_BLOCKS - EXPERTS) + EXPERTS

                def body(i):
                    up(i, 1)
                    turn_x(i + 1)
                    down(i - 1, 6 * i + 2, (2, 0))
                    turn_h(i)
                body(1)
                with pe.Fori(2, blocks) as i:
                    body(i)
                down(blocks - 1, 6 * blocks - 2, (1, 2))
                return blocks

            route(0, M_ROUTE_A, T_LN1A, 1)
            blocks = moe_pe(0, M_QKV)
            for t in range(TILES):
                pe.wait_ge(ln_out, 2 * TILES + t + 1)
                turn(t, T_LN2A, x)
            pe.wait_ge(tr_low, T_LN2A + 10)
            pe.wait_ge(moe[0]["y_ready"], blocks)

            def turn_kq(kk, step):
                m = ROWS[kk % 5]
                pe.wait_ge(proj_free, step + 1)
                after(pe, kq_copied, kk - 1)
                for j in range(4):
                    mm = pe.transpose(ps[:, 6 + kk % 2, j * P:j * P + m], stg[0:m, kk % 5, j * P:(j + 1) * P],
                                      ident[0:m, 0:m])
                mm.then_inc(kq_tr, 1)
            for j in range(6):
                between = None
                if j in (1, 2, 5):
                    kk0 = 5 * (j - 1) if j < 5 else 10
                    def between(t, kk0=kk0, j=j):
                        turn_kq(kk0 + t, M_QKV + 5 * (j - 1) + t)
                project("b", 2 * j, M_QKV + 5 * j, between)
            for t in range(TILES):
                turn_kq(15 + t, M_QKV + 25 + t)

            def scores(n):
                qt, h = n // HEADS, n % HEADS
                w = (qt + 1) * P
                after(pe, at_exp, n)
                for part in range(2):
                    r = slice(64 * part, 64 * part + 64)
                    mm = pe.matmul(ps[:, part, 0:w], QT[r, h, qt * P:(qt + 1) * P], KT[r, h, 0:w],
                                   start=True, stop=True)
                mm.then_inc(at_s, 1)

            def turn_p(n):
                pe.wait_ge(at_p, n + 1)
                after(pe, at_ptc, n)
                for b in range(n // HEADS + 1):
                    mm = pe.transpose(ps[:, 2, b * P:(b + 1) * P], Pm[:, n % 2, b * P:(b + 1) * P], ident)
                mm.then_inc(at_pt, 1)

            def values(n):
                qt, h = n // HEADS, n % HEADS
                pe.wait_ge(at_ptc, n + 1)
                after(pe, at_o, n)
                for b in range(qt + 1):
                    mm = pe.matmul(ps[:, 3, 0:P], PTs[:, n % 2, b * P:(b + 1) * P], x[:, b, h * P:(h + 1) * P],
                                   start=(b == 0), stop=(b == qt))
                mm.then_inc(at_pv, 1)

            def cache_chunk(g, j):
                c = B_CACHE + 4 * g + j
                pe.wait_ge(raw_b[c % RAW_SLOTS], landed_b[c])
                return raw[:, c % RAW_SLOTS].rearrange("p (a k) n -> p a (k n)", a=2)

            def turn_keys(g, hk):
                b2, page, half = hk // 4, hk // 2 % 2, hk % 2
                keys = cache_chunk(g, b2)
                after(pe, sm_ktc, 8 * g + hk)
                for jj in range(4):
                    h = 4 * half + jj
                    mm = pe.transpose(ps[:, 4, jj * P:(jj + 1) * P], keys[:, page, h * P:(h + 1) * P], ident)
                mm.then_inc(sm_kt, 1)

            def sample_scores(g, b2, half):
                if half == 0:
                    pe.wait_ge(sm_ktc, 8 * g + 4 * b2 + 4)
                    pe.sem_inc(keys_used, 1)
                    if b2 == 0:
                        pe.wait_ge(sm_q, g + 1)
                        after(pe, sm_ptz, g)
                for h in range(4 * half, 4 * half + 4):
                    lhs = qpad[:, (b2 * 8 + h) * P:(b2 * 8 + h + 1) * P]
                    pe.matmul(ps[:, 5, 0:256], lhs, kts[:, b2, h], start=(b2 == 0 and h == 0), stop=False,
                              skip_group_check=True)
                    mm = pe.matmul(ps[:, 5, 256:288], lhs, KT[:, h, SEQ:NTOK], start=False,
                                   stop=(b2 == 1 and h == HEADS - 1), skip_group_check=True)
                if half:
                    mm.then_inc(sm_s, 1)

            def turn_sample_p(g):
                pe.wait_ge(sm_p, g + 1)
                pe.transpose(ps[:, 5, 0:P], Ps[:, 0:P], ident)
                pe.transpose(ps[:, 5, P:2 * P], Ps[:, P:2 * P], ident)
                pe.transpose(ps[0:NSAMP, 5, 2 * P:3 * P], Ps[:, 256:288], ident).then_inc(sm_pt, 1)

            def sample_values(g, b2):
                vals = cache_chunk(g, 2 + b2)
                pe.wait_ge(sm_ptz, g + 1)
                for page in range(2):
                    for h in range(HEADS):
                        mm = pe.matmul(ps[0:NSAMP, 6 + h // 4, h % 4 * P:(h % 4 + 1) * P], ptz[:, page, b2, h],
                                       vals[:, page, h * P:(h + 1) * P],
                                       start=(g == 0 and b2 == 0 and page == 0 and h % 4 == 0), stop=False,
                                       skip_group_check=True)
                mm.then_inc(vals_used, 1)
                if b2:
                    pe.wait_ge(vals_used, 2 * g + 2)
                    pe.sem_inc(sm_pv, 1)

            pe.wait_ge(kq_copied, 20)
            pe.wait_ge(proj_free, M_WO)
            steps = 4 * HEADS
            scores(0)
            for n in range(steps):
                g, j = n // 8, n % 8
                if n + 1 < steps:
                    scores(n + 1)
                if j < 4:
                    turn_keys(g, 2 * j)
                turn_p(n)
                if n >= 1:
                    values(n - 1)
                if j < 4:
                    turn_keys(g, 2 * j + 1)
                if j == 1 and g:
                    turn_sample_p(g - 1)
                if j == 2 and g:
                    sample_values(g - 1, 0)
                if 3 <= j < 7:
                    sample_scores(g, (j - 3) // 2, (j - 3) % 2)
                if j == 7 and g:
                    sample_values(g - 1, 1)
            values(steps - 1)
            turn_sample_p(3)
            sample_values(3, 0)
            sample_values(3, 1)
            for h in range(HEADS):
                mm = pe.matmul(ps[0:NSAMP, 6 + h // 4, h % 4 * P:(h % 4 + 1) * P], ptn[:, h],
                               x[0:NSAMP, 4, h * P:(h + 1) * P], start=False, stop=(h % 4 == 3), skip_group_check=True)
            mm.then_inc(sm_pv, 1)

            pe.wait_ge(sm_o, 1)
            for t in range(TILES):
                pe.wait_ge(om_r, t + 1)
                turn(t, T_O, o)
            pe.wait_ge(tr_low, T_O + 10)
            for cb in range(2):
                project("b", B_CACHE + 2 * cb, M_WO + 5 * cb)
            route(1, M_ROUTE_B, T_LN1B, 3)
            moe_pe(1, M_END)


IN_NAMES = ["con", "con16", "cmix", "x_prompt", "x_sample", "x_prompt_T", "x_sample_T", "w_s_T", "b_s_T", "b_s_rep",
            "cache_k", "cache_v", "page_table", "ln1_g", "ln1_b", "ln2_g", "ln2_b", "a_w_in", "a_b_in", "a_lnv_g",
            "a_lnv_b", "a_w_out", "w_k", "w_v", "b_w_q", "b_lam_q1", "b_lam_k1", "b_lam_q2", "b_lam_k2", "b_subln_g",
            "b_w_o", "router_w", "router_bias", "moe_w_up", "moe_w_down"]
OUT_SHAPES = [(1, SEQ, D), (DEC_B, DEC_T, D), (1, SEQ, HEADS, P), (1, SEQ, HEADS, P), (DEC_B, DEC_T, HEADS, P),
              (DEC_B, DEC_T, HEADS, P), (1, DEC_B, DEC_T, D)]


def kernel(**inputs):
    import concourse.bacc as bacc
    from concourse.bass_utils import run_bass_kernel_spmd

    arrays = {k: np.asarray(x) for k, x in inputs.items()}
    arrays["x_prompt_T"] = arrays["x_prompt"][0].T
    arrays["x_sample_T"] = arrays["x_sample"].reshape(NSAMP, D).T
    arrays["w_s_T"] = arrays["a_w_s"][0].transpose(2, 0, 1)
    arrays["b_s_T"] = arrays["a_b_s"][0].T
    arrays["b_s_rep"] = np.tile(arrays["a_b_s"][0, :, 0:DEC_T].T, (DEC_B, 1))
    arrays["con"], arrays["con16"], arrays["cmix"] = constants()

    nc = bacc.Bacc("TRN2", target_bir_lowering=False, num_devices=1)
    given, aps = {}, {}
    for name in IN_NAMES:
        arr = np.ascontiguousarray(arrays[name])
        given[f"in_{name}"] = arr
        aps[name] = nc.dram_tensor(f"in_{name}", arr.shape, mybir.dt.from_np(arr.dtype), kind="ExternalInput").ap()
    outs = [nc.dram_tensor(f"out_{i}", s, F32, kind="ExternalOutput").ap() for i, s in enumerate(OUT_SHAPES)]
    trunk(nc, aps, outs)
    r = run_bass_kernel_spmd(nc, [given], core_ids=[0])
    return tuple(r.results[0][f"out_{i}"] for i in range(len(OUT_SHAPES)))
```

```python
import math
from contextlib import ExitStack

import numpy as np

import concourse.bass as bass
from concourse import mybir

F32 = mybir.dt.float32
F32R = mybir.dt.float32r
F16 = mybir.dt.float16
BF16 = mybir.dt.bfloat16
I32 = mybir.dt.int32
ALU = mybir.AluOpType
ACT = mybir.ActivationFunctionType
AX = mybir.AxisListType.X

P = 128
D = 1024
KT_D = D // P
SEQ = 512
DEC_B, DEC_T = 8, 4
NSAMP = DEC_B * DEC_T
NTOK = SEQ + NSAMP
TILES = 5
ROWS = [P, P, P, P, NSAMP]
LAYERS = 2
ALPHA = (2.0 * LAYERS) ** 0.25
EPS = 1e-5
NEG = -1e30
HEADS = 8
HEAD_DIM = 64
SCALE = HEAD_DIM ** -0.5
LAM_INIT = 0.8 - 0.6 * math.exp(-0.3 * 1)
EXPERTS, GROUPS, PER_GROUP = 16, 4, 4
MAX_BLOCKS = EXPERTS + (2 * NTOK) // P
LIST_COLS = MAX_BLOCKS + 1
RAW_SLOTS = 6
SPLIT_SLOTS = 3
HALF = 512
PROJ_BANKS = 6
NO_ROW = 8192.0

A_WS, A_WOUT, A_CHUNKS, A_SPLITS = 8, 9, 13, 12
B_CACHE, B_WO, B_CHUNKS, B_SPLITS = 12, 28, 32, 16

M_WIN, M_MIX, M_WOUT, M_ROUTE_A, M_QKV, M_WO, M_ROUTE_B, M_END = 0, 20, 30, 40, 43, 73, 83, 86
T_US, T_LN1A, T_LN2A, T_O, T_LN1B = 0, 10, 20, 30, 40

C_IDENT, C_CAUSAL, C_IOTA, C_SMASK, C_RK4, C_RK16, C_IOTA16, C_IOTA8, C_THR, C_ID1, C_VALID, C_COEF, C_BEYOND, C_END = (
    0, 128, 256, 384, 512, 516, 532, 548, 556, 560, 570, 575, 577, 582)


def constants():
    c = np.zeros((P, C_END), np.float32)
    i = np.arange(P)
    c[:, C_IDENT:C_IDENT + P] = np.eye(P)
    c[:, C_CAUSAL:C_CAUSAL + P] = np.where(i[None, :] <= i[:, None], 0.0, NEG)
    c[:, C_IOTA:C_IOTA + P] = i[None, :]
    row_b, row_q = i // 64, i % 4
    for g in range(4):
        j = np.arange(NSAMP)
        ok = (j[None, :] // DEC_T == 2 * g + row_b[:, None]) & (j[None, :] % DEC_T <= row_q[:, None])
        c[:, C_SMASK + 32 * g:C_SMASK + 32 * g + 32] = np.where(ok, 0.0, NEG)
    c[:, C_RK4:C_RK4 + 4] = 4 - np.arange(4)
    c[:, C_RK16:C_RK16 + 16] = 16 - np.arange(16)
    c[:, C_IOTA16:C_IOTA16 + 16] = np.arange(16)
    c[:, C_IOTA8:C_IOTA8 + 8] = np.arange(8)
    c[:, C_THR:C_THR + 4] = 128.0 * (1 + np.arange(4))
    for k in range(2):
        for t in range(TILES):
            c[:ROWS[t], C_ID1 + k * TILES + t] = k * NTOK + t * P + i[:ROWS[t]] + 1
    c[:, C_VALID:C_VALID + TILES] = 1.0
    c[NSAMP:, C_VALID + TILES - 1] = 0.0
    c[NSAMP:, C_BEYOND + TILES - 1] = 1.0
    part = (i // 4) % 2
    c[:, C_COEF] = part == 0
    c[:, C_COEF + 1] = part == 1
    c16 = np.zeros((P, 2 * P), np.float16)
    c16[:, 0:P] = i[:, None] < i[None, :]
    c16[:, P:2 * P] = 1.0
    s = np.arange(NSAMP)
    cmix = np.zeros((P, P + NSAMP), np.float32)
    cmix[:, 0:P] = i[:, None] <= i[None, :]
    cmix[:NSAMP, P:] = (s[:, None] // DEC_T == s[None, :] // DEC_T) & (s[:, None] <= s[None, :])
    return c, c16, cmix


def last_before(slot, slots, count):
    return max(i for i in range(count) if i % slots == slot)


def trunk(nc, a, outs):
    y_prompt, y_sample, k_prompt, v_prompt, k_sample, v_sample, state_v = outs
    with ExitStack() as ctx:
        def sem(name):
            return ctx.enter_context(nc.semaphore(name))

        top = [(nc.sbuf_base + 63) // 64 * 64]

        def place(name, shape, dt, at=None):
            size = int(np.prod(shape[1:])) * (2 if dt in (F16, BF16) else 4)
            off = top[0] if at is None else at
            t = nc.alloc_sbuf_tensor_at(name, shape, dt, offset=off)
            if at is None:
                top[0] += (size + 31) // 32 * 32
                assert top[0] <= nc.sbuf_usable_end
            assert off + size <= nc.sbuf_usable_end
            return t, off + (size + 31) // 32 * 32

        raw = place("raw", [P, RAW_SLOTS, 4, HALF], F32)[0]
        x = place("x", [P, TILES, D], F32)[0]
        xT_at = top[0]
        xTh = place("xTh", [P, KT_D, NTOK], F32R)[0]
        xTl = place("xTl", [P, KT_D, NTOK], F32R)[0]
        split_at = top[0]
        wh = place("wh", [P, SPLIT_SLOTS, 4, HALF], F32R)[0]
        wl = place("wl", [P, SPLIT_SLOTS, 4, HALF], F32R)[0]
        gb = place("gb", [P, 2 * D], F32)[0]
        con = place("con", [P, C_END], F32)[0]
        con16 = place("con16", [P, 2 * P], F16)[0]
        idmask = place("idmask", [P, 2, P], BF16)[0]
        rwhl = place("rwhl", [P, KT_D, 2, EXPERTS], F32R)[0]
        rwh, rwl = rwhl[:, :, 0], rwhl[:, :, 1]
        rbias = place("rbias", [P, EXPERTS], F32)[0]
        stats = place("stats", [P, TILES, 2, 6], F32)[0]
        mv = place("mv", [P, TILES, 2], F32)[0]
        lns = place("lns", [P, 4, TILES], F32)[0]
        gates = place("gates", [P, 2, TILES], F32)[0]
        gidx = place("gidx", [P, LIST_COLS], I32)[0]
        sidx = place("sidx", [P, LIST_COLS], I32)[0]
        gcur = place("gcur", [P, 1], I32)[0]
        scur = place("scur", [P, 1], I32)[0]
        table = place("table", [P, LIST_COLS], I32)[0]
        pages = place("pages", [P, 16], I32)[0]
        lamc = place("lamc", [P, 12], F32)[0]
        warm = place("warm", [P, 4], F32)[0]
        arena = top[0]
        u, n = place("u", [P, TILES, D], F32, arena)
        v, n = place("v", [P, TILES, D], F32, n)
        cmix, n = place("cmix", [P, P + NSAMP], F32, n)
        wsm, n = place("wsm", [NSAMP, HEADS, NSAMP], F32, n)
        bsp, n = place("bsp", [P, 8], F32, n)
        bss, n = place("bss", [NSAMP, 8], F32, n)
        xT0 = place("xT0", [P, KT_D, NTOK], F32, arena)[0]
        rw_raw = place("rw_raw", [P, KT_D, EXPERTS], F32, arena + 20480)[0]
        QT, n = place("QT", [P, HEADS, NTOK], F32, arena)
        KT, n = place("KT", [P, HEADS, NTOK], F32, n)
        stg, _ = place("stg", [P, TILES, HALF], F32, n)
        slot_bytes = 4 * HALF * 4
        wl_at = split_at + SPLIT_SLOTS * slot_bytes
        E, _ = place("E", [P, 2, 2, HALF], F32, split_at)
        Pm, n2 = place("Pm", [P, 2, HALF], F32, wl_at)
        PTs, _ = place("PTs", [P, 2, HALF], F32, n2)
        o01, _ = place("o01", [P, 2, D], F32, split_at + 2 * slot_bytes)
        o23, _ = place("o23", [P, 2, D], F32, wl_at + 2 * slot_bytes)
        o4, n = place("o4", [P, 1, D], F32, n)
        osq, n = place("osq", [P, D], F32, n)
        lamp, n = place("lamp", [P, 2, HEAD_DIM], F32, n)
        oss, n = place("oss", [P, 3, TILES, HEADS], F32, n)
        mxs, n = place("mxs", [P, 4, 2, 2], F32, n)
        o = [o01[:, 0], o01[:, 1], o23[:, 0], o23[:, 1], o4[:, 0]]
        kts, n = place("kts", [P, 2, HEADS, 256], F32, xT_at)
        qpad, n = place("qpad", [P, 2176], F32, n)
        Es, n = place("Es", [P, 288], F32, n)
        Ps, n = place("Ps", [P, 288], F32, n)
        ptz, n = place("ptz", [P, 2, 2, HEADS, NSAMP], F32, n)
        ptn, n = place("ptn", [NSAMP, HEADS, NSAMP], F32, n)
        smx, n = place("smx", [P, 6], F32, n)
        assert n <= split_at
        subg = lamc[:, 8:9]
        xg, n = place("xg", [P, D], F32, arena)
        xgTh, n = place("xgTh", [P, KT_D, P], F32R, n)
        xgTl, n = place("xgTl", [P, KT_D, P], F32R, n)
        sg, n = place("sg", [P, HALF], F32, n)
        hb, n = place("hb", [P, HALF], F32, n)
        hTh, n = place("hTh", [P, 4, P], F32R, n)
        hTl, n = place("hTl", [P, 4, P], F32R, n)
        yb, n = place("yb", [P, D], F32, n)
        yl, _ = place("yl", [P, TILES, 2, D], F32, arena)
        lg, n = place("lg", [P, TILES, EXPERTS], F32, n)
        prob, n = place("prob", [P, TILES, EXPERTS], F32, n)
        sel, n = place("sel", [P, TILES, EXPERTS], F32, n)
        tmp, n = place("tmp", [P, 2, TILES, EXPERTS], F32, n)
        oh, n = place("oh", [P, 2, TILES, EXPERTS], F32, n)
        hilo, n = place("hilo", [P, 2, TILES * GROUPS, 2], F32, n)
        gsc, n = place("gsc", [P, 4, TILES, GROUPS], F32, n)
        col, n = place("col", [P, 12, 2, TILES], F32, n)
        cnt, n = place("cnt", [P, 6, EXPERTS], F32, n)
        thr, n = place("thr", [P, 16, 16], F32, n)
        tblf, n = place("tblf", [P, LIST_COLS], F32, n)
        lst, n = place("lst", [P, 4, LIST_COLS], F32, n)
        m16, n = place("m16", [P, TILES, EXPERTS], F16, n)
        lo16, n = place("lo16", [P, 2 * TILES, P], F16, n)
        hi16, n = place("hi16", [P, 2 * TILES, LIST_COLS + 1], F16, n)
        ahead_up = [place(f"ahead_up{q}", [P, 4, HALF], F32, xT_at + q * slot_bytes)[0] for q in range(4)]
        assert 4 * slot_bytes <= split_at - xT_at
        ahead_down = place("ahead_down", [P, 4, HALF], F32, n)[0]
        ps = nc.alloc_psum_tensor("ps", [P, 8, HALF], F32)

        x_rows = [nc.dram_tensor(f"x_rows{l}", (NTOK, D), F32).ap() for l in range(LAYERS)]
        y_rows = [nc.dram_tensor(f"y_rows{l}", (2 * NTOK, D), F32).ap() for l in range(LAYERS)]
        x_parked = nc.dram_tensor("x_parked", (NTOK, D), F32).ap()

        con_in = sem("con_in"); rb_in = sem("rb_in"); xT0_in = sem("xT0_in"); rw_in = sem("rw_in"); x_in = sem("x_in")
        mixc_in = sem("mixc_in"); wsm_in = sem("wsm_in"); gb_in = sem("gb_in"); lam_in = sem("lam_in")
        pages_in = sem("pages_in")
        x0_high = sem("x0_high"); x0_low = sem("x0_low")
        rw_high = sem("rw_high"); rw_low = sem("rw_low")
        wsm_zeroed = sem("wsm_zeroed"); ws_masked = sem("ws_masked")
        raw_a = [sem(f"raw_a{i}") for i in range(RAW_SLOTS)]
        raw_b = [sem(f"raw_b{i}") for i in range(RAW_SLOTS)]
        raw_m = [[sem(f"raw_m{l}_{i}") for i in range(RAW_SLOTS)] for l in range(LAYERS)]
        y_in = [sem(f"y_in{t}") for t in range(TILES)]
        ahead_in = [sem(f"ahead{q}") for q in range(5)]
        high = {k: sem(f"high_{k}") for k in ("a", "b", "m0", "m1")}
        low = {k: sem(f"low_{k}") for k in ("a", "b", "m0", "m1")}
        used = {k: sem(f"used_{k}") for k in ("a", "b", "m0", "m1")}
        mix_done = sem("mix_done")
        proj_done = sem("proj_done"); proj_free = sem("proj_free")
        gelu_done = sem("gelu_done")
        tr_done = sem("tr_done"); tr_high = sem("tr_high"); tr_low = sem("tr_low")
        ln_var = sem("ln_var"); ln_std = sem("ln_std"); ln_rs = sem("ln_rs"); ln_norm = sem("ln_norm")
        ln_gain = sem("ln_gain"); ln_out = sem("ln_out")
        dve_step = sem("dve_step")
        stg_out = [sem(f"stg_out{t}") for t in range(TILES)]
        vs_out = sem("vs_out"); x_out = sem("x_out"); park_out = sem("park_out"); park_in = sem("park_in")
        kv_out = sem("kv_out"); y_out = sem("y_out")
        kq_tr = sem("kq_tr"); kq_copied = sem("kq_copied")
        exp_r = sem("exp_r"); lam_exp = sem("lam_exp"); lam_sum = sem("lam_sum")
        idmask_ready = sem("idmask_ready")
        at_s = sem("at_s"); at_max = sem("at_max"); at_exp = sem("at_exp"); at_p = sem("at_p")
        at_pt = sem("at_pt"); at_ptc = sem("at_ptc"); at_pv = sem("at_pv"); at_o = sem("at_o")
        sm_kt = sem("sm_kt"); sm_ktc = sem("sm_ktc"); sm_s = sem("sm_s"); sm_q = sem("sm_q")
        sm_max = sem("sm_max"); sm_exp = sem("sm_exp"); sm_p = sem("sm_p"); sm_pt = sem("sm_pt")
        sm_zero = sem("sm_zero"); sm_ptz = sem("sm_ptz"); sm_pv = sem("sm_pv"); sm_o = sem("sm_o")
        keys_used = sem("keys_used"); vals_used = sem("vals_used"); lnv_in = sem("lnv_in")
        om_var = sem("om_var"); om_std = sem("om_std"); om_r = sem("om_r")
        logit_max = sem("logit_max"); plan = sem("plan"); onehots = sem("onehots"); masks = sem("masks")
        moe = [{k: sem(f"{k}{l}") for k in (
            "gcopy", "gathered", "xg_tr", "xg_high", "xg_low", "silu", "h_ready", "h_tr", "h_high", "h_low",
            "y_ready", "scopy", "scattered", "xg_zero", "scaled")} for l in range(LAYERS)]

        ident = con[:, C_IDENT:C_IDENT + P]

        def after(eng, s, count):
            if not isinstance(count, int) or count > 0:
                eng.wait_ge(s, count)

        def dram_tile(t, ap):
            return ap[t * P:t * P + ROWS[t]]

        def chunk(w, kh, cb):
            return w[kh * HALF:(kh + 1) * HALF, cb * HALF:(cb + 1) * HALF].rearrange("(k p) n -> p k n", p=P)

        def down_chunk(w, cb):
            return w[:, cb * HALF:(cb + 1) * HALF].rearrange("(k p) n -> p k n", p=P)

        w_in, w_out = a["a_w_in"][0], a["a_w_out"][0]
        WIN_COLS = [2, 3, 0, 1]
        block = ctx.enter_context(nc.Block())
        low_a = {c: c + 1 - (c > A_WS) for c in range(A_CHUNKS) if c != A_WS}
        low_b = {c: c + 1 - (B_WO - B_CACHE) * (c >= B_WO) for c in range(B_CHUNKS) if not B_CACHE <= c < B_WO}
        landed_b = {c: sum(32 if B_CACHE <= d < B_WO else 16 for d in range(c % RAW_SLOTS, c + 1, RAW_SLOTS))
                    for c in range(B_CHUNKS)}

        def landed_a(c):
            return 16 * (c // RAW_SLOTS + 1)

        @block.sync
        def _(sp):
            def up(l, e, i, slot_free):
                for q in range(4):
                    slot_free(q)
                    sp.dma_start(raw[:, q], chunk(a["moe_w_up"][l, e], q % 2, q // 2)).then_inc(raw_m[l][q], 16)

            def down(l, e, i, slot_free):
                for r in range(1 if isinstance(i, int) and i == 1 else 0, 2):
                    slot_free(4 + r)
                    sp.dma_start(raw[:, 4 + r], down_chunk(a["moe_w_down"][l, e], r)).then_inc(raw_m[l][4 + r], 16)

            def moe_stream(l, first_free):
                low_m = low[f"m{l}"]

                def previous(i):
                    def free(slot):
                        if slot < 4:
                            sp.wait_ge(low_m, (slot if isinstance(i, int) and i == 2 else 6 * (i - 1) - 2 + slot) + 1)
                        else:
                            sp.wait_ge(low_m, 6 * (i - 1) + 8 + (slot - 4) + 1)
                    return free
                up(l, 0, 0, first_free)
                down(l, 0, 0, first_free)
                sp.wait_ge(proj_done, (M_ROUTE_B if l else M_ROUTE_A) + 1)
                sp.wait_ge(vs_out, 16)
                for q in range(4):
                    sp.dma_start(ahead_up[q][:], chunk(a["moe_w_up"][l, 1], q % 2, q // 2)).then_inc(ahead_in[q], 16)
                sp.dma_start(ahead_down[:], down_chunk(a["moe_w_down"][l, 1], 0)).then_inc(ahead_in[4], 16)
                up(l, 2, 2, previous(2))
                down(l, 1, 1, previous(1))
                with sp.Fori(3, EXPERTS - 1) as i:
                    up(l, i, i, previous(i))
                    down(l, i - 1, i - 1, previous(i - 1))
                sp.wait_ge(plan, l + 1)
                blocks = sp.value_load(table[0:1, LIST_COLS - 1:LIST_COLS], min_val=0, max_val=MAX_BLOCKS - EXPERTS) + EXPERTS
                with sp.Fori(EXPERTS - 1, blocks) as i:
                    e = sp.value_load(table[0:1, bass.ds(i, 1)], min_val=0, max_val=EXPERTS - 1)
                    up(l, e, i, previous(i))
                    before = sp.value_load(table[0:1, bass.ds(i - 1, 1)], min_val=0, max_val=EXPERTS - 1)
                    down(l, before, i - 1, previous(i - 1))
                e = sp.value_load(table[0:1, bass.ds(blocks - 1, 1)], min_val=0, max_val=EXPERTS - 1)
                down(l, e, blocks - 1, previous(blocks - 1))
                return blocks

            sp.dma_start(xT0[:, :, 0:SEQ], a["x_prompt_T"].rearrange("(k p) n -> p k n", p=P)).then_inc(xT0_in, 16)
            sp.dma_start(xT0[:, :, SEQ:NTOK], a["x_sample_T"].rearrange("(k p) n -> p k n", p=P)).then_inc(xT0_in, 16)
            for c in range(A_CHUNKS):
                s = c % RAW_SLOTS
                if c >= RAW_SLOTS:
                    sp.wait_ge(low["a"], low_a[c - RAW_SLOTS])
                if c < A_WS:
                    src = chunk(w_in, c % 2, WIN_COLS[c // 2])
                elif c == A_WS:
                    src = a["w_s_T"].rearrange("s (a g) t -> s a (g t)", a=2)
                else:
                    src = chunk(w_out, (c - A_WOUT) % 2, (c - A_WOUT) // 2)
                sp.dma_start(raw[:, s, 0:src.shape[1]], src).then_inc(raw_a[s], 16)

            def after_a(slot):
                c = last_before(slot, RAW_SLOTS, A_CHUNKS)
                if c == A_WS:
                    sp.wait_ge(mix_done, 1)
                else:
                    sp.wait_ge(low["a"], low_a[c])
            blocks = moe_stream(0, after_a)

            sp.wait_ge(pages_in, 16)

            def cache_freed(c):
                pair, which, b2 = (c - B_CACHE) // 4, (c - B_CACHE) // 2 % 2, (c - B_CACHE) % 2
                sp.wait_ge(vals_used if which else keys_used, 2 * pair + b2 + 1)
            for c in range(B_CHUNKS):
                s = c % RAW_SLOTS
                if c == 4:
                    sp.wait_ge(y_in[4], 16)
                if c < RAW_SLOTS:
                    sp.wait_ge(low["m0"], 6 * blocks - 7 + s if s < 4 else 6 * blocks - 1 + (s - 4))
                elif B_CACHE <= c - RAW_SLOTS < B_WO:
                    cache_freed(c - RAW_SLOTS)
                else:
                    sp.wait_ge(low["b"], low_b[c - RAW_SLOTS])
                if B_CACHE <= c < B_WO:
                    pair, which, b2 = (c - B_CACHE) // 4, (c - B_CACHE) // 2 % 2, (c - B_CACHE) % 2
                    cache = a["cache_v"] if which else a["cache_k"]
                    for page in range(2):
                        j = (2 * pair + b2) * 2 + page
                        phys = sp.value_load(pages[0:1, j:j + 1], min_val=0, max_val=cache.shape[0] - 1)
                        sp.dma_start(raw[:, s, 2 * page:2 * page + 2, :].rearrange("p k n -> p (k n)"),
                                     cache[phys].rearrange("r h d -> r (h d)")).then_inc(raw_b[s], 16)
                else:
                    w = [a["w_k"], a["w_v"], a["b_w_q"][0]][c // 4] if c < B_CACHE else a["b_w_o"][0]
                    sp.dma_start(raw[:, s], chunk(w, c % 2, c // 2 % 2)).then_inc(raw_b[s], 16)

            def after_b(slot):
                c = last_before(slot, RAW_SLOTS, B_CHUNKS)
                if B_CACHE <= c < B_WO:
                    cache_freed(c)
                else:
                    sp.wait_ge(low["b"], low_b[c])
            moe_stream(1, after_b)

        @block.gpsimd
        def _(pool):
            def row(ap):
                return ap.unsqueeze(0).broadcast_to([P, ap.shape[0]])

            def load_gb(g, b):
                pool.dma_start(gb[:, 0:D], row(g)).then_inc(gb_in, 16)
                pool.dma_start(gb[:, D:2 * D], row(b)).then_inc(gb_in, 16)

            def gain(call, src):
                if call:
                    pool.wait_ge(gb_in, 16 + 32 * call)
                else:
                    pool.wait_ge(lnv_in, 32)
                for t in range(TILES):
                    m = ROWS[t]
                    pool.wait_ge(ln_norm, TILES * call + t + 1)
                    pool.tensor_tensor(src[0:m, t], src[0:m, t], gb[0:m, 0:D] if call else x[0:m, 0], ALU.mult).then_inc(ln_gain, 1)

            pool.dma_start(rw_raw[:], a["router_w"].rearrange("(k p) e -> p k e", p=P)).then_inc(rw_in, 16)
            pool.dma_start(gb[:], row(a["a_b_in"][0])).then_inc(gb_in, 16)
            pool.dma_start(rbias[:], row(a["router_bias"])).then_inc(rb_in, 16)
            pool.dma_start(x[:, 0], row(a["a_lnv_g"][0])).then_inc(lnv_in, 16)
            pool.dma_start(x[:, 1], row(a["a_lnv_b"][0])).then_inc(lnv_in, 16)
            pool.dma_start(pages[0:1, :], a["page_table"].rearrange("b n -> (b n)").unsqueeze(0)).then_inc(pages_in, 16)
            pool.dma_start(cmix[:], a["cmix"]).then_inc(mixc_in, 16)
            pool.dma_start(bsp[:], a["b_s_T"]).then_inc(mixc_in, 16)
            pool.dma_start(bss[:], a["b_s_rep"]).then_inc(mixc_in, 16)
            pool.wait_ge(wsm_zeroed, 1)
            with nc.allow_non_contiguous_dma("4-row blocks of the spatial weights"):
                for b in range(DEC_B):
                    pool.dma_start(wsm[b * DEC_T:(b + 1) * DEC_T, :, b * DEC_T:(b + 1) * DEC_T],
                                   a["w_s_T"][0:DEC_T, :, 0:DEC_T]).then_inc(wsm_in, 16)

            gain(0, v)
            pool.wait_ge(ln_out, TILES)
            pool.wait_ge(ln_gain, TILES)
            for t in range(TILES):
                src = dram_tile(t, a["x_prompt"][0]) if t < 4 else a["x_sample"].rearrange("b t d -> (b t) d")
                pool.dma_start(x[0:ROWS[t], t], src).then_inc(x_in, 16)
            pool.dma_start(state_v.rearrange("l b t d -> (l b t) d"), v[0:NSAMP, 4]).then_inc(vs_out, 16)

            def moe_pool(l):
                s = moe[l]
                if l == 0:
                    pool.wait_ge(proj_free, M_WIN + 20)
                load_gb(a["ln1_g"][l], a["ln1_b"][l])
                gain(1 + 2 * l, x)
                for t in range(TILES):
                    pool.wait_ge(ln_out, TILES * (1 + 2 * l) + t + 1)
                    pool.dma_start(dram_tile(t, x_rows[l]), x[0:ROWS[t], t]).then_inc(x_out, 16)
                load_gb(a["ln2_g"][l], a["ln2_b"][l])
                pool.memset(xg[:], 0.0).then_inc(s["xg_zero"], 1)
                pool.wait_ge(s["xg_zero"], 1)
                pool.wait_ge(plan, l + 1)
                pool.wait_ge(x_out, 16 * TILES * (l + 1))
                blocks = pool.value_load(table[0:1, LIST_COLS - 1:LIST_COLS], min_val=0, max_val=MAX_BLOCKS - EXPERTS) + EXPERTS

                def wait_apart(n, *sems):
                    if isinstance(n, int):
                        count = n
                    else:
                        count = pool.to_reg(n)
                    pool.wait_ge(plan, l + 1)
                    for sm in sems:
                        pool.wait_ge(sm, count)

                def gather(i):
                    after(pool, s["xg_tr"], i)
                    after(pool, s["gathered"], 16 * i)
                    pool.tensor_copy(gcur[:], gidx[:, bass.ds(i, 1)]).then_inc(s["gcopy"], 1)
                    wait_apart(i + 1, s["gcopy"])
                    pool.indirect_dma_start(xg[:], None, x_rows[l], bass.IndirectOffsetOnAxis(ap=gcur[:, 0:1], axis=0),
                                            bounds_check=NTOK - 1, oob_is_err=False).then_inc(s["gathered"], 16)

                def scatter(i):
                    after(pool, s["scattered"], 16 * i)
                    pool.tensor_copy(scur[:], sidx[:, bass.ds(i, 1)]).then_inc(s["scopy"], 1)
                    wait_apart(i + 1, s["scopy"], s["y_ready"])
                    pool.indirect_dma_start(y_rows[l], bass.IndirectOffsetOnAxis(ap=scur[:, 0:1], axis=0), yb[:], None,
                                            bounds_check=2 * NTOK - 1, oob_is_err=False).then_inc(s["scattered"], 16)

                def scale(tiles):
                    for t in tiles:
                        m = ROWS[t]
                        pool.tensor_scalar(x[0:m, t], x[0:m, t], ALPHA, None, ALU.mult).then_inc(s["scaled"], 1)
                gather(0)
                gather(1)
                gather(2)
                scale(range(0, 2))
                gather(3)
                scale(range(2, 3))
                scatter(0)
                scale(range(3, TILES))
                with pool.Fori(3, blocks) as i:
                    gather(i + 1)
                    scatter(i - 2)
                scatter(blocks - 2)
                scatter(blocks - 1)
                wait_apart(16 * blocks, s["scattered"])
                wait_apart(blocks + 1, s["xg_low"])
                pairs = y_rows[l].rearrange("(k n) d -> n k d", k=2)
                for t in range(TILES):
                    pool.dma_start(yl[0:ROWS[t], t], dram_tile(t, pairs)).then_inc(y_in[t], 16)
                gain(2 + 2 * l, x)

            moe_pool(0)
            for t in range(TILES):
                pool.wait_ge(ln_out, 2 * TILES + t + 1)
                pool.dma_start(dram_tile(t, x_parked), x[0:ROWS[t], t]).then_inc(park_out, 16)
            for j, name in enumerate(("b_lam_q1", "b_lam_k1", "b_lam_q2", "b_lam_k2")):
                pool.dma_start(gb[:, j * HEAD_DIM:(j + 1) * HEAD_DIM], row(a[name][0])).then_inc(lam_in, 16)
            pool.dma_start(subg, a["b_subln_g"][0].unsqueeze(1)).then_inc(lam_in, 16)
            k_rows = [k_prompt[0].rearrange("s h d -> s (h d)"), k_sample.rearrange("b t h d -> (b t) (h d)")]
            v_rows = [v_prompt[0].rearrange("s h d -> s (h d)"), v_sample.rearrange("b t h d -> (b t) (h d)")]

            def out_tile(rows, t):
                return dram_tile(t, rows[0]) if t < 4 else rows[1]
            for cb in range(2):
                for t in range(TILES):
                    pool.wait_ge(proj_free, M_QKV + cb * TILES + t + 1)
                    pool.dma_start(out_tile(k_rows, t)[:, cb * HALF:(cb + 1) * HALF], stg[0:ROWS[t], t]
                                   ).then_inc(stg_out[t], 16)
            for t in range(TILES):
                pool.wait_ge(proj_free, M_QKV + 3 * TILES + t + 1)
                pool.dma_start(out_tile(v_rows, t), x[0:ROWS[t], t]).then_inc(kv_out, 16)
            pool.wait_ge(used["b"], B_CACHE)
            for g in range(4):
                after(pool, sm_pv, g)
                pool.memset(ptz[:], 0.0).then_inc(sm_zero, 1)
            pool.wait_ge(kv_out, 16 * TILES)
            pool.wait_ge(park_out, 16 * TILES)
            pool.wait_ge(sm_o, 1)
            pool.wait_ge(at_o, 4 * HEADS)
            for t in range(TILES):
                pool.dma_start(x[0:ROWS[t], t], dram_tile(t, x_parked)).then_inc(park_in, 16)
            pool.wait_ge(lam_sum, 1)
            moe_pool(1)
            y_tiles = [y_prompt[0], y_sample.rearrange("b t d -> (b t) d")]
            for t in range(TILES):
                pool.wait_ge(ln_out, 4 * TILES + t + 1)
                pool.dma_start(out_tile(y_tiles, t), x[0:ROWS[t], t]).then_inc(y_out, 16)
            pool.wait_ge(y_out, 16 * TILES)
            pool.wait_ge(vs_out, 16)
            for t in range(TILES):
                pool.wait_ge(stg_out[t], 32)

        @block.scalar
        def _(act):
            act.dma_start(con[:], a["con"]).then_inc(con_in, 16)
            act.dma_start(con16[:], a["con16"]).then_inc(con_in, 16)

            def split_high(key, n, slot, src, landed, count):
                act.wait_ge(landed, count)
                if not (isinstance(n, int) and n < SPLIT_SLOTS):
                    act.wait_ge(used[key], n - SPLIT_SLOTS + 1)
                act.activation(wh[:, slot], src, ACT.Copy).then_inc(high[key], 1)

            def split_a(s):
                c = s + (s >= A_WS)
                split_high("a", s, s % SPLIT_SLOTS, raw[:, c % RAW_SLOTS], raw_a[c % RAW_SLOTS], landed_a(c))

            def split_b(s):
                c = s if s < B_CACHE else s - B_CACHE + B_WO
                split_high("b", s, s % SPLIT_SLOTS, raw[:, c % RAW_SLOTS], raw_b[c % RAW_SLOTS], landed_b[c])

            def turn_high(n0, gain=1.0):
                for n in (n0, n0 + 1):
                    t, half = n % 10 // 2, n % 2
                    act.wait_ge(tr_done, n + 1)
                    act.activation(xTh[:, 4 * half:4 * half + 4, t * P:t * P + ROWS[t]],
                                   ps[:, 6 + n % 2].rearrange("p (k m) -> p k m", k=4)[:, :, 0:ROWS[t]],
                                   ACT.Copy, scale=gain).then_inc(tr_high, 1)

            def gelu(dst, m0, cols):
                for t in range(TILES):
                    act.wait_ge(proj_free, m0 + t + 1)
                    w = dst[0:ROWS[t], t, cols:cols + HALF]
                    act.activation(w, w, ACT.Gelu_apprx_tanh).then_inc(gelu_done, 1)

            def normalise(call, t, src):
                m, n = ROWS[t], TILES * call + t + 1
                act.wait_ge(ln_var, n)
                act.activation(lns[0:m, 1, t:t + 1], lns[0:m, 0, t:t + 1], ACT.Sqrt).then_inc(ln_std, 1)
                act.wait_ge(ln_rs, n)
                act.activation(src[0:m, t], src[0:m, t], ACT.Identity, bias=lns[0:m, 3, t:t + 1],
                               scale=lns[0:m, 2, t:t + 1]).then_inc(ln_norm, 1)

            def ln_tiles(call, src, t0):
                for i in range(TILES + 3):
                    if i >= 3:
                        turn_high(t0 + 2 * (i - 3))
                    if i < TILES:
                        normalise(call, i, src)

            act.wait_ge(xT0_in, 32)
            for half in range(2):
                act.activation(xTh[:, 4 * half:4 * half + 4], xT0[:, 4 * half:4 * half + 4], ACT.Copy).then_inc(x0_high, 1)
            split_a(0)
            split_a(1)
            act.wait_ge(rw_in, 16)
            act.activation(rwh, rw_raw[:], ACT.Copy).then_inc(rw_high, 1)
            for j in range(4):
                split_a(2 * j + 2)
                split_a(2 * j + 3)
                if j == 2:
                    for t in range(TILES):
                        normalise(0, t, v)
                gelu(v if j < 2 else u, M_WIN + 5 * j, j % 2 * HALF)
            for t in range(TILES):
                turn_high(T_US + 2 * t)
            split_a(10)
            split_a(11)

            def moe_act(l, first_used, base_key):
                s, key = moe[l], f"m{l}"

                def split(n, slot, q, i):
                    if isinstance(i, int) and i == 1 and q < 5:
                        src = ahead_up[q] if q < 4 else ahead_down
                        split_high(key, n, slot, src[:], ahead_in[q], 16 * (l + 1))
                    elif (isinstance(i, int) and i == 0) or q == 5:
                        split_high(key, n, slot, raw[:, q], raw_m[l][q], 16 * (i + 1))
                    else:
                        split_high(key, n, slot, raw[:, q], raw_m[l][q], 16 * i)

                for n in range(3):
                    if n == 2:
                        act.wait_ge(logit_max, l + 1)
                        act.activation(prob[:], lg[:], ACT.Exp).then_inc(exp_r, 1)
                        act.activation(warm[:, 1 + 2 * l:2 + 2 * l], ident[:, 0:1], ACT.Silu)
                    act.wait_ge(used[base_key], first_used[n])
                    split(n, n, n, 0)
                    if n == 1:
                        act.activation(warm[:, 2 * l:1 + 2 * l], ident[:, 0:1], ACT.Exp)

                def xg_high(i):
                    act.wait_ge(s["xg_tr"], i + 1)
                    act.activation(xgTh[:], ps[:, 2:4].rearrange("p a (k m) -> p (a k) m", m=P), ACT.Copy
                                   ).then_inc(s["xg_high"], 1)

                def silu(i):
                    act.wait_ge(used[key], 6 * i + 2 if not (isinstance(i, int) and i == 0) else 4)
                    after(act, s["h_ready"], i)
                    act.activation(sg[:], ps[:, 0], ACT.Silu).then_inc(s["silu"], 1)

                def h_high(i):
                    act.wait_ge(s["h_tr"], i + 1)
                    act.activation(hTh[:], ps[:, 6].rearrange("p (k m) -> p k m", k=4), ACT.Copy
                                   ).then_inc(s["h_high"], 1)

                def y_out_(i, n_last):
                    act.wait_ge(used[key], n_last)
                    after(act, s["scattered"], 16 * i)
                    act.activation(yb[:], ps[:, 4:6].rearrange("p a n -> p (a n)"), ACT.Copy).then_inc(s["y_ready"], 1)

                def body(i, first=False):
                    if not first:
                        split(6 * i - 2, 1, 0, i)
                        split(6 * i - 1, 2, 1, i)
                        y_out_(i - 2, 6 * i - 2)
                    h_high(i - 1)
                    for q in range(2, 4):
                        split(6 * i - 2 + q, (q + 1) % 3, q, i)
                    for r in range(2):
                        split(6 * i + 2 + r, (r + 5) % 3, 4 + r, i - 1)
                    silu(i)
                    xg_high(i + 1)

                xg_high(0)
                split(3, 0, 3, 0)
                split(4, 1, 0, 1)
                split(5, 2, 1, 1)
                silu(0)
                xg_high(1)
                body(1, True)
                body(2)
                act.wait_ge(plan, l + 1)
                blocks = act.value_load(table[0:1, LIST_COLS - 1:LIST_COLS], min_val=0, max_val=MAX_BLOCKS - EXPERTS) + EXPERTS
                with act.Fori(3, blocks) as i:
                    body(i)
                for r in range(2):
                    split(6 * blocks - 2 + r, r + 1, 4 + r, blocks - 1)
                y_out_(blocks - 2, 6 * blocks - 2)
                h_high(blocks - 1)
                y_out_(blocks - 1, 6 * blocks)
                return blocks

            ln_tiles(1, x, T_LN1A)
            blocks = moe_act(0, [10, 11, 12], "a")
            act.wait_ge(used["m0"], 6 * blocks)
            for n in range(3):
                split_b(n)
            ln_tiles(2, x, T_LN2A)

            def kq_copy(kk):
                dst, cb, t = (KT if kk < 10 else QT), kk % 10 // 5, kk % 5
                act.wait_ge(kq_tr, kk + 1)
                act.activation(dst[:, 4 * cb:4 * cb + 4, t * P:t * P + ROWS[t]],
                               ps[:, 6 + kk % 2].rearrange("p (k m) -> p k m", k=4)[:, :, 0:ROWS[t]],
                               ACT.Copy, scale=1.0 if kk < 10 else SCALE).then_inc(kq_copied, 1)
            for j in range(6):
                if 0 < j < 5:
                    split_b(2 * j + 2)
                if j in (1, 2, 5):
                    for t in range(TILES):
                        kq_copy((0 if j < 5 else 10) + (j - 1) % 4 * 5 + t)
                if j < 5:
                    split_b(2 * j + 3)
            for t in range(TILES):
                kq_copy(15 + t)
            act.wait_ge(lam_sum, 1)
            act.activation(lamc[:, 2:4], lamc[:, 0:2], ACT.Exp).then_inc(lam_exp, 1)

            act.wait_ge(used["b"], B_CACHE)

            def att_exp(n, part):
                w = (n // HEADS + 1) * P
                act.wait_ge(at_max, 2 * n + part + 1)
                after(act, at_p, n - 1)
                act.activation(E[:, n % 2, part, 0:w], ps[:, part, 0:w], ACT.Exp, bias=mxs[:, 1, n % 2, part:part + 1],
                               accum_out=mxs[:, 2, n % 2, part:part + 1]).then_inc(at_exp, 1)

            def att_pt(n):
                w = (n // HEADS + 1) * P
                act.wait_ge(at_pt, n + 1)
                after(act, at_pv, n - 1)
                act.activation(PTs[:, n % 2, 0:w], ps[:, 2, 0:w], ACT.Copy).then_inc(at_ptc, 1)

            def att_o(n):
                act.wait_ge(at_pv, n + 1)
                act.activation(o[n // HEADS][:, n % HEADS * P:(n % HEADS + 1) * P], ps[:, 3, 0:P],
                               ACT.Copy, scale=mxs[:, 3, n % 2, 0:1]).then_inc(at_o, 1)

            def keys_copy(g, hk):
                b2, page, half = hk // 4, hk // 2 % 2, hk % 2
                act.wait_ge(sm_kt, 8 * g + hk + 1)
                after(act, sm_s, 2 * (g - 1) + b2 + 1)
                act.activation(kts[:, b2, 4 * half:4 * half + 4, page * P:(page + 1) * P],
                               ps[:, 4].rearrange("p (h m) -> p h m", m=P), ACT.Copy).then_inc(sm_ktc, 1)

            steps = 4 * HEADS
            for n in range(steps + 2):
                g, j = n // 8, n % 8
                if n < steps:
                    att_exp(n, 0)
                if n >= 2:
                    att_o(n - 2)
                if n < steps and j < 4:
                    keys_copy(g, 2 * j)
                if 1 <= n <= steps:
                    att_pt(n - 1)
                if n < steps:
                    att_exp(n, 1)
                    if j < 4:
                        keys_copy(g, 2 * j + 1)
                    if j == 6:
                        act.wait_ge(sm_max, g + 1)
                        act.activation(Es[:], ps[:, 5, 0:288], ACT.Exp, bias=smx[:, 1:2],
                                       accum_out=smx[:, 2:3]).then_inc(sm_exp, 1)
            act.wait_ge(at_p, steps)
            split_b(12)

            def head_std(part, tiles):
                act.wait_ge(om_var, part)
                act.activation(oss[:, 1, tiles], oss[:, 0, tiles], ACT.Sqrt).then_inc(om_std, 1)
            head_std(1, slice(0, 4))
            split_b(13)
            act.wait_ge(sm_pv, 5)
            act.activation(o[4][0:NSAMP], ps[0:NSAMP, 6:8].rearrange("p a n -> p (a n)"), ACT.Copy).then_inc(sm_o, 1)
            turn_high(T_O, subg)
            turn_high(T_O + 2, subg)
            head_std(2, slice(4, 5))
            for t in range(2, TILES):
                turn_high(T_O + 2 * t, subg)
            split_b(14)
            split_b(15)
            ln_tiles(3, x, T_LN1B)
            moe_act(1, [16, 14, 15], "b")
            for t in range(TILES):
                normalise(4, t, x)

        @block.vector
        def _(dve):
            chain = [0]

            def link(ins):
                chain[0] += 1
                ins.then_inc(dve_step, 1)
                dve.wait_ge(dve_step, chain[0])

            def split_low(key, n, slot, src):
                dve.wait_ge(high[key], n + 1)
                dve.tensor_tensor(wl[:, slot], src, wh[:, slot].bitcast(F32), ALU.subtract).then_inc(low[key], 1)

            def split_a(s):
                split_low("a", s, s % SPLIT_SLOTS, raw[:, (s + (s >= A_WS)) % RAW_SLOTS])

            def split_b(s):
                c = s if s < B_CACHE else s - B_CACHE + B_WO
                split_low("b", s, s % SPLIT_SLOTS, raw[:, c % RAW_SLOTS])

            def turn_low(n0, gain=1.0):
                for n in (n0, n0 + 1):
                    t, half = n % 10 // 2, n % 2
                    dve.wait_ge(tr_high, n + 1)
                    w = (slice(None), slice(4 * half, 4 * half + 4), slice(t * P, t * P + ROWS[t]))
                    dve.scalar_tensor_tensor(
                        out=xTl[w], in0=ps[:, 6 + n % 2].rearrange("p (k m) -> p k m", k=4)[:, :, 0:ROWS[t]],
                        scalar=gain, in1=xTh[w].bitcast(F32), op0=ALU.mult, op1=ALU.subtract).then_inc(tr_low, 1)

            def ln_stats(call, t, src):
                m = ROWS[t]
                dve.bn_stats(stats[0:m, t, 0], src[0:m, t, 0:HALF])
                link(dve.bn_stats(stats[0:m, t, 1], src[0:m, t, HALF:D]))
                link(dve.bn_aggr(mv[0:m, t], stats[0:m, t].rearrange("p a b -> p (a b)")))
                dve.tensor_scalar(lns[0:m, 0, t:t + 1], mv[0:m, t, 1:2], EPS, None, ALU.add).then_inc(ln_var, 1)

            def ln_scale(call, t):
                m = ROWS[t]
                dve.wait_ge(ln_std, TILES * call + t + 1)
                link(dve.reciprocal(lns[0:m, 2, t:t + 1], lns[0:m, 1, t:t + 1]))
                dve.scalar_tensor_tensor(out=lns[0:m, 3, t:t + 1], in0=mv[0:m, t, 0:1], scalar=-1.0,
                                         in1=lns[0:m, 2, t:t + 1], op0=ALU.mult, op1=ALU.mult).then_inc(ln_rs, 1)

            def ln_shift(call, t, src):
                m = ROWS[t]
                dve.wait_ge(ln_gain, TILES * call + t + 1)
                shift = gb[0:m, D:2 * D] if call else x[0:m, 1]
                dve.tensor_tensor(src[0:m, t], src[0:m, t], shift, ALU.add).then_inc(ln_out, 1)

            def ln_tiles(call, produce, t0):
                for i in range(TILES + 3):
                    if i < TILES:
                        produce(i)
                        ln_stats(call, i, x)
                    if 0 <= i - 2 < TILES:
                        ln_shift(call, i - 2, x)
                    if i < TILES:
                        ln_scale(call, i)
                    if i >= 3 and t0 is not None:
                        turn_low(t0 + 2 * (i - 3))

            def residual(m_step, t, cb):
                m = ROWS[t]
                dve.wait_ge(proj_done, m_step + 1)
                w = x[0:m, t, cb * HALF:(cb + 1) * HALF]
                dve.scalar_tensor_tensor(out=w, in0=w, scalar=ALPHA, in1=ps[0:m, m_step % PROJ_BANKS],
                                         op0=ALU.mult, op1=ALU.add).then_inc(proj_free, 1)

            dve.memset(wsm[:], 0.0).then_inc(wsm_zeroed, 1)
            dve.wait_ge(con_in, 32)
            dve.tensor_copy(idmask[:, 0], ident)
            dve.tensor_copy(idmask[:, 1], con[:, C_CAUSAL:C_CAUSAL + P]).then_inc(idmask_ready, 1)
            for half in range(2):
                dve.wait_ge(x0_high, half + 1)
                w = (slice(None), slice(4 * half, 4 * half + 4))
                dve.tensor_tensor(xTl[w], xT0[w], xTh[w].bitcast(F32), ALU.subtract).then_inc(x0_low, 1)
            split_a(0)
            split_a(1)
            dve.wait_ge(rw_high, 1)
            dve.tensor_tensor(rwl, rw_raw[:], rwh.bitcast(F32), ALU.subtract).then_inc(rw_low, 1)
            dve.wait_ge(rw_low, 1)
            dve.wait_ge(gb_in, 16)
            for j in range(4):
                split_a(2 * j + 2)
                split_a(2 * j + 3)
                if j == 2:
                    for t in range(TILES):
                        dve.wait_ge(gelu_done, TILES + t + 1)
                        ln_stats(0, t, v)
                        ln_scale(0, t)
                if j == 3:
                    for t in range(TILES):
                        ln_shift(0, t, v)
                    dve.wait_ge(mixc_in, 48)
                    dve.wait_ge(raw_a[A_WS % RAW_SLOTS], landed_a(A_WS))
                    w = raw[:, A_WS % RAW_SLOTS, 0:2].rearrange("p a (g t) -> p (a g) t", t=P)
                    dve.tensor_tensor(w, w, cmix[:, 0:P].unsqueeze(1).broadcast_to([P, HEADS, P]), ALU.mult
                                      ).then_inc(ws_masked, 1)
                    dve.wait_ge(wsm_in, 16 * DEC_B)
                    dve.tensor_tensor(wsm[:], wsm[:],
                                      cmix[0:NSAMP, P:P + NSAMP].unsqueeze(1).broadcast_to([NSAMP, HEADS, NSAMP]),
                                      ALU.mult).then_inc(ws_masked, 1)
                dst, cols = (v if j < 2 else u), j % 2 * HALF
                for t in range(TILES):
                    m, step = ROWS[t], M_WIN + 5 * j + t
                    dve.wait_ge(proj_done, step + 1)
                    bias = gb[0:m, WIN_COLS[j] * HALF:(WIN_COLS[j] + 1) * HALF]
                    dve.tensor_tensor(dst[0:m, t, cols:cols + HALF], ps[0:m, step % PROJ_BANKS], bias, ALU.add
                                      ).then_inc(proj_free, 1)
            dve.wait_ge(gelu_done, 4 * TILES)
            for g in range(HEADS):
                step = M_MIX + g
                w = u[:, 0:4, g * P:(g + 1) * P]
                dve.wait_ge(proj_done, step + 1)
                dve.scalar_tensor_tensor(out=w, in0=ps[:, step % PROJ_BANKS].rearrange("p (c n) -> p c n", c=4),
                                         scalar=bsp[:, g:g + 1], in1=w, op0=ALU.add, op1=ALU.mult
                                         ).then_inc(proj_free, 1)
            for half in range(2):
                step = M_MIX + 8 + half
                dve.wait_ge(proj_done, step + 1)
                for j in range(4):
                    g = 4 * half + j
                    w = u[0:NSAMP, 4, g * P:(g + 1) * P]
                    ins = dve.scalar_tensor_tensor(out=w, in0=ps[0:NSAMP, step % PROJ_BANKS, j * P:(j + 1) * P],
                                                   scalar=bss[:, g:g + 1], in1=w, op0=ALU.add, op1=ALU.mult)
                ins.then_inc(proj_free, 1)
            for t in range(TILES):
                turn_low(T_US + 2 * t)
            split_a(10)
            dve.wait_ge(x_in, 16 * TILES)
            for t in range(TILES):
                if t == TILES - 1:
                    split_a(11)
                residual(M_WOUT + t, t, 0)

            def second_half(m0):
                def produce(t):
                    residual(m0 + t, t, 1)
                    dve.wait_ge(proj_free, m0 + t + 1)
                return produce
            ln_tiles(1, second_half(M_WOUT + 5), T_LN1A)

            def route(l, m0):
                def first_max(out, val, mx, rank, n, work):
                    shape = [P, TILES, n]
                    link(dve.tensor_tensor(work, val, mx.unsqueeze(2).broadcast_to(shape), ALU.is_equal))
                    link(dve.tensor_tensor(work, work, rank.unsqueeze(1).broadcast_to(shape), ALU.mult))
                    link(dve.tensor_reduce(col[:, 11, 0], work, AX, ALU.max))
                    link(dve.tensor_tensor(out, work, col[:, 11, 0].unsqueeze(2).broadcast_to(shape), ALU.is_equal))

                full = [P, TILES, EXPERTS]
                bank = m0 % PROJ_BANKS
                link(dve.memset(lg[:], 0.0))
                dve.wait_ge(proj_done, m0 + 1)
                dve.wait_ge(rb_in, 16)
                parts = ps[:, bank, 0:2 * TILES * EXPERTS].rearrange("p (t a e) -> p t a e", a=2, e=EXPERTS)
                dve.tensor_copy(lg[:, 0:4], parts[:, 0:4, 0])
                link(dve.tensor_copy(lg[0:NSAMP, 4], parts[0:NSAMP, 4, 0]))
                dve.tensor_tensor(lg[:, 0:4], lg[:, 0:4], parts[:, 0:4, 1], ALU.add)
                link(dve.tensor_tensor(lg[0:NSAMP, 4], lg[0:NSAMP, 4], parts[0:NSAMP, 4, 1], ALU.add))
                dve.sem_inc(proj_free, 1)
                link(dve.tensor_reduce(col[:, 0, 0], lg[:], AX, ALU.max))
                dve.tensor_tensor(lg[:], lg[:], col[:, 0, 0].unsqueeze(2).broadcast_to(full), ALU.subtract
                                  ).then_inc(logit_max, 1)
                dve.wait_ge(exp_r, l + 1)
                link(dve.tensor_reduce(col[:, 1, 0], prob[:], AX, ALU.add))
                link(dve.reciprocal(col[:, 2, 0], col[:, 1, 0]))
                link(dve.tensor_tensor(prob[:], prob[:], col[:, 2, 0].unsqueeze(2).broadcast_to(full), ALU.mult))
                link(dve.tensor_tensor(sel[:], prob[:], rbias[:].unsqueeze(1).broadcast_to(full), ALU.add))
                s4 = sel[:].rearrange("p t (g e) -> p (t g) e", e=PER_GROUP)
                dve.tensor_tensor(hilo[:, 0], s4[:, :, 0::2], s4[:, :, 1::2], ALU.max)
                link(dve.tensor_tensor(hilo[:, 1], s4[:, :, 0::2], s4[:, :, 1::2], ALU.min))
                gv = [gsc[:, j].rearrange("p t g -> p (t g)") for j in range(4)]
                dve.tensor_tensor(gv[0], hilo[:, 0, :, 0], hilo[:, 0, :, 1], ALU.max)
                dve.tensor_tensor(gv[1], hilo[:, 0, :, 0], hilo[:, 0, :, 1], ALU.min)
                link(dve.tensor_tensor(gv[2], hilo[:, 1, :, 0], hilo[:, 1, :, 1], ALU.max))
                link(dve.tensor_tensor(gv[1], gv[1], gv[2], ALU.max))
                link(dve.tensor_tensor(gv[0], gv[0], gv[1], ALU.add))
                link(dve.tensor_reduce(col[:, 3, 0], gsc[:, 0], AX, ALU.max))
                first_max(gsc[:, 3], gsc[:, 0], col[:, 3, 0], con[:, C_RK4:C_RK4 + 4], GROUPS, gsc[:, 2])
                link(dve.tensor_scalar(gsc[:, 1], gsc[:, 3], 1.0, -NEG, ALU.subtract, ALU.mult))
                four = [P, TILES * GROUPS, PER_GROUP]
                g3 = gsc[:, 3].rearrange("p t g -> p (t g)").unsqueeze(2).broadcast_to(four)
                g1 = gsc[:, 1].rearrange("p t g -> p (t g)").unsqueeze(2).broadcast_to(four)
                link(dve.tensor_tensor(s4, s4, g3, ALU.mult))
                link(dve.tensor_tensor(s4, s4, g1, ALU.add))
                link(dve.tensor_reduce(col[:, 4, 0], sel[:], AX, ALU.max))
                rk16 = con[:, C_RK16:C_RK16 + 16]
                first_max(oh[:, 0], sel[:], col[:, 4, 0], rk16, EXPERTS, tmp[:, 0])
                link(dve.scalar_tensor_tensor(out=sel[:], in0=oh[:, 0], scalar=3 * NEG, in1=sel[:],
                                              op0=ALU.mult, op1=ALU.add))
                link(dve.tensor_reduce(col[:, 5, 0], sel[:], AX, ALU.max))
                first_max(oh[:, 1], sel[:], col[:, 5, 0], rk16, EXPERTS, tmp[:, 0])
                both = [P, 2, TILES, EXPERTS]
                link(dve.tensor_tensor(oh[:], oh[:], con[:, C_VALID:C_VALID + TILES].unsqueeze(1).unsqueeze(3)
                                       .broadcast_to(both), ALU.mult))
                dve.tensor_tensor(m16[:], oh[:, 0], oh[:, 1], ALU.add).then_inc(masks, 1)
                dve.wait_ge(proj_done, m0 + 2)
                bank = (m0 + 1) % PROJ_BANKS
                rank = ps[:, bank, 0:TILES * EXPERTS].rearrange("p (t e) -> p t e", e=EXPERTS)
                e_of = con[:, C_IOTA16:C_IOTA16 + 16].unsqueeze(1).unsqueeze(1)
                dve.tensor_copy(cnt[:, 0], ps[:, bank, TILES * EXPERTS:(TILES + 1) * EXPERTS])
                link(dve.tensor_tensor(tmp[:], oh[:], rank.unsqueeze(1).broadcast_to(both), ALU.mult))
                dve.sem_inc(proj_free, 1)
                c_thr = con[:, C_THR:C_THR + 4]
                dve.tensor_tensor(thr[:, :, 0:4], cnt[:, 0].unsqueeze(2).broadcast_to([P, EXPERTS, 4]),
                                  c_thr.unsqueeze(1).broadcast_to([P, EXPERTS, 4]), ALU.is_gt)
                link(dve.tensor_reduce(col[:, 0], tmp[:], AX, ALU.add))
                dve.tensor_reduce(cnt[:, 1], thr[:, :, 0:4], AX, ALU.add)
                link(dve.tensor_tensor(tmp[:], oh[:], e_of.broadcast_to(both), ALU.mult))
                dve.tensor_copy(cnt[:, 2], cnt[:, 1])
                dve.tensor_scalar(col[:, 3], col[:, 0], 1.0 * P, None, ALU.is_ge)
                link(dve.tensor_reduce(col[:, 2], tmp[:], AX, ALU.add))
                a_, b_ = 2, 3
                for j, sh in enumerate((1, 2, 4, 8)):
                    dve.tensor_copy(cnt[:, b_, 0:sh], cnt[:, a_, 0:sh])
                    if j < 3:
                        dve.scalar_tensor_tensor(out=col[:, 3], in0=col[:, 0], scalar=1.0 * P * (j + 2), in1=col[:, 3],
                                                 op0=ALU.is_ge, op1=ALU.add)
                    else:
                        dve.scalar_tensor_tensor(out=col[:, 4], in0=col[:, 3], scalar=-1.0 * P, in1=col[:, 0],
                                                 op0=ALU.mult, op1=ALU.add)
                    link(dve.tensor_tensor(cnt[:, b_, sh:16], cnt[:, a_, sh:16], cnt[:, a_, 0:16 - sh], ALU.add))
                    a_, b_ = b_, a_
                incl = cnt[:, a_]
                link(dve.tensor_tensor(cnt[:, 4], incl, cnt[:, 1], ALU.subtract))
                link(dve.tensor_tensor(tmp[:], oh[:], cnt[:, 4].unsqueeze(1).unsqueeze(1).broadcast_to(both), ALU.mult))
                link(dve.tensor_reduce(col[:, 1], tmp[:], AX, ALU.add))
                link(dve.tensor_tensor(col[:, 5], col[:, 1], col[:, 3], ALU.add))
                link(dve.scalar_tensor_tensor(out=col[:, 5], in0=col[:, 5], scalar=EXPERTS - 1.0, in1=col[:, 2],
                                              op0=ALU.add, op1=ALU.subtract))
                link(dve.scalar_tensor_tensor(out=col[:, 5], in0=col[:, 3], scalar=0.0, in1=col[:, 5],
                                              op0=ALU.is_gt, op1=ALU.mult))
                link(dve.tensor_tensor(col[:, 5], col[:, 5], col[:, 2], ALU.add))
                iota = con[:, C_IOTA:C_IOTA + P]
                pairs = 2 * TILES
                slot_of = col[:, 4].rearrange("p k t -> p (k t)").unsqueeze(2)
                block_of = col[:, 5].rearrange("p k t -> p (k t)").unsqueeze(2)
                dve.tensor_tensor(lo16[:], iota.unsqueeze(1).broadcast_to([P, pairs, P]),
                                  slot_of.broadcast_to([P, pairs, P]), ALU.is_equal)
                hi_shape = [P, pairs, LIST_COLS]
                link(dve.tensor_tensor(hi16[:, :, 0:LIST_COLS], iota[:, 0:LIST_COLS].unsqueeze(1).broadcast_to(hi_shape),
                                       block_of.broadcast_to(hi_shape), ALU.is_equal))
                dve.tensor_tensor(hi16[:, :, 0:LIST_COLS], hi16[:, :, 0:LIST_COLS],
                                  con[:, C_ID1:C_ID1 + pairs].unsqueeze(2).broadcast_to(hi_shape), ALU.mult
                                  ).then_inc(onehots, 1)
                link(dve.tensor_tensor(thr[:, 0:8], incl.unsqueeze(1).broadcast_to([P, 8, EXPERTS]),
                                       con[:, C_IOTA8:C_IOTA8 + 8].unsqueeze(2).broadcast_to([P, 8, EXPERTS]),
                                       ALU.is_le))
                link(dve.tensor_copy(tblf[:, 0:EXPERTS], con[:, C_IOTA16:C_IOTA16 + 16]))
                link(dve.tensor_reduce(tblf[:, EXPERTS:MAX_BLOCKS], thr[:, 0:8], AX, ALU.add))
                link(dve.tensor_scalar(tblf[:, 0:MAX_BLOCKS], tblf[:, 0:MAX_BLOCKS], EXPERTS - 1.0, None, ALU.min))
                link(dve.tensor_copy(tblf[:, MAX_BLOCKS:LIST_COLS], incl[:, 15:16]))
                dve.tensor_copy(table[:], tblf[:])
                dve.wait_ge(proj_done, m0 + 3)
                val = ps[:, (m0 + 2) % PROJ_BANKS, 0:LIST_COLS]
                link(dve.tensor_scalar(lst[:, 0], val, 0.0, NO_ROW, ALU.is_equal, ALU.mult))
                link(dve.tensor_scalar(lst[:, 1], val, 1.0, None, ALU.subtract))
                dve.sem_inc(proj_free, 1)
                link(dve.tensor_tensor(lst[:, 0], lst[:, 0], lst[:, 1], ALU.add))
                dve.tensor_copy(sidx[:], lst[:, 0])
                link(dve.tensor_scalar(lst[:, 2], lst[:, 0], 1.0 * NTOK, -1.0 * NTOK, ALU.is_ge, ALU.mult))
                link(dve.tensor_tensor(lst[:, 1], lst[:, 0], lst[:, 2], ALU.add))
                link(dve.tensor_copy(gidx[:], lst[:, 1]))
                dve.sem_inc(plan, 1)
                link(dve.tensor_tensor(tmp[:], oh[:], prob[:].unsqueeze(1).broadcast_to(both), ALU.mult))
                link(dve.tensor_reduce(gates[:], tmp[:], AX, ALU.add))
                link(dve.tensor_tensor(col[:, 6, 0], gates[:, 0], gates[:, 1], ALU.add))
                link(dve.tensor_tensor(col[:, 6, 0], col[:, 6, 0], con[:, C_BEYOND:C_BEYOND + TILES], ALU.add))
                link(dve.reciprocal(col[:, 6, 1], col[:, 6, 0]))
                link(dve.tensor_tensor(gates[:], gates[:], col[:, 6, 1].unsqueeze(1).broadcast_to([P, 2, TILES]),
                                       ALU.mult))

            def moe_dve(l, m0):
                s, key = moe[l], f"m{l}"

                def split(n, slot, q, i):
                    if isinstance(i, int) and i == 1 and q < 5:
                        split_low(key, n, slot, (ahead_up[q] if q < 4 else ahead_down)[:])
                    else:
                        split_low(key, n, slot, raw[:, q])

                split(0, 0, 0, 0)
                split(1, 1, 1, 0)
                route(l, m0)
                split(2, 2, 2, 0)

                def xg_low(i):
                    dve.wait_ge(s["xg_high"], i + 1)
                    dve.tensor_tensor(xgTl[:], ps[:, 2:4].rearrange("p a (k m) -> p (a k) m", m=P),
                                      xgTh[:].bitcast(F32), ALU.subtract).then_inc(s["xg_low"], 1)

                def gate_up(i):
                    dve.wait_ge(s["silu"], i + 1)
                    after(dve, s["h_tr"], i)
                    dve.tensor_tensor(hb[:], sg[:], ps[:, 1], ALU.mult).then_inc(s["h_ready"], 1)

                def h_low(i):
                    dve.wait_ge(s["h_high"], i + 1)
                    dve.tensor_tensor(hTl[:], ps[:, 6].rearrange("p (k m) -> p k m", k=4), hTh[:].bitcast(F32),
                                      ALU.subtract).then_inc(s["h_low"], 1)

                def body(i, first=False):
                    if not first:
                        split(6 * i - 2, 1, 0, i)
                        split(6 * i - 1, 2, 1, i)
                    h_low(i - 1)
                    for q in range(2, 4):
                        split(6 * i - 2 + q, (q + 1) % 3, q, i)
                    for r in range(2):
                        split(6 * i + 2 + r, (r + 5) % 3, 4 + r, i - 1)
                    gate_up(i)
                    xg_low(i + 1)

                xg_low(0)
                split(3, 0, 3, 0)
                split(4, 1, 0, 1)
                split(5, 2, 1, 1)
                gate_up(0)
                xg_low(1)
                blocks = dve.value_load(table[0:1, LIST_COLS - 1:LIST_COLS], min_val=0, max_val=MAX_BLOCKS - EXPERTS) + EXPERTS
                body(1, True)
                body(2)
                with dve.Fori(3, blocks) as i:
                    body(i)
                for r in range(2):
                    split(6 * blocks - 2 + r, r + 1, 4 + r, blocks - 1)
                h_low(blocks - 1)

            def add_experts(l):
                s = moe[l]

                def produce(t):
                    m = ROWS[t]
                    dve.wait_ge(s["scaled"], t + 1)
                    dve.wait_ge(y_in[t], 16 * (l + 1))
                    for k in range(2):
                        link(dve.scalar_tensor_tensor(out=x[0:m, t], in0=yl[0:m, t, k], scalar=gates[0:m, k, t:t + 1],
                                                      in1=x[0:m, t], op0=ALU.mult, op1=ALU.add))
                return produce

            moe_dve(0, M_ROUTE_A)
            for n in range(3):
                split_b(n)
            ln_tiles(2, add_experts(0), T_LN2A)

            for j in range(6):
                if 0 < j < 5:
                    split_b(2 * j + 2)
                if j < 5:
                    split_b(2 * j + 3)
                for t in range(TILES):
                    m, step = ROWS[t], M_QKV + 5 * j + t
                    if j in (2, 3):
                        dve.wait_ge(park_out, 16 * TILES)
                        dst = x[0:m, t, (j - 2) * HALF:(j - 1) * HALF]
                    else:
                        kk = (5 * j if j < 2 else 10 + 5 * (j - 4)) + t
                        after(dve, kq_tr, kk - 4)
                        if 5 <= kk < 15:
                            dve.wait_ge(stg_out[t], 16 * (kk // 5))
                        dst = stg[0:m, t]
                    dve.wait_ge(proj_done, step + 1)
                    dve.tensor_copy(dst, ps[0:m, step % PROJ_BANKS]).then_inc(proj_free, 1)

            dve.wait_ge(lam_in, 16 * 5)
            dve.wait_ge(used["b"], B_CACHE)
            dve.wait_ge(kq_tr, 20)
            lq = gb[:, 0:4 * HEAD_DIM].rearrange("p (a b d) -> p a b d", a=2, b=2)
            link(dve.tensor_tensor(lamp[:], lq[:, :, 0], lq[:, :, 1], ALU.mult))
            dve.tensor_reduce(lamc[:, 0:2], lamp[:], AX, ALU.add).then_inc(lam_sum, 1)
            dve.wait_ge(lam_exp, 1)
            link(dve.tensor_tensor(lamc[:, 4:5], lamc[:, 3:4], lamc[:, 2:3], ALU.subtract))
            link(dve.tensor_scalar(lamc[:, 5:6], lamc[:, 4:5], LAM_INIT, None, ALU.subtract))
            link(dve.tensor_tensor(lamc[:, 6:7], con[:, C_COEF + 1:C_COEF + 2], lamc[:, 5:6], ALU.mult))
            link(dve.tensor_tensor(lamc[:, 7:8], lamc[:, 6:7], con[:, C_COEF:C_COEF + 1], ALU.add))
            link(dve.memset(oss[:], 1.0))
            neg_lam, coef = lamc[:, 5:6], lamc[:, 7:8]

            def att_max(n, part):
                w = (n // HEADS + 1) * P
                dve.wait_ge(at_s, 2 * n + part + 1)
                dve.tensor_reduce(mxs[:, 1, n % 2, part:part + 1], ps[:, part, 0:w], AX, ALU.max, negate=True
                                  ).then_inc(at_max, 1)

            def att_p(n):
                w = (n // HEADS + 1) * P
                dve.wait_ge(at_exp, 2 * n + 2)
                after(dve, at_o, n - 1)
                link(dve.reciprocal(mxs[:, 3, n % 2], mxs[:, 2, n % 2]))
                link(dve.tensor_scalar(mxs[:, 0, n % 2, 0:1], mxs[:, 2, n % 2, 0:1], mxs[:, 3, n % 2, 1:2], neg_lam,
                                       ALU.mult, ALU.mult))
                after(dve, at_pt, n - 1)
                dve.scalar_tensor_tensor(out=Pm[:, n % 2, 0:w], in0=E[:, n % 2, 1, 0:w],
                                         scalar=mxs[:, 0, n % 2, 0:1], in1=E[:, n % 2, 0, 0:w],
                                         op0=ALU.mult, op1=ALU.add).then_inc(at_p, 1)

            def queries(g):
                after(dve, sm_s, 2 * g)
                for b2 in range(2):
                    b = 2 * g + b2
                    for part in range(2):
                        r = slice(64 * part, 64 * part + 64)
                        wide = qpad[r, b2 * 1088:(b2 + 1) * 1088].rearrange("p (h c) -> p h c", c=136)
                        ins = dve.tensor_copy(wide[:, :, 4 * part:4 * part + 4],
                                              QT[r, :, SEQ + b * DEC_T:SEQ + (b + 1) * DEC_T])
                ins.then_inc(sm_q, 1)

            def sample_max(g):
                dve.wait_ge(sm_s, 2 * g + 2)
                new = ps[:, 5, 256:288]
                link(dve.tensor_tensor(new, new, con[:, C_SMASK + 32 * g:C_SMASK + 32 * g + 32], ALU.add))
                dve.tensor_reduce(smx[:, 1:2], ps[:, 5, 0:288], AX, ALU.max, negate=True).then_inc(sm_max, 1)

            def sample_p(g):
                dve.wait_ge(sm_exp, g + 1)
                link(dve.reciprocal(smx[:, 3:4], smx[:, 2:3]))
                dve.tensor_scalar(Ps[:], Es[:], smx[:, 3:4], coef, ALU.mult, ALU.mult).then_inc(sm_p, 1)

            def sample_columns(g):
                dve.wait_ge(sm_zero, g + 1)
                dve.wait_ge(sm_pt, g + 1)
                for half in range(2):
                    for b2 in range(2):
                        c0 = (2 * g + b2) * DEC_T
                        for page in range(3):
                            m, dst = (P, ptz[:, page, b2]) if page < 2 else (NSAMP, ptn[:])
                            rows = ps[0:m, 5, page * P + b2 * 64:page * P + b2 * 64 + 64].rearrange(
                                "p (h a q) -> p h a q", a=2, q=DEC_T)
                            mine = dst[:, :, c0:c0 + DEC_T]
                            if half == 0:
                                ins = dve.tensor_copy(mine, rows[:, :, 0])
                            else:
                                ins = dve.tensor_tensor(mine, mine, rows[:, :, 1], ALU.add)
                    if half == 0:
                        link(ins)
                ins.then_inc(sm_ptz, 1)

            def squares(t):
                m = ROWS[t]
                link(dve.tensor_tensor(osq[0:m], o[t][0:m], o[t][0:m], ALU.mult))
                link(dve.tensor_reduce(oss[0:m, 2, t], osq[0:m].rearrange("p (h e) -> p h e", e=P), AX, ALU.add))

            link(dve.memset(qpad[:], 0.0))
            steps = 4 * HEADS
            for n in range(steps + 1):
                g, j = n // 8, n % 8
                if n < steps:
                    att_max(n, 0)
                if n:
                    att_p(n - 1)
                if n < steps:
                    att_max(n, 1)
                if n == steps:
                    break
                if j == 0:
                    queries(g)
                    if g:
                        sample_columns(g - 1)
                if j == 3 and g:
                    dve.wait_ge(at_o, 8 * g)
                    squares(g - 1)
                if j == 6:
                    sample_max(g)
                if j == 7:
                    sample_p(g)
            sample_columns(3)

            def head_var(tiles):
                dve.tensor_scalar(oss[:, 0, tiles], oss[:, 2, tiles], 1.0 / P, EPS, ALU.mult, ALU.add
                                  ).then_inc(om_var, 1)

            def head_norm(part, tiles):
                dve.wait_ge(om_std, part)
                link(dve.reciprocal(oss[:, 2, tiles], oss[:, 1, tiles]))
                link(dve.tensor_scalar(oss[:, 2, tiles], oss[:, 2, tiles], 1.0 - LAM_INIT, None, ALU.mult))
                for t in range(TILES)[tiles]:
                    m = ROWS[t]
                    ot = o[t][0:m].rearrange("p (h e) -> p h e", e=P)
                    dve.tensor_tensor(ot, ot, oss[0:m, 2, t].unsqueeze(2).broadcast_to([m, HEADS, P]), ALU.mult
                                      ).then_inc(om_r, 1)
            dve.wait_ge(at_o, steps)
            squares(3)
            head_var(slice(0, 4))
            dve.wait_ge(at_pv, steps)
            split_b(12)
            head_norm(1, slice(0, 4))
            split_b(13)
            turn_low(T_O, subg)
            turn_low(T_O + 2, subg)
            dve.wait_ge(sm_o, 1)
            squares(4)
            head_var(slice(4, 5))
            head_norm(2, slice(4, 5))
            for t in range(2, TILES):
                turn_low(T_O + 2 * t, subg)
            split_b(14)
            dve.wait_ge(park_in, 16 * TILES)
            for t in range(TILES):
                if t == TILES - 1:
                    split_b(15)
                residual(M_WO + t, t, 0)
            ln_tiles(3, second_half(M_WO + 5), T_LN1B)
            moe_dve(1, M_ROUTE_B)
            ln_tiles(4, add_experts(1), None)

        @block.tensor
        def _(pe):
            def three(out, high_, low_, w_high, w_low, start, stop):
                pe.matmul(out, high_, w_high, start=start, stop=False)
                pe.matmul(out, high_, w_low, start=False, stop=False)
                return pe.matmul(out, low_, w_high, start=False, stop=stop)

            def bank_for(step):
                after(pe, proj_free, step - PROJ_BANKS + 1)
                return step % PROJ_BANKS

            def project(key, s0, m0, between=None):
                for kh in range(2):
                    s = s0 + kh
                    pe.wait_ge(low[key], s + 1)
                    for t in range(TILES):
                        bank = (m0 + t) % PROJ_BANKS
                        if kh == 0:
                            bank_for(m0 + t)
                        tok = slice(t * P, t * P + ROWS[t])
                        for j in range(4):
                            k = 4 * kh + j
                            mm = three(ps[0:ROWS[t], bank], xTh[:, k, tok], xTl[:, k, tok],
                                       wh[:, s % SPLIT_SLOTS, j], wl[:, s % SPLIT_SLOTS, j],
                                       start=(k == 0), stop=(k == KT_D - 1))
                            if k == KT_D - 1 and t < TILES - 1:
                                mm.then_inc(proj_done, 1)
                        if kh == 0 and between:
                            between(t)
                    if kh == 0:
                        mm.then_inc(used[key], 1)
                    else:
                        mm.then_inc(proj_done, 1)
                        pe.wait_ge(proj_done, m0 + TILES)
                        pe.sem_inc(used[key], 1)

            def turn(t, n0, src):
                m = ROWS[t]
                for half in range(2):
                    n = n0 + 2 * t + half
                    after(pe, tr_low, n - 1)
                    for j in range(4):
                        k = 4 * half + j
                        mm = pe.transpose(ps[:, 6 + n % 2, j * P:j * P + m], src[0:m, k * P:(k + 1) * P],
                                          ident[0:m, 0:m])
                    mm.then_inc(tr_done, 1)

            def project_by_tile(key, s0, m0, turned=None, prepare=None):
                for i in range(TILES + 1):
                    if i < TILES and prepare:
                        prepare(i)
                    if i == 0:
                        continue
                    t = i - 1
                    if prepare:
                        pe.wait_ge(tr_low, turned + 2 * t + 2)
                    bank = bank_for(m0 + t)
                    tok = slice(t * P, t * P + ROWS[t])
                    for kh in range(2):
                        s = s0 + kh
                        if t == 0:
                            pe.wait_ge(low[key], s + 1)
                        for j in range(4):
                            k = 4 * kh + j
                            mm = three(ps[0:ROWS[t], bank], xTh[:, k, tok], xTl[:, k, tok],
                                       wh[:, s % SPLIT_SLOTS, j], wl[:, s % SPLIT_SLOTS, j],
                                       start=(k == 0), stop=(k == KT_D - 1))
                        if kh == 0 and t == TILES - 1:
                            mm.then_inc(used[key], 1)
                    mm.then_inc(proj_done, 1)
                pe.wait_ge(proj_done, m0 + TILES)
                pe.sem_inc(used[key], 1)

            pe.wait_ge(con_in, 32)
            pe.wait_ge(x0_low, 2)
            for j in range(4):
                project("a", 2 * j, M_WIN + 5 * j)
            pe.wait_ge(ln_out, TILES)
            pe.wait_ge(ws_masked, 2)
            ws = raw[:, A_WS % RAW_SLOTS, 0:2].rearrange("p a (g t) -> p (a g) t", t=P)
            for g in range(HEADS):
                bank = bank_for(M_MIX + g)
                mm = pe.matmul(ps[:, bank].rearrange("p (c n) -> p c n", c=4), ws[:, g], v[:, 0:4, g * P:(g + 1) * P],
                               start=True, stop=True)
                mm.then_inc(proj_done, 1)
            for half in range(2):
                bank = bank_for(M_MIX + 8 + half)
                for j in range(4):
                    g = 4 * half + j
                    mm = pe.matmul(ps[0:NSAMP, bank, j * P:(j + 1) * P], wsm[:, g], v[0:NSAMP, 4, g * P:(g + 1) * P],
                                   start=True, stop=True)
                mm.then_inc(proj_done, 1)
            pe.wait_ge(proj_done, M_MIX + 8)
            pe.sem_inc(mix_done, 1)
            pe.wait_ge(proj_free, M_MIX + 10)
            project_by_tile("a", 8, M_WOUT, T_US, lambda t: turn(t, T_US, u[:, t]))
            project_by_tile("a", 10, M_WOUT + 5)

            def route(l, m0, t0, call):
                pe.wait_ge(rw_low, 1)
                bank = bank_for(m0)
                for t in range(TILES + 1):
                    if t < TILES:
                        pe.wait_ge(ln_out, TILES * call + t + 1)
                        turn(t, t0, x[:, t])
                    if t:
                        b = t - 1
                        tok = slice(b * P, b * P + ROWS[b])
                        pe.wait_ge(tr_low, t0 + 2 * t)
                        for k in range(KT_D):
                            pe.matmul(ps[0:ROWS[b], bank, b * 2 * EXPERTS:(b + 1) * 2 * EXPERTS], xTh[:, k, tok],
                                      rwhl[:, k].rearrange("p a e -> p (a e)"), start=(k == 0), stop=False,
                                      skip_group_check=True)
                            mm = pe.matmul(ps[0:ROWS[b], bank, b * 2 * EXPERTS:(b * 2 + 1) * EXPERTS], xTl[:, k, tok],
                                           rwh[:, k], start=False, stop=(k == KT_D - 1), skip_group_check=True)
                mm.then_inc(proj_done, 1)
                before, ones = con16[:, 0:P], con16[:, P:2 * P]
                bank = bank_for(m0 + 1)
                pe.wait_ge(masks, l + 1)
                for t in range(TILES + 1):
                    for b in range(min(t + 1, TILES)):
                        mm = pe.matmul(ps[:, bank, t * EXPERTS:(t + 1) * EXPERTS], before if b == t else ones, m16[:, b],
                                       start=(b == 0), stop=(b == min(t, TILES - 1)))
                mm.then_inc(proj_done, 1)
                bank = bank_for(m0 + 2)
                pe.wait_ge(onehots, l + 1)
                for n in range(2 * TILES):
                    mm = pe.matmul(ps[:, bank, 0:LIST_COLS], lo16[:, n], hi16[:, n, 0:LIST_COLS],
                                   start=(n == 0), stop=(n == 2 * TILES - 1))
                mm.then_inc(proj_done, 1)

            def moe_pe(l, m_end):
                s, key = moe[l], f"m{l}"
                pe.wait_ge(proj_free, m_end)

                def up(i, n0):
                    pe.wait_ge(s["xg_low"], i + 1)
                    after(pe, s["h_ready"], i)
                    for q in range(4):
                        slot = (q + 1) % 3 if n0 else q % 3
                        pe.wait_ge(low[key], (6 * i - 2 + q if n0 else q) + 1)
                        for j in range(4):
                            k = 4 * (q % 2) + j
                            mm = three(ps[:, q // 2], xgTh[:, k], xgTl[:, k], wh[:, slot, j], wl[:, slot, j],
                                       start=(k == 0), stop=(k == KT_D - 1))
                        mm.then_inc(used[key], 1)

                def turn_x(i):
                    pe.wait_ge(s["gathered"], 16 * (i + 1))
                    after(pe, s["xg_low"], i)
                    for k in range(KT_D):
                        mm = pe.transpose(ps[:, 2 + k // 4, k % 4 * P:(k % 4 + 1) * P], xg[:, k * P:(k + 1) * P], ident)
                    mm.then_inc(s["xg_tr"], 1)

                def turn_h(i):
                    pe.wait_ge(s["h_ready"], i + 1)
                    after(pe, s["h_low"], i)
                    for k in range(4):
                        mm = pe.transpose(ps[:, 6, k * P:(k + 1) * P], hb[:, k * P:(k + 1) * P], ident)
                    mm.then_inc(s["h_tr"], 1)

                def down(i, n, slots):
                    pe.wait_ge(s["h_low"], i + 1)
                    after(pe, s["y_ready"], i)
                    for r in range(2):
                        pe.wait_ge(low[key], n + r + 1)
                        for j in range(4):
                            mm = three(ps[:, 4 + r], hTh[:, j], hTl[:, j], wh[:, slots[r], j], wl[:, slots[r], j],
                                       start=(j == 0), stop=(j == 3))
                        mm.then_inc(used[key], 1)

                turn_x(0)
                up(0, 0)
                turn_x(1)
                turn_h(0)
                pe.wait_ge(plan, l + 1)
                blocks = pe.value_load(table[0:1, LIST_COLS - 1:LIST_COLS], min_val=0, max_val=MAX_BLOCKS - EXPERTS) + EXPERTS

                def body(i):
                    up(i, 1)
                    turn_x(i + 1)
                    down(i - 1, 6 * i + 2, (2, 0))
                    turn_h(i)
                body(1)
                with pe.Fori(2, blocks) as i:
                    body(i)
                down(blocks - 1, 6 * blocks - 2, (1, 2))
                return blocks

            route(0, M_ROUTE_A, T_LN1A, 1)
            blocks = moe_pe(0, M_QKV)
            pe.wait_ge(moe[0]["y_ready"], blocks)

            def turn_x_a(t):
                pe.wait_ge(ln_out, 2 * TILES + t + 1)
                turn(t, T_LN2A, x[:, t])
            project_by_tile("b", 0, M_QKV, T_LN2A, turn_x_a)

            def turn_kq(kk, step):
                m = ROWS[kk % 5]
                pe.wait_ge(proj_free, step + 1)
                after(pe, kq_copied, kk - 1)
                for j in range(4):
                    mm = pe.transpose(ps[:, 6 + kk % 2, j * P:j * P + m], stg[0:m, kk % 5, j * P:(j + 1) * P],
                                      ident[0:m, 0:m])
                mm.then_inc(kq_tr, 1)
            for j in range(1, 6):
                between = None
                if j in (1, 2, 5):
                    kk0 = 5 * (j - 1) if j < 5 else 10
                    def between(t, kk0=kk0, j=j):
                        turn_kq(kk0 + t, M_QKV + 5 * (j - 1) + t)
                project("b", 2 * j, M_QKV + 5 * j, between)
            for t in range(TILES):
                turn_kq(15 + t, M_QKV + 25 + t)

            def scores(n, part):
                qt, h = n // HEADS, n % HEADS
                w = (qt + 1) * P
                r = slice(64 * part, 64 * part + 64)
                after(pe, at_exp, 2 * (n - 1) + part + 1)
                pe.matmul(ps[:, part, 0:w], QT[r, h, qt * P:(qt + 1) * P], KT[r, h, 0:w], start=True, stop=False,
                          skip_group_check=True)
                pe.matmul(ps[:, part, w - P:w], idmask[:, 0], idmask[:, 1], start=False, stop=True,
                          skip_group_check=True).then_inc(at_s, 1)

            def turn_p(n):
                pe.wait_ge(at_p, n + 1)
                after(pe, at_ptc, n)
                for b in range(n // HEADS + 1):
                    mm = pe.transpose(ps[:, 2, b * P:(b + 1) * P], Pm[:, n % 2, b * P:(b + 1) * P], ident)
                mm.then_inc(at_pt, 1)

            def values(n):
                qt, h = n // HEADS, n % HEADS
                pe.wait_ge(at_ptc, n + 1)
                after(pe, at_o, n)
                for b in range(qt + 1):
                    mm = pe.matmul(ps[:, 3, 0:P], PTs[:, n % 2, b * P:(b + 1) * P], x[:, b, h * P:(h + 1) * P],
                                   start=(b == 0), stop=(b == qt))
                mm.then_inc(at_pv, 1)

            def cache_chunk(g, j):
                c = B_CACHE + 4 * g + j
                pe.wait_ge(raw_b[c % RAW_SLOTS], landed_b[c])
                return raw[:, c % RAW_SLOTS].rearrange("p (a k) n -> p a (k n)", a=2)

            def turn_keys(g, hk):
                b2, page, half = hk // 4, hk // 2 % 2, hk % 2
                keys = cache_chunk(g, b2)
                after(pe, sm_ktc, 8 * g + hk)
                for jj in range(4):
                    h = 4 * half + jj
                    mm = pe.transpose(ps[:, 4, jj * P:(jj + 1) * P], keys[:, page, h * P:(h + 1) * P], ident)
                mm.then_inc(sm_kt, 1)

            def sample_scores(g, b2, half):
                if half == 0:
                    pe.wait_ge(sm_ktc, 8 * g + 4 * b2 + 4)
                    pe.sem_inc(keys_used, 1)
                    if b2 == 0:
                        pe.wait_ge(sm_q, g + 1)
                        after(pe, sm_ptz, g)
                for h in range(4 * half, 4 * half + 4):
                    lhs = qpad[:, (b2 * 8 + h) * P:(b2 * 8 + h + 1) * P]
                    pe.matmul(ps[:, 5, 0:256], lhs, kts[:, b2, h], start=(b2 == 0 and h == 0), stop=False,
                              skip_group_check=True)
                    mm = pe.matmul(ps[:, 5, 256:288], lhs, KT[:, h, SEQ:NTOK], start=False,
                                   stop=(b2 == 1 and h == HEADS - 1), skip_group_check=True)
                if half:
                    mm.then_inc(sm_s, 1)

            def turn_sample_p(g):
                pe.wait_ge(sm_p, g + 1)
                pe.transpose(ps[:, 5, 0:P], Ps[:, 0:P], ident)
                pe.transpose(ps[:, 5, P:2 * P], Ps[:, P:2 * P], ident)
                pe.transpose(ps[0:NSAMP, 5, 2 * P:3 * P], Ps[:, 256:288], ident).then_inc(sm_pt, 1)

            def sample_values(g, b2, page):
                vals = cache_chunk(g, 2 + b2)
                pe.wait_ge(sm_ptz, g + 1)
                for h in range(HEADS):
                    mm = pe.matmul(ps[0:NSAMP, 6 + h // 4, h % 4 * P:(h % 4 + 1) * P], ptz[:, page, b2, h],
                                   vals[:, page, h * P:(h + 1) * P],
                                   start=(g == 0 and b2 == 0 and page == 0 and h % 4 == 0), stop=False,
                                   skip_group_check=True)
                if page:
                    mm.then_inc(vals_used, 1)
                    if b2:
                        pe.wait_ge(vals_used, 2 * g + 2)
                        pe.sem_inc(sm_pv, 1)

            pe.wait_ge(kq_copied, 20)
            pe.wait_ge(proj_free, M_WO)
            pe.wait_ge(idmask_ready, 1)
            steps = 4 * HEADS
            for n in range(steps + 2):
                g, j = n // 8, n % 8
                if n < steps:
                    scores(n, 0)
                if n >= 2:
                    values(n - 2)
                if n < steps:
                    if j < 4:
                        turn_keys(g, 2 * j)
                    if j == 0 and g:
                        turn_sample_p(g - 1)
                    if 1 <= j < 5 and g:
                        sample_values(g - 1, (j - 1) // 2, (j - 1) % 2)
                    scores(n, 1)
                if 1 <= n <= steps:
                    turn_p(n - 1)
                if n < steps:
                    if j < 4:
                        turn_keys(g, 2 * j + 1)
                    if 2 <= j < 6:
                        sample_scores(g, (j - 2) // 2, (j - 2) % 2)
            turn_sample_p(3)
            for b2 in range(2):
                for page in range(2):
                    sample_values(3, b2, page)
            for h in range(HEADS):
                mm = pe.matmul(ps[0:NSAMP, 6 + h // 4, h % 4 * P:(h % 4 + 1) * P], ptn[:, h],
                               x[0:NSAMP, 4, h * P:(h + 1) * P], start=False, stop=(h % 4 == 3), skip_group_check=True)
            mm.then_inc(sm_pv, 1)

            pe.wait_ge(sm_o, 1)

            def turn_o(t):
                pe.wait_ge(om_r, t + 1)
                turn(t, T_O, o[t])
            project_by_tile("b", B_CACHE, M_WO, T_O, turn_o)
            project_by_tile("b", B_CACHE + 2, M_WO + 5)
            route(1, M_ROUTE_B, T_LN1B, 3)
            moe_pe(1, M_END)


IN_NAMES = ["con", "con16", "cmix", "x_prompt", "x_sample", "x_prompt_T", "x_sample_T", "w_s_T", "b_s_T", "b_s_rep",
            "cache_k", "cache_v", "page_table", "ln1_g", "ln1_b", "ln2_g", "ln2_b", "a_w_in", "a_b_in", "a_lnv_g",
            "a_lnv_b", "a_w_out", "w_k", "w_v", "b_w_q", "b_lam_q1", "b_lam_k1", "b_lam_q2", "b_lam_k2", "b_subln_g",
            "b_w_o", "router_w", "router_bias", "moe_w_up", "moe_w_down"]
OUT_SHAPES = [(1, SEQ, D), (DEC_B, DEC_T, D), (1, SEQ, HEADS, P), (1, SEQ, HEADS, P), (DEC_B, DEC_T, HEADS, P),
              (DEC_B, DEC_T, HEADS, P), (1, DEC_B, DEC_T, D)]


def kernel(**inputs):
    import concourse.bacc as bacc
    from concourse.bass_utils import run_bass_kernel_spmd

    arrays = {k: np.asarray(x) for k, x in inputs.items()}
    arrays["x_prompt_T"] = arrays["x_prompt"][0].T
    arrays["x_sample_T"] = arrays["x_sample"].reshape(NSAMP, D).T
    arrays["w_s_T"] = arrays["a_w_s"][0].transpose(2, 0, 1)
    arrays["b_s_T"] = arrays["a_b_s"][0].T
    arrays["b_s_rep"] = np.tile(arrays["a_b_s"][0, :, 0:DEC_T].T, (DEC_B, 1))
    arrays["con"], arrays["con16"], arrays["cmix"] = constants()

    nc = bacc.Bacc("TRN2", target_bir_lowering=False, num_devices=1)
    given, aps = {}, {}
    for name in IN_NAMES:
        arr = np.ascontiguousarray(arrays[name])
        given[f"in_{name}"] = arr
        aps[name] = nc.dram_tensor(f"in_{name}", arr.shape, mybir.dt.from_np(arr.dtype), kind="ExternalInput").ap()
    outs = [nc.dram_tensor(f"out_{i}", s, F32, kind="ExternalOutput").ap() for i, s in enumerate(OUT_SHAPES)]
    trunk(nc, aps, outs)
    r = run_bass_kernel_spmd(nc, [given], core_ids=[0])
    return tuple(r.results[0][f"out_{i}"] for i in range(len(OUT_SHAPES)))
```
